# Optimizing a Trainium2 kernel written in Bass

```python
import jax, jax.numpy as jnp
from jax import lax
import numpy as np

D_MODEL = 1024
BATCH = 1
SEQ = 512
DEPTH = 2

CHUNK = 64
EPS = 1e-6

GLA_HEADS = 4
GLA_DK = 64
GLA_DV = 128
GLA_GATE_RANK = 16
GLA_GATE_TAU = 16.0
GLA_QK = GLA_HEADS * GLA_DK
GLA_V = GLA_HEADS * GLA_DV

GDN_HEADS = 4
GDN_DK = 128
GDN_DV = 128
GDN_CONV = 4
GDN_QK = GDN_HEADS * GDN_DK
GDN_V = GDN_HEADS * GDN_DV
GDN_QKV = 2 * GDN_QK + GDN_V

AB_SPLITS = [GLA_QK, GLA_QK, GLA_V, GLA_GATE_RANK, GLA_V, GDN_QKV, GDN_HEADS, GDN_HEADS, GDN_V]
AB_IN = sum(AB_SPLITS)
AB_MIX = GLA_V + GDN_V

SWA_Q_HEADS = 16
SWA_KV_HEADS = 4
SWA_GROUP = SWA_Q_HEADS // SWA_KV_HEADS
SWA_HEAD_DIM = 64
WINDOW = 128
WIN_CHUNKS = WINDOW // CHUNK
ROPE_THETA = 10000.0
SWA_SPLITS = [SWA_Q_HEADS * SWA_HEAD_DIM, SWA_KV_HEADS * SWA_HEAD_DIM, SWA_KV_HEADS * SWA_HEAD_DIM]
SWA_IN = sum(SWA_SPLITS)
SWA_OUT = SWA_Q_HEADS * SWA_HEAD_DIM

N_EXPERTS = 16
N_GROUPS = 4
EXPERTS_PER_GROUP = N_EXPERTS // N_GROUPS
TOPK_GROUPS = 1
TOP_K = 2
D_EXPERT = 512

N_EVEN = (DEPTH + 1) // 2
N_ODD = DEPTH // 2

kernel_name = 'hybrid_gla_gdn_swa_grouped_moe_adaln'

def _split(t, sizes):
    idx = [int(i) for i in np.cumsum(sizes)[:-1]]
    return jnp.split(t, idx, axis=-1)

def rms_norm(x, gain):
    xf = x.astype(jnp.float32)
    y = xf * lax.rsqrt(jnp.mean(xf * xf, axis=-1, keepdims=True) + EPS)
    return (y * gain.astype(jnp.float32)).astype(x.dtype)

def l2_norm(x):
    xf = x.astype(jnp.float32)
    return (xf * lax.rsqrt(jnp.sum(xf * xf, axis=-1, keepdims=True) + EPS)).astype(x.dtype)

def to_chunks(t):
    b, s, h, d = t.shape
    return t.reshape(b, s // CHUNK, CHUNK, h, d).transpose(0, 3, 1, 2, 4)

def from_chunks(t):
    b, h, n, c, d = t.shape
    return t.transpose(0, 2, 3, 1, 4).reshape(b, n * c, h, d)

def rope(x, positions):
    half = x.shape[-1] // 2
    inv_freq = ROPE_THETA ** (-jnp.arange(half, dtype=jnp.float32) / half)
    ang = positions.astype(jnp.float32)[..., None] * inv_freq
    cos = jnp.cos(ang)[:, :, None, :]
    sin = jnp.sin(ang)[:, :, None, :]
    xf = x.astype(jnp.float32)
    x1, x2 = xf[..., :half], xf[..., half:]
    return jnp.concatenate([x1 * cos - x2 * sin, x2 * cos + x1 * sin], axis=-1).astype(x.dtype)

def causal_depthwise_conv(x, w):
    k, ch = w.shape
    return lax.conv_general_dilated(x, w[:, None, :], window_strides=(1,), padding=[(k - 1, 0)],
                                    dimension_numbers=('NWC', 'WIO', 'NWC'), feature_group_count=ch)

def gla_chunked(q, k, v, g):
    b = jnp.cumsum(g, axis=-2)
    b_last = b[..., -1:, :]
    q_dec = q * jnp.exp(b)
    k_dec = k * jnp.exp(-b)
    incl = jnp.tril(jnp.ones((CHUNK, CHUNK), dtype=bool))
    a = jnp.where(incl, jnp.einsum('bhnid,bhnjd->bhnij', q_dec, k_dec), 0.0)
    o_intra = jnp.einsum('bhnij,bhnjv->bhniv', a, v)
    upd = jnp.einsum('bhncd,bhncv->bhndv', k * jnp.exp(b_last - b), v)
    dec = jnp.exp(b_last[..., 0, :])

    def step(state, inp):
        d_n, u_n = inp
        return d_n[..., None] * state + u_n, state

    s0 = jnp.zeros(q.shape[:2] + (q.shape[-1], v.shape[-1]), q.dtype)
    _, s_prev = lax.scan(step, s0, (jnp.moveaxis(dec, 2, 0), jnp.moveaxis(upd, 2, 0)))
    s_prev = jnp.moveaxis(s_prev, 0, 2)
    return o_intra + jnp.einsum('bhncd,bhndv->bhncv', q_dec, s_prev)

def gated_delta_chunked(q, k, v, g, beta):
    b = jnp.cumsum(g, axis=-1)
    incl = jnp.tril(jnp.ones((CHUNK, CHUNK), dtype=bool))
    strict = jnp.tril(jnp.ones((CHUNK, CHUNK), dtype=bool), -1)
    gamma = jnp.exp(jnp.where(incl, b[..., :, None] - b[..., None, :], -jnp.inf))
    k_beta = k * beta[..., None]
    a_low = jnp.where(strict, jnp.einsum('bhnid,bhnjd->bhnij', k_beta, k) * gamma, 0.0)
    eye = jnp.eye(CHUNK, dtype=q.dtype)
    rhs = jnp.concatenate([v * beta[..., None], k_beta * jnp.exp(b)[..., None]], axis=-1)
    sol = lax.linalg.triangular_solve(eye + a_low, rhs, left_side=True, lower=True, unit_diagonal=True)
    dv = v.shape[-1]
    u, w = sol[..., :dv], sol[..., dv:]
    qk = jnp.einsum('bhnid,bhnjd->bhnij', q, k) * gamma
    q_dec = q * jnp.exp(b)[..., None]
    k_upd = k * jnp.exp(b[..., -1:] - b)[..., None]
    dec = jnp.exp(b[..., -1])

    def step(state, inp):
        u_n, w_n, qd_n, qk_n, ku_n, d_n = inp
        v_new = u_n - jnp.einsum('bhcd,bhdv->bhcv', w_n, state)
        o_n = jnp.einsum('bhcd,bhdv->bhcv', qd_n, state) + jnp.einsum('bhij,bhjv->bhiv', qk_n, v_new)
        state = d_n[..., None, None] * state + jnp.einsum('bhcd,bhcv->bhdv', ku_n, v_new)
        return state, o_n

    s0 = jnp.zeros(q.shape[:2] + (q.shape[-1], dv), q.dtype)
    xs = (jnp.moveaxis(u, 2, 0), jnp.moveaxis(w, 2, 0), jnp.moveaxis(q_dec, 2, 0),
          jnp.moveaxis(qk, 2, 0), jnp.moveaxis(k_upd, 2, 0), jnp.moveaxis(dec, 2, 0))
    _, o = lax.scan(step, s0, xs)
    return jnp.moveaxis(o, 0, 2)

def mix_gla_gdn(h, w_in, gla_w2, gla_b, gla_norm, conv_w, a_log, dt_bias, gdn_norm, w_out):
    bsz, s, _ = h.shape
    f32 = jnp.float32
    qa, ka, va, ga, za, qkvb, ab, bb, zb = _split(h @ w_in, AB_SPLITS)
    qa = qa.reshape(bsz, s, GLA_HEADS, GLA_DK).astype(f32) * GLA_DK ** -0.5
    ka = ka.reshape(bsz, s, GLA_HEADS, GLA_DK).astype(f32)
    va = va.reshape(bsz, s, GLA_HEADS, GLA_DV).astype(f32)
    gk = jax.nn.log_sigmoid((ga @ gla_w2 + gla_b).astype(f32)) / GLA_GATE_TAU
    gk = gk.reshape(bsz, s, GLA_HEADS, GLA_DK)
    oa = from_chunks(gla_chunked(to_chunks(qa), to_chunks(ka), to_chunks(va), to_chunks(gk)))
    oa = rms_norm(oa, gla_norm) * jax.nn.silu(za.reshape(bsz, s, GLA_HEADS, GLA_DV).astype(f32))
    qkvb = jax.nn.silu(causal_depthwise_conv(qkvb, conv_w)).astype(f32)
    qb, kb, vb = _split(qkvb, [GDN_QK, GDN_QK, GDN_V])
    qb = l2_norm(qb.reshape(bsz, s, GDN_HEADS, GDN_DK)) * GDN_DK ** -0.5
    kb = l2_norm(kb.reshape(bsz, s, GDN_HEADS, GDN_DK))
    vb = vb.reshape(bsz, s, GDN_HEADS, GDN_DV)
    gb = -jnp.exp(a_log.astype(f32)) * jax.nn.softplus(ab.astype(f32) + dt_bias.astype(f32))
    beta = jax.nn.sigmoid(bb.astype(f32))
    ob = gated_delta_chunked(to_chunks(qb), to_chunks(kb), to_chunks(vb),
                             to_chunks(gb[..., None])[..., 0], to_chunks(beta[..., None])[..., 0])
    ob = rms_norm(from_chunks(ob), gdn_norm) * jax.nn.silu(zb.reshape(bsz, s, GDN_HEADS, GDN_DV).astype(f32))
    o = jnp.concatenate([oa.reshape(bsz, s, GLA_V), ob.reshape(bsz, s, GDN_V)], axis=-1).astype(h.dtype)
    return o @ w_out

def _shift_chunks(t, j, n):
    pad = [(0, 0)] * t.ndim
    pad[1] = (j, 0)
    return jnp.pad(t, pad)[:, :n]

def mix_swa(h, positions, w_in, q_norm, k_norm, sinks, w_out):
    bsz, s, _ = h.shape
    n = s // CHUNK
    q, k, v = _split(h @ w_in, SWA_SPLITS)
    q = rope(rms_norm(q.reshape(bsz, s, SWA_Q_HEADS, SWA_HEAD_DIM), q_norm), positions)
    k = rope(rms_norm(k.reshape(bsz, s, SWA_KV_HEADS, SWA_HEAD_DIM), k_norm), positions)
    v = v.reshape(bsz, s, SWA_KV_HEADS, SWA_HEAD_DIM)
    q = q.reshape(bsz, n, CHUNK, SWA_KV_HEADS, SWA_GROUP, SWA_HEAD_DIM)
    k = k.reshape(bsz, n, CHUNK, SWA_KV_HEADS, SWA_HEAD_DIM)
    v = v.reshape(bsz, n, CHUNK, SWA_KV_HEADS, SWA_HEAD_DIM)
    k_band = jnp.concatenate([_shift_chunks(k, j, n) for j in range(WIN_CHUNKS - 1, -1, -1)], axis=2)
    v_band = jnp.concatenate([_shift_chunks(v, j, n) for j in range(WIN_CHUNKS - 1, -1, -1)], axis=2)
    src_chunk = jnp.arange(n)[:, None] - jnp.repeat(jnp.arange(WIN_CHUNKS - 1, -1, -1), CHUNK)[None, :]
    valid = (src_chunk >= 0)[:, None, :]
    scores = jnp.einsum('bnqhgd,bnkhd->bhgnqk', q, k_band).astype(jnp.float32) * SWA_HEAD_DIM ** -0.5
    scores = jnp.where(valid, scores, -jnp.inf)
    sink = sinks.astype(jnp.float32).reshape(SWA_KV_HEADS, SWA_GROUP)[None, :, :, None, None, None]
    m = jnp.maximum(jnp.max(scores, axis=-1, keepdims=True), sink)
    p = jnp.exp(scores - m)
    attn = p / (jnp.sum(p, axis=-1, keepdims=True) + jnp.exp(sink - m))
    o = jnp.einsum('bhgnqk,bnkhd->bnqhgd', attn.astype(v.dtype), v_band).reshape(bsz, s, SWA_OUT)
    return o @ w_out

def moe(h, router_w, router_bias, w_gate, w_up, w_down):
    bsz, s, d = h.shape
    t = h.reshape(-1, d)
    scores = jax.nn.sigmoid((t @ router_w).astype(jnp.float32))
    sel = scores + router_bias.astype(jnp.float32)
    grp_score = jnp.sum(lax.top_k(sel.reshape(-1, N_GROUPS, EXPERTS_PER_GROUP), TOP_K)[0], axis=-1)
    _, top_grp = lax.top_k(grp_score, TOPK_GROUPS)
    grp_mask = jnp.sum(jax.nn.one_hot(top_grp, N_GROUPS, dtype=jnp.float32), axis=1) > 0
    exp_mask = jnp.repeat(grp_mask, EXPERTS_PER_GROUP, axis=1)
    _, top_e = lax.top_k(jnp.where(exp_mask, sel, -jnp.inf), TOP_K)
    w = jnp.take_along_axis(scores, top_e, axis=-1)
    w = w / jnp.sum(w, axis=-1, keepdims=True)
    combine = jnp.sum(jax.nn.one_hot(top_e, N_EXPERTS, dtype=jnp.float32) * w[..., None], axis=1).astype(t.dtype)
    y = jnp.zeros_like(t)
    for e in range(N_EXPERTS):
        he = jax.nn.silu(t @ w_gate[e]) * (t @ w_up[e])
        y = y + combine[:, e:e + 1] * (he @ w_down[e])
    return y.reshape(bsz, s, d)

def setup_inputs(seed: int = 0) -> dict:
    key = jax.random.key(seed)
    ks = iter(jax.random.split(key, 40))
    f32 = jnp.float32

    def nrm(shape, scale):
        return jax.random.normal(next(ks), shape, f32) * scale

    D = D_MODEL
    x = nrm((BATCH, SEQ, D), 1.0)
    c = nrm((BATCH, D), 1.0)
    offs = jax.random.randint(next(ks), (BATCH, 1), 0, 4096, dtype=jnp.int32)
    positions = (offs + jnp.arange(SEQ, dtype=jnp.int32)[None, :]).astype(jnp.int32)
    router_w = nrm((D, N_EXPERTS), D ** -0.5)
    router_bias = nrm((N_EXPERTS,), 0.01)
    ada_w = nrm((DEPTH, D, 6 * D), 0.5 * D ** -0.5)
    ada_b = nrm((DEPTH, 6 * D), 0.02)
    norm_mix = 1.0 + nrm((DEPTH, D), 0.02)
    norm_ffn = 1.0 + nrm((DEPTH, D), 0.02)
    ab_w_in = nrm((N_EVEN, D, AB_IN), D ** -0.5)
    gla_gate_w2 = nrm((N_EVEN, GLA_GATE_RANK, GLA_QK), GLA_GATE_RANK ** -0.5)
    gla_gate_b = nrm((N_EVEN, GLA_QK), 0.1)
    gla_norm = 1.0 + nrm((N_EVEN, GLA_DV), 0.02)
    gdn_conv = nrm((N_EVEN, GDN_CONV, GDN_QKV), GDN_CONV ** -0.5)
    gdn_a_log = jnp.log(jax.random.uniform(next(ks), (N_EVEN, GDN_HEADS), f32, 1.0, 16.0))
    dt = jnp.exp(jax.random.uniform(next(ks), (N_EVEN, GDN_HEADS), f32, float(np.log(1e-3)), float(np.log(1e-1))))
    gdn_dt_bias = dt + jnp.log(-jnp.expm1(-dt))
    gdn_norm = 1.0 + nrm((N_EVEN, GDN_DV), 0.02)
    ab_w_out = nrm((N_EVEN, AB_MIX, D), AB_MIX ** -0.5)
    swa_w_in = nrm((N_ODD, D, SWA_IN), D ** -0.5)
    swa_q_norm = 1.0 + nrm((N_ODD, SWA_HEAD_DIM), 0.02)
    swa_k_norm = 1.0 + nrm((N_ODD, SWA_HEAD_DIM), 0.02)
    swa_sinks = nrm((N_ODD, SWA_Q_HEADS), 0.5)
    swa_w_out = nrm((N_ODD, SWA_OUT, D), SWA_OUT ** -0.5)
    moe_w_gate = nrm((DEPTH, N_EXPERTS, D, D_EXPERT), D ** -0.5)
    moe_w_up = nrm((DEPTH, N_EXPERTS, D, D_EXPERT), D ** -0.5)
    moe_w_down = nrm((DEPTH, N_EXPERTS, D_EXPERT, D), D_EXPERT ** -0.5)
    return {'x': x, 'c': c, 'positions': positions, 'router_w': router_w, 'router_bias': router_bias,
            'ada_w': ada_w, 'ada_b': ada_b, 'norm_mix': norm_mix, 'norm_ffn': norm_ffn,
            'ab_w_in': ab_w_in, 'gla_gate_w2': gla_gate_w2, 'gla_gate_b': gla_gate_b, 'gla_norm': gla_norm,
            'gdn_conv': gdn_conv, 'gdn_a_log': gdn_a_log, 'gdn_dt_bias': gdn_dt_bias, 'gdn_norm': gdn_norm,
            'ab_w_out': ab_w_out, 'swa_w_in': swa_w_in, 'swa_q_norm': swa_q_norm, 'swa_k_norm': swa_k_norm,
            'swa_sinks': swa_sinks, 'swa_w_out': swa_w_out, 'moe_w_gate': moe_w_gate, 'moe_w_up': moe_w_up,
            'moe_w_down': moe_w_down}

def reference(x, c, positions, router_w, router_bias, ada_w, ada_b, norm_mix, norm_ffn,
              ab_w_in, gla_gate_w2, gla_gate_b, gla_norm, gdn_conv, gdn_a_log, gdn_dt_bias, gdn_norm,
              ab_w_out, swa_w_in, swa_q_norm, swa_k_norm, swa_sinks, swa_w_out,
              moe_w_gate, moe_w_up, moe_w_down):
    cond = jax.nn.silu(c)
    for layer in range(DEPTH):
        mod = cond @ ada_w[layer] + ada_b[layer]
        sh1, sc1, g1, sh2, sc2, g2 = [m[:, None, :] for m in jnp.split(mod, 6, axis=-1)]
        h = rms_norm(x, norm_mix[layer]) * (1 + sc1) + sh1
        i = layer // 2
        if layer % 2 == 0:
            mix = mix_gla_gdn(h, ab_w_in[i], gla_gate_w2[i], gla_gate_b[i], gla_norm[i], gdn_conv[i],
                              gdn_a_log[i], gdn_dt_bias[i], gdn_norm[i], ab_w_out[i])
        else:
            mix = mix_swa(h, positions, swa_w_in[i], swa_q_norm[i], swa_k_norm[i], swa_sinks[i], swa_w_out[i])
        x = x + g1 * mix
        h = rms_norm(x, norm_ffn[layer]) * (1 + sc2) + sh2
        x = x + g2 * moe(h, router_w, router_bias, moe_w_gate[layer], moe_w_up[layer], moe_w_down[layer])
    return x


_drawn_inputs = setup_inputs


def setup_inputs(seed=0):
    import zlib

    import numpy as np

    out = dict(_drawn_inputs(seed))
    spreads = {}
    factors = {'norm_mix': 2.727,
     'gla_norm': 5.626,
     'gdn_dt_bias': 3.234,
     'gdn_norm': 3.632,
     'swa_q_norm': 8.0,
     'swa_k_norm': 8.0,
     'swa_sinks': 8.0}
    for name, (base, spread) in spreads.items():
        noise = np.random.default_rng([zlib.crc32(name.encode()), seed]).standard_normal(out[name].shape)
        drawn = base * np.exp(spread * noise) if base else spread * noise
        out[name] = __import__('jax').numpy.asarray(drawn.astype(out[name].dtype))
    for name, factor in factors.items():
        out[name] = (out[name] * factor).astype(out[name].dtype)
    return out
```

```python
from contextlib import ExitStack

import concourse.bass as bass
import numpy as np
from concourse import mybir

P = 128
SEQ, D = 512, 1024
TT = SEQ // P
KD = D // P
CHUNK = 64
EPS = 1e-6
HEADS = 4
GLA_DK, DV = 64, 128
RANK = 16
QW, NQ, NKV, HD = 1024, 16, 4, 64
NE, NGRP, FF = 16, 4, 512
EG = 4
RING = 4
SLOTS = 128
MAXOVER = (2 * SEQ - 1) // SLOTS
NEG = -1e30
NWORK = 18700

F32 = mybir.dt.float32
I32 = mybir.dt.int32
U32 = mybir.dt.uint32
ALU = mybir.AluOpType
ACT = mybir.ActivationFunctionType
AX = mybir.AxisListType

C_GA = 2 * HEADS * GLA_DK + HEADS * DV
C_ZA = C_GA + RANK
C_QKVB = C_ZA + HEADS * DV
C_AB = C_QKVB + 3 * HEADS * DV
C_ZB = C_AB + 2 * HEADS

DESC_TOP = 1000.0
ROUND = 1.5 * 2.0 ** 23
TURN = (6.28125, 0.0019340515136718750, float(2 * np.pi - 6.28125 - 0.0019340515136718750))
PI_BELOW = 3.1415925

CONST_WIDTHS = [
    ("ident", P), ("tri", P), ("later", P), ("strict_bias", P), ("incl_bias", P), ("lev", 6 * P),
    ("in_chunk", 2 * P), ("ones", P), ("before", P), ("iota", P), ("swa_bias", 2 * 192),
    ("inv_freq", 32), ("desc16", 16), ("desc48", 48),
]
CONST_AT, _n = {}, 0
for _name, _w in CONST_WIDTHS:
    CONST_AT[_name] = (_n, _w)
    _n += _w
NCONST = _n


def constants():
    j, i = np.arange(P)[:, None], np.arange(P)[None, :]
    same = (j // CHUNK) == (i // CHUNK)
    c = {
        "ident": j == i, "tri": same & (j <= i), "later": same & (j > i),
        "strict_bias": np.where(same & (j < i), 0.0, NEG), "incl_bias": np.where(same & (j <= i), 0.0, NEG),
        "ones": np.ones((P, P)), "before": j < i, "iota": np.broadcast_to(i, (P, P)),
        "inv_freq": np.broadcast_to((10000.0 ** (-np.arange(32) / 32))[None, :], (P, 32)),
        "desc16": np.broadcast_to(16.0 - np.arange(16)[None, :], (P, 16)),
        "desc48": np.broadcast_to(DESC_TOP - np.arange(48)[None, :], (P, 48)),
    }
    lev = []
    for n in range(6):
        s = 1 << n
        lev.append(((i // (2 * s)) == (j // (2 * s))) & ((i // s) % 2 == 1) & ((j // s) % 2 == 0))
    c["lev"] = np.concatenate(lev, axis=1)
    c["in_chunk"] = np.concatenate([np.broadcast_to(j // CHUNK == n, (P, P)) for n in range(2)], axis=1)
    q, k = np.arange(P)[:, None], np.arange(192)[None, :]
    seen = (k // CHUNK == q // CHUNK) | (k // CHUNK == q // CHUNK + 1)
    c["swa_bias"] = np.concatenate([np.where(seen & (k >= CHUNK), 0.0, NEG), np.where(seen, 0.0, NEG)], axis=1)
    out = np.zeros((P, NCONST), np.float32)
    for name, (a, w) in CONST_AT.items():
        out[:, a:a + w] = c[name].astype(np.float32)
    return out


class Steps:

    def __init__(self, sem, names, credit=0):
        self.sem, self.names, self.n, self.credit, self.k = sem, list(names), len(names), credit, 0

    def at(self, t, name):
        return (t + self.credit) * self.n + self.names.index(name) + 1

    def one(self, name):
        assert self.names[self.k % self.n] == name, (self.names[self.k % self.n], name)
        self.k += 1
        return 1


def build_block(nc, a, out):
    ctx = ExitStack()
    with ctx:
        def sem(name):
            return ctx.enter_context(nc.semaphore(name))

        def sb(name, shape, dt=F32):
            return ctx.enter_context(nc.sbuf_tensor(name, shape, dt))

        ring = sb("ring", [P, RING, KD, 512])
        x = sb("x", [P, TT, D])
        hT = sb("hT", [P, KD, SEQ])
        mod = sb("mod", [P, 6 * D])
        const = sb("const", [P, NCONST])
        NPAR = 960
        par = sb("par", [P, NPAR])
        NW = NWORK
        work = sb("work", [P, NW])
        ovl_i = sb("ovl_i", [P, 32], I32)
        pos_i = sb("pos_i", [P, TT], I32)
        ps = ctx.enter_context(nc.psum_tensor("ps", [P, 8, 512], F32))

        def cst(name, lo=0, n=None):
            o, w = CONST_AT[name]
            return const[:, o + lo:o + lo + (w if n is None else n)]

        top = {"par": 0, "work": 0}

        def carve(which, *shape):
            n = int(np.prod(shape))
            t = par if which == "par" else work
            o = top[which]
            top[which] = o + n
            assert top[which] <= (NPAR if which == "par" else NW), (which, top[which])
            v = t[:, o:o + n]
            if len(shape) == 2:
                v = v.rearrange("p (a b) -> p a b", a=shape[0])
            elif len(shape) == 3:
                v = v.rearrange("p (a b c) -> p a b c", a=shape[0], b=shape[1])
            elif len(shape) == 4:
                v = v.rearrange("p (a b c d) -> p a b c d", a=shape[0], b=shape[1], c=shape[2])
            return v

        def bank(b, *shape):
            v = ps[:, b, :]
            if len(shape) == 2:
                v = v[:, 0:shape[0] * shape[1]].rearrange("p (a b) -> p a b", a=shape[0])
            elif len(shape) == 3:
                v = v[:, 0:shape[0] * shape[1] * shape[2]].rearrange("p (a b c) -> p a b c", a=shape[0], b=shape[1])
            return v

        ident = cst("ident")

        cond = carve("par", KD)
        w2aug = carve("par", HEADS * GLA_DK)
        conv_w = carve("par", 12, 4)
        gla_gain = carve("par", DV)
        gdn_gain = carve("par", DV)
        q_gain = carve("par", HD)
        k_gain = carve("par", HD)
        sink = carve("par", NQ)
        router_w = carve("par", KD, NE)
        router_b = carve("par", NE)
        a_log = carve("par", HEADS)
        dt_bias = carve("par", HEADS)
        ss = carve("par", TT)
        var = carve("par", TT)
        rstd = carve("par", TT)
        nt1 = carve("par", TT)
        nt2 = carve("par", TT)

        const_in = sem("const_in")
        params_in = sem("params_in")
        x_in = sem("x_in")
        small_in = sem("small_in")
        bias_in = [sem(f"bias_in{l}") for l in range(2)]
        chunk_in = [sem(f"chunk_in{s}") for s in range(RING)]
        chunk_used = sem("chunk_used")
        phase_done = sem("phase_done")
        out_written = sem("out_written")
        cond_dve = Steps(sem("cond_dve"), ["e1", "rec", "silu"])
        rep_dve = Steps(sem("rep_dve"), ["rep"])
        cond_act = Steps(sem("cond_act"), ["exp"])
        ada_pe = Steps(sem("ada_pe"), ["mod"])
        ada_dve = Steps(sem("ada_dve"), ["mod"])
        amod_dve = Steps(sem("amod_dve"), ["a1", "a2"])
        norm_act = Steps(sem("norm_act"), ["ss0", "ss1", "ss2", "ss3", "ln", "exp", "ev0", "ev1", "ev2", "ev3"])
        norm_dve = Steps(sem("norm_dve"), ["var", "n1", "n2", "n3", "rstd", "hx0", "h0", "hx1", "h1", "hx2", "h2",
                                           "hx3", "h3", "ev0", "ev1", "ev2", "ev3"])
        norm_pe = Steps(sem("norm_pe"), [f"{n}{t}" for t in range(TT) for n in ("lo", "hi")])
        proj_pe = Steps(sem("proj_pe"), ["job"])
        proj_act = Steps(sem("proj_act"), ["ev"])
        proj_dve = Steps(sem("proj_dve"), ["ev"])
        conv_dve = Steps(sem("conv_dve"), ["t0", "t1", "t2", "t3"])
        conv_act = Steps(sem("conv_act"), ["silu", "sq"])
        conv_pe = Steps(sem("conv_pe"), ["ss"])
        init_dve = sem("init_dve")

        GLA_PE = Steps(sem("gla_pe"), ["gaT", "qkT", "z", "cums", "A", "u0", "u1", "o", "int0", "int1", "oT"])
        GLA_ACT = Steps(sem("gla_act"), ["abs", "e", "l", "eb", "enb", "ekb", "ss", "ln", "exp", "oT"])
        GLA_DVE = Steps(sem("gla_dve"), ["gaT", "g", "qd", "kz", "ku", "A", "s0", "s1", "zg", "var", "n1", "n2",
                                         "n3", "rstd", "on"])
        PRE_DVE = Steps(sem("gdn_pre_dve"), ["u", "au", "mx", "g", "lnb", "lk", "lq", "lbk", "pre", "colj"])
        PRE_ACT = Steps(sem("gdn_pre_act"), ["e", "l", "expa", "lnss", "exp"])
        PRE_PE = Steps(sem("gdn_pre_pe"), ["cum"])
        LV = [f"{n}{l}" for l in range(1, 6) for n in ("atm", "xt", "x")]
        LV.remove("x5")
        GDN_DVE = Steps(sem("gdn_dve"), ["rep", "d1", "d2", "at", "qk", "qd", "ku", "kb", "vb", "atm0", "xt0"] + LV
                        + ["u", "vn0", "s0", "vn1", "s1", "zg", "var", "n1", "n2", "n3", "rstd", "on"])
        GDN_ACT = Steps(sem("gdn_act"), ["exp", "eq", "x0"] + [f"p{l}" for l in range(1, 6)]
                        + ["wT", "ss", "ln", "rs", "oT"])
        GDN_PE = Steps(sem("gdn_pe"), ["rows", "kk", "kv", "x0"] + [f"{n}{l}" for l in range(1, 6) for n in ("p", "y")]
                       + ["uw", "ws0", "o0", "up0", "ws1", "o1", "up1", "oT"])
        outp_pe = Steps(sem("outp_pe"), ["job"])
        outp_dve = Steps(sem("outp_dve"), ["tmp", "x"])

        ROPE_DVE = Steps(sem("rope_dve"), ["pos", "ang", "k1", "k2", "r1", "r2", "r3", "r", "c1", "c2", "c3", "c"])
        ROPE_ACT = Steps(sem("rope_act"), ["sin", "cos"])
        QK_ACT = Steps(sem("qk_act"), [f"sq{t}" for t in range(TT)] + ["ln", "exp"])
        QK_DVE = Steps(sem("qk_dve"), [f"ss{t}" for t in range(TT)] + ["var", "n1", "n2", "n3", "rstd"]
                       + [f"{n}{t}" for t in range(TT) for n in ("a", "b", "c", "rope", "k")] + ["q3"])
        QK_PE = Steps(sem("qk_pe"), [f"{n}{t}" for t in range(TT) for n in ("q", "k")])
        QT_ACT = Steps(sem("qt_act"), ["q"])
        SWA_PE = Steps(sem("swa_pe"), [f"s{n}" for n in range(8)] + [f"{n}{i}" for i in range(8) for n in ("t", "v")])
        SWA_DVE = Steps(sem("swa_dve"), [f"s{n}" for n in range(8)] + ["max", "m", "nm", "es", "den", "rec", "p"])
        SWA_ACT = Steps(sem("swa_act"), ["es", "exp"] + [f"t{n}" for n in range(8)] + ["o"])

        RT_DVE = Steps(sem("router_dve"), ["e1", "sc", "sel", "pairs", "top", "low", "second", "gs", "gmax", "geq", "gw",
                                           "gmw", "gmask", "goff", "selm", "max1", "eq1", "w1", "mw1", "mk1", "selm2",
                                           "max2", "eq2", "w2", "mw2", "mk2", "mk", "wr", "wsum", "wrec", "wgt", "off",
                                           "posm", "fl", "key", "top8", "nov", "ent", "enti", "sh", "ei", "base", "ovl"])
        RT_PE = Steps(sem("router_pe"), ["logits", "pos"])
        RT_ACT = Steps(sem("router_act"), ["exp"])

        def expert_steps(tag, E):
            es = range(E)
            return (
                Steps(sem(f"{tag}_pe"), [f"hg{k}" for k in range(KD)] + [f"pT{e}" for e in es] + ["ws"]
                      + [f"{n}{e}" for e in es for n in ("g", "u", "hT", "y0", "y1")] + [f"c{j}" for j in range(8)], credit=1),
                Steps(sem(f"{tag}_act"), [f"hg{k}" for k in range(0, KD, 2)] + [f"pT{e}" for e in range(0, E, 2)]
                      + [f"{n}{e}" for e in es for n in ("sg", "hT")], credit=1),
                Steps(sem(f"{tag}_dve"), ["pw", "disp"] + [f"hg{k}" for k in range(1, KD, 2)]
                      + [f"pT{e}" for e in range(1, E, 2)] + ["ws"] + [f"{n}{e}" for e in es for n in ("he", "y0", "y1")]
                      + [f"x{j}" for j in range(8)], credit=1),
            )

        moe_steps = [expert_steps(f"moe{l}", EG) for l in range(2)]
        over_steps = [expert_steps(f"over{l}", 1) for l in range(2)]
        over_in = [sem(f"over_in{l}") for l in range(2)]
        over_col = [sem(f"over_col{l}") for l in range(2)]

        n_chunks = {"ada": 12, "ab": 8, "abo": 2, "moe": 48, "swa": 3, "swo": 2}
        order = [("ada", 0), ("ab", 0), ("abo", 0), ("moe", 0), ("ada", 1), ("swa", 1), ("swo", 1), ("moe", 1)]
        first, n = {}, 0
        for o in order:
            first[o] = n
            n += n_chunks[o[0]]

        def loaded(c):
            return 16 * (c // RING + 1)

        def slot(c):
            return ring[:, c % RING]

        def expert_view(v, w):
            return v if w < 2 else v.rearrange("p (k a) f -> p k (a f)", a=2)

        def rows(w, n):
            return w.rearrange("(k p) f -> p k f", p=P)[:, :, n]


        h = carve("work", TT, D)
        cond_rep = h[:, 0].rearrange("p (k m) -> p k m", k=KD)
        gain1, gain2 = h[:, 1], h[:, 2]
        junk_wide = work[:, NW - D:NW]

        top["work"] = 0
        pqk = carve("work", TT, 512)
        pv = carve("work", TT, 512)
        pz = carve("work", TT, 512)
        gaT = carve("work", P)
        az, ee, gg = (mod[:, o:o + 256] for o in (128, 384, 640))
        eb = carve("work", 2, P)
        enb = carve("work", 2, P)
        ekb = carve("work", 256)
        qd = carve("work", 2, P)
        kz = carve("work", 2, 2, P)
        ku = carve("work", 2, 256)
        at_g = carve("work", HEADS, P)
        st_g = carve("work", 2, 256)
        on_g = mod[:, 1024:1536].rearrange("p (a b) -> p a b", a=HEADS)
        sm_g = carve("work", 5, HEADS)
        gla_end = top["work"]
        top["work"] = 0
        rep = carve("work", 3, HEADS, P)
        ex = carve("work", 2, HEADS, P)
        eq = carve("work", HEADS, P)
        atb = carve("work", HEADS, P)
        atm = carve("work", HEADS, P)
        xx = carve("work", HEADS, P)
        xt = carve("work", HEADS, P)
        pm = carve("work", HEADS, P)
        qkt = carve("work", HEADS, P)
        ku_b = carve("work", 2, HEADS, P)
        kb_b = carve("work", HEADS, P)
        vb_b = carve("work", HEADS, P)
        vn = carve("work", HEADS, P)
        st_b = carve("work", HEADS, P)
        sm_b = carve("work", 5, HEADS)
        u_b, wt_b, qd_b, on_b, zg_b = pm, atm, eq, xx, kb_b
        top["work"] = max(gla_end, top["work"])
        pzb = carve("work", TT, 512)
        psm = carve("work", TT, 24)
        qkvT = carve("work", 12, 3 + SEQ)
        pre_u = carve("work", TT, 8)
        pre_a = carve("work", TT, 8)
        pre_l = carve("work", TT, 8)
        g_b = carve("work", TT, HEADS)
        lnb = carve("work", TT, HEADS)
        nexpa = carve("work", HEADS)
        ssk = carve("work", TT, 2 * HEADS)
        lk = carve("work", TT, HEADS)
        lq = carve("work", TT, HEADS)
        lbk = carve("work", TT, HEADS)
        pre = carve("work", 5, TT, HEADS)
        pexp = carve("work", 5, TT, HEADS)
        colj = carve("work", TT, HEADS)
        conv_t = mod[:, 0:1024].rearrange("p (a b) -> p a b", a=2)
        conv_sq = mod[:, 1024:2048].rearrange("p (a b) -> p a b", a=2)
        junk = mod[:, 1536:2048]
        res_tmp = mod[:, 0:512]
        oT = hT

        top["work"] = 0
        p2 = carve("work", TT, 3 * 512)
        kTz = carve("work", NKV, 2, CHUNK + SEQ)
        sm = carve("work", NQ, 256)
        pT = carve("work", 2, 2, 2, P)
        cs = carve("work", TT, 32)
        sn = carve("work", TT, 32)
        rang = carve("work", TT, 32)
        rk = carve("work", TT, 32)
        rr = carve("work", TT, 32)
        rc = carve("work", TT, 32)
        posf = carve("work", TT)
        qk_s = carve("work", 4, TT, 20)
        sw_s = carve("work", 6, NQ)
        smf = sm.rearrange("p a b -> p (a b)")
        rope_t = [smf[:, 640 * i:640 * i + 640].rearrange("p (a b) -> p a b", a=20) for i in range(4)]
        sq2 = smf[:, 2560:2560 + 1280]
        qT = hT

        top["work"] = TT * D
        pd = carve("work", TT, EG * P)
        pdT = carve("work", EG, SEQ)
        ys = carve("work", EG, D)
        sg = carve("work", FF)
        he = carve("work", FF)
        heT = carve("work", 4, P)
        ws = carve("work", EG)
        pcol = carve("work", TT, EG)
        wcol = carve("work", TT, EG)
        posm = carve("work", TT, NE)
        wgt = carve("work", TT, NE)
        r_e = carve("work", TT, NE)
        r_sc = carve("work", TT, NE)
        r_sel = carve("work", TT, NE)
        r_a = carve("work", TT, NE)
        r_b = carve("work", TT, NE)
        mk1 = carve("work", TT, NE)
        mk = carve("work", TT, NE)
        r_g = [carve("work", TT, NGRP) for _ in range(8)]
        r_t = carve("work", TT)
        r_u = carve("work", TT)
        fl = carve("work", 3, NE)
        key = carve("work", 3, NE)
        top8 = carve("work", 8)
        ent = carve("work", 8)
        basef = carve("work", 8)
        nov = carve("work", 1)
        hgT = hT

        def cols(t):
            return slice(P * t, P * t + P)

        AB_COLS = [0, C_GA, 512, C_QKVB, C_QKVB + 512, C_QKVB + 1024, C_ZA, C_ZB]
        AB_KIND = ["qk", "small", "v", "f0", "f1", "f2", "za", "zb"]
        jobs = [(n, t, AB_KIND[n]) for n in range(8) for t in range(TT)]
        emptied, counts = [], {"s": 0, "v": 0}
        for j, (n, t, kind) in enumerate(jobs):
            e = "s" if kind in ("za", "zb") or j % 2 else "v"
            emptied.append((e, counts[e]))
            counts[e] += 1

        swa_jobs = [(n, t) for n in range(3) for t in range(TT)]
        for j, _ in enumerate(swa_jobs):
            e = "s" if j % 2 else "v"
            emptied.append((e, counts[e]))
            counts[e] += 1
        NJ = len(jobs)

        def emptier(j):
            e, k = emptied[j]
            st = proj_act if e == "s" else proj_dve
            return st.sem, st.at(k, "ev")

        block = ctx.enter_context(nc.Block())

        @block.sync
        def _(sp):
            sp.dma_start(const[:], a["consts"]).then_inc(const_in, 16)

            def load(c, dst, src):
                if c >= RING:
                    sp.wait_ge(chunk_used, c - RING + 1)
                sp.dma_start(dst, src).then_inc(chunk_in[c % RING], 16)

            def load_columns(key, w, starts):
                for n, lo in enumerate(starts):
                    c = first[key] + n
                    load(c, slot(c), rows(w, slice(lo, lo + 512)))

            load_columns(("ada", 0), a["ada_w"][0], range(0, 6 * D, 512))
            for n, lo in enumerate(AB_COLS):
                c = first[("ab", 0)] + n
                if n == 1:
                    if c >= RING:
                        sp.wait_ge(chunk_used, c - RING + 1)
                    sp.dma_start(slot(c)[:, :, 0:RANK], rows(a["ab_w_in"][0], slice(C_GA, C_GA + RANK))
                                 ).then_inc(small_in, 16)
                    load(c, slot(c)[:, :, RANK:RANK + 8], rows(a["ab_w_in"][0], slice(C_AB, C_AB + 8)))
                else:
                    load(c, slot(c), rows(a["ab_w_in"][0], slice(lo, lo + 512)))
            load_columns(("abo", 0), a["ab_w_out"][0], range(0, D, 512))
            def experts(l):
                c0 = first[("moe", l)]
                ws_ = [a["moe_w_gate"][l], a["moe_w_up"][l], a["moe_w_down"][l]]
                with sp.Fori(0, NE // EG) as i:
                    for e in range(EG):
                        for w in range(3):
                            m = 3 * e + w
                            c = c0 + m
                            sp.wait_ge(chunk_used, c0 + m - RING + 1 + 3 * EG * i)
                            sp.dma_start(expert_view(slot(c), w), ws_[w][EG * i + e].rearrange("(k p) f -> p k f", p=P)
                                         ).then_inc(chunk_in[c % RING], 16)
                sp.wait_ge(RT_DVE.sem, RT_DVE.at(l, "ovl"))
                n_over = sp.value_load(ovl_i[0:1, 8:9], min_val=0, max_val=MAXOVER)
                st_pe = over_steps[l][0]
                with sp.Fori(0, MAXOVER) as j:
                    e = sp.value_load(ovl_i[0:1, bass.ds(j, 1)], min_val=0, max_val=NE - 1)
                    with sp.If(n_over > j):
                        sp.wait_ge(chunk_used, c0 + 3 * NE)
                        sp.wait_ge(st_pe.sem, st_pe.at(j - 1, "y10"))
                        for w in range(3):
                            sp.dma_start(expert_view(ring[:, w], w), ws_[w][e].rearrange("(k p) f -> p k f", p=P)
                                         ).then_inc(over_in[l], 16)


            experts(0)
            sp.wait_ge(phase_done, 3 * 5)
            load_columns(("ada", 1), a["ada_w"][1], range(0, 6 * D, 512))
            load_columns(("swa", 1), a["swa_w_in"][0], range(0, 3 * 512, 512))
            load_columns(("swo", 1), a["swa_w_out"][0], range(0, D, 512))
            experts(1)
            sp.wait_ge(phase_done, 3 * 9)
            sp.dma_start(out[0].rearrange("(t p) d -> p t d", p=P), x[:]).then_inc(out_written, 16)
            sp.wait_ge(out_written, 16)

        @block.gpsimd
        def _(pool):
            def param(dst, src):
                nc.gpsimd.dma_start(dst, src).then_inc(params_in, 16)

            def bc(v):
                return v.partition_broadcast(P)

            param(cond, a["c_cols"])
            for l in range(2):
                if l == 1:
                    pool.wait_ge(phase_done, 3 * 5)
                nc.gpsimd.dma_start(mod[:], bc(a["ada_b"][l])).then_inc(bias_in[l], 16)
                nc.gpsimd.dma_start(gain1, bc(a["norm_mix"][l])).then_inc(bias_in[l], 16)
                nc.gpsimd.dma_start(gain2, bc(a["norm_ffn"][l])).then_inc(bias_in[l], 16)
                if l == 0:
                    nc.gpsimd.dma_start(x[:], a["x"][0].rearrange("(t p) d -> p t d", p=P)).then_inc(x_in, 16)
                    param(w2aug[0:RANK, :], a["gla_gate_w2"][0])
                    param(w2aug[RANK:RANK + 1, :], a["gla_gate_b"][0:1])
                    param(conv_w.rearrange("p c k -> p (c k)"), a["conv_cols"])
                    param(gla_gain, bc(a["gla_norm"][0]))
                    param(gdn_gain, bc(a["gdn_norm"][0]))
                    param(q_gain, bc(a["swa_q_norm"][0]))
                    param(k_gain, bc(a["swa_k_norm"][0]))
                    param(sink, bc(a["swa_sinks"][0]))
                    param(router_w, a["router_w"].rearrange("(k p) e -> p k e", p=P))
                    param(router_b, bc(a["router_bias"]))
                    param(a_log, bc(a["gdn_a_log"][0]))
                    param(dt_bias, bc(a["gdn_dt_bias"][0]))
                    param(pos_i[:], a["pos_cols"])

        NPARAMS = 14

        @block.tensor
        def _(pe):
            mm = nc.tensor.matmul

            def turn(dst, src, k=P):
                return nc.tensor.transpose(dst, src, ident[0:k, 0:k])

            def used(ins):
                ins.then_inc(chunk_used, 1)

            def ada(l):
                pe.wait_ge(rep_dve.sem, rep_dve.at(l, "rep"))
                for n in range(12):
                    c = first[("ada", l)] + n
                    r = 12 * l + n
                    pe.wait_ge(chunk_in[c % RING], loaded(c))
                    if r >= 4:
                        pe.wait_ge(ada_dve.sem, ada_dve.at(r - 4, "mod"))
                    for k in range(KD):
                        ins = mm(bank(n % 4), cond_rep[:, k], slot(c)[:, k], start=(k == 0), stop=(k == KD - 1))
                    ins.then_inc(ada_pe.sem, ada_pe.one("mod"))
                    pe.wait_ge(ada_pe.sem, ada_pe.at(r, "mod"))
                    pe.sem_inc(chunk_used, 1)

            def norm(s):
                for t in range(TT):
                    pe.wait_ge(norm_dve.sem, norm_dve.at(s, f"h{t}"))
                    if t >= 2:
                        pe.wait_ge(norm_act.sem, norm_act.at(s, f"ev{t - 2}"))
                        pe.wait_ge(norm_dve.sem, norm_dve.at(s, f"ev{t - 2}"))
                    for half, name in enumerate(("lo", "hi")):
                        for k in range(4):
                            kk = 4 * half + k
                            ins = turn(bank(4 + 2 * (t % 2) + half)[:, cols(k)], h[:, t, kk * P:kk * P + P])
                        ins.then_inc(norm_pe.sem, norm_pe.one(f"{name}{t}"))

            def project_ab():
                pe.wait_ge(norm_act.sem, norm_act.at(0, "ev3"))
                pe.wait_ge(norm_dve.sem, norm_dve.at(0, "ev3"))

                def sums(ct):
                    pe.wait_ge(conv_act.sem, conv_act.at(ct, "sq"))
                    for t in range(TT):
                        ins = mm(bank(5, TT, 8)[:, t, ct:ct + 1], conv_sq[:, ct % 2, cols(t)], cst("ones", 0, 1),
                                 start=True, stop=True)
                    ins.then_inc(conv_pe.sem, conv_pe.one("ss"))

                for j, (n, t, kind) in enumerate(jobs):
                    c = first[("ab", 0)] + n
                    if t == 0:
                        pe.wait_ge(chunk_in[c % RING], loaded(c))
                        if n == 1:
                            pe.wait_ge(small_in, 16)
                    if j >= 4:
                        pe.wait_ge(*emptier(j - 4))
                    for k in range(KD):
                        if kind[0] == "f":
                            ins = mm(bank(j % 4), slot(c)[:, k, cols(t)], hT[:, k], start=(k == 0), stop=(k == 7))
                        else:
                            w = 24 if kind == "small" else 512
                            ins = mm(bank(j % 4)[:, 0:w], hT[:, k, cols(t)], slot(c)[:, k, 0:w], start=(k == 0),
                                     stop=(k == 7))
                    ins.then_inc(proj_pe.sem, proj_pe.one("job"))
                    if t == TT - 1:
                        pe.wait_ge(proj_pe.sem, proj_pe.at(j, "job"))
                        pe.sem_inc(chunk_used, 1)
                    ct = j - 12
                    if 1 <= ct <= 8:
                        sums(ct - 1)

            def gla(t):
                if t:
                    pe.wait_ge(GLA_DVE.sem, GLA_DVE.at(t - 1, "on"))
                turn(bank(4)[0:RANK, 0:P], psm[:, t, 0:RANK]).then_inc(GLA_PE.sem, GLA_PE.one("gaT"))
                for n in range(4):
                    ins = turn(bank(6)[:, cols(n)], pqk[:, t, cols(n)])
                ins.then_inc(GLA_PE.sem, GLA_PE.one("qkT"))
                pe.wait_ge(GLA_DVE.sem, GLA_DVE.at(t, "gaT"))
                mm(bank(4)[:, P:P + 256], gaT[0:RANK + 1, :], w2aug[0:RANK + 1, :], start=True, stop=True).then_inc(GLA_PE.sem, GLA_PE.one("z"))
                pe.wait_ge(GLA_DVE.sem, GLA_DVE.at(t, "g"))
                for f in range(2):
                    mm(bank(5)[:, cols(f)], gg[:, cols(f)], cst("tri"), start=True, stop=True)
                mm(bank(5)[:, 256:512], cst("later"), gg, start=True, stop=True).then_inc(GLA_PE.sem, GLA_PE.one("cums"))
                pe.wait_ge(GLA_DVE.sem, GLA_DVE.at(t, "kz"))
                for hd in range(HEADS):
                    ins = mm(bank(7)[:, cols(hd)], kz[:, hd % 2, hd // 2], qd[:, hd // 2], start=True, stop=True)
                ins.then_inc(GLA_PE.sem, GLA_PE.one("A"))
                pe.wait_ge(GLA_DVE.sem, GLA_DVE.at(t, "ku"))
                for c in range(2):
                    for f in range(2):
                        ins = mm(bank(c)[:, 256 * f:256 * f + 256], ku[:, c, cols(f)], pv[:, t, 256 * f:256 * f + 256],
                                 start=True, stop=True)
                    ins.then_inc(GLA_PE.sem, GLA_PE.one(f"u{c}"))
                pe.wait_ge(GLA_DVE.sem, GLA_DVE.at(t, "A"))
                for hd in range(HEADS):
                    ins = mm(bank(2)[:, cols(hd)], at_g[:, hd], pv[:, t, cols(hd)], start=(hd == 0), stop=False,
                             skip_group_check=True)
                ins.then_inc(GLA_PE.sem, GLA_PE.one("o"))
                for c in range(2):
                    if c:
                        pe.wait_ge(GLA_DVE.sem, GLA_DVE.at(t, "s0"))
                    r = slice(CHUNK * c, CHUNK * c + CHUNK)
                    for f in range(2):
                        ins = mm(bank(2)[r, 256 * f:256 * f + 256], qd[:, f, r], st_g[:, f], start=False, stop=(f == 1),
                                 skip_group_check=True)
                    ins.then_inc(GLA_PE.sem, GLA_PE.one(f"int{c}"))
                pe.wait_ge(GLA_DVE.sem, GLA_DVE.at(t, "on"))
                if t:
                    pe.wait_ge(GLA_ACT.sem, GLA_ACT.at(t - 1, "oT"))
                for hd in range(HEADS):
                    ins = turn(bank(3)[:, cols(hd)], on_g[:, hd])
                ins.then_inc(GLA_PE.sem, GLA_PE.one("oT"))

            def gdn_pre():
                pe.wait_ge(PRE_DVE.sem, PRE_DVE.at(0, "g"))
                gf = g_b.rearrange("p t h -> p (t h)")
                for n, m in enumerate((cst("tri"), cst("later"), cst("in_chunk", 0, P), cst("in_chunk", P, P))):
                    ins = mm(bank(4)[:, 16 * n:16 * n + 16], m, gf, start=True, stop=True)
                ins.then_inc(PRE_PE.sem, PRE_PE.one("cum"))

            def gdn(t):
                tk = slice(3 + P * t, 3 + P * t + P)
                pe.wait_ge(GDN_DVE.sem, GDN_DVE.at(t, "rep"))
                if t:
                    pe.wait_ge(GDN_ACT.sem, GDN_ACT.at(t - 1, "oT"))
                for b, r in ((0, 1), (1, 2)):
                    for hd in range(HEADS):
                        mm(bank(b)[:, cols(hd)], rep[:, 0, hd], cst("tri"), start=True, stop=False)
                        ins = mm(bank(b)[:, cols(hd)], rep[:, r, hd], ident, start=False, stop=True)
                ins.then_inc(GDN_PE.sem, GDN_PE.one("rows"))
                for b, f in ((2, 4), (3, 0)):
                    for hd in range(HEADS):
                        ins = mm(bank(b)[:, cols(hd)], qkvT[:, 4 + hd, tk], qkvT[:, f + hd, tk], start=True, stop=True)
                ins.then_inc(GDN_PE.sem, GDN_PE.one("kk"))
                for b, f in ((6, 4), (7, 8)):
                    for hd in range(HEADS):
                        ins = turn(bank(b)[:, cols(hd)], qkvT[:, f + hd, tk])
                ins.then_inc(GDN_PE.sem, GDN_PE.one("kv"))
                pe.wait_ge(GDN_DVE.sem, GDN_DVE.at(t, "xt0"))
                for hd in range(HEADS):
                    ins = turn(bank(2)[:, cols(hd)], xt[:, hd])
                ins.then_inc(GDN_PE.sem, GDN_PE.one("x0"))
                pe.wait_ge(GDN_ACT.sem, GDN_ACT.at(t, "x0"))
                for l in range(1, 6):
                    pe.wait_ge(GDN_DVE.sem, GDN_DVE.at(t, f"atm{l}"))
                    for hd in range(HEADS):
                        ins = mm(bank(6)[:, cols(hd)], atm[:, hd], xx[:, hd], start=True, stop=True)
                    ins.then_inc(GDN_PE.sem, GDN_PE.one(f"p{l}"))
                    pe.wait_ge(GDN_ACT.sem, GDN_ACT.at(t, f"p{l}"))
                    for hd in range(HEADS):
                        ins = mm(bank(7)[:, cols(hd)], pm[:, hd], xt[:, hd], start=True, stop=True)
                    if l < 5:
                        for hd in range(HEADS):
                            ins = mm(bank(2)[:, cols(hd)], xt[:, hd], pm[:, hd], start=True, stop=True)
                    ins.then_inc(GDN_PE.sem, GDN_PE.one(f"y{l}"))
                pe.wait_ge(GDN_DVE.sem, GDN_DVE.at(t, "xt5"))
                for hd in range(HEADS):
                    mm(bank(3)[:, cols(hd)], xt[:, hd], vb_b[:, hd], start=True, stop=True)
                for hd in range(HEADS):
                    ins = mm(bank(6)[:, cols(hd)], kb_b[:, hd], xt[:, hd], start=True, stop=True)
                ins.then_inc(GDN_PE.sem, GDN_PE.one("uw"))
                pe.wait_ge(GDN_ACT.sem, GDN_ACT.at(t, "wT"))
                for c in range(2):
                    r = slice(CHUNK * c, CHUNK * c + CHUNK)
                    if c:
                        pe.wait_ge(GDN_DVE.sem, GDN_DVE.at(t, "s0"))
                    for hd in range(HEADS):
                        ins = mm(bank(4)[r, cols(hd)], wt_b[:, hd, r], st_b[:, hd], start=True, stop=True)
                    ins.then_inc(GDN_PE.sem, GDN_PE.one(f"ws{c}"))
                    pe.wait_ge(GDN_DVE.sem, GDN_DVE.at(t, f"vn{c}"))
                    for hd in range(HEADS):
                        mm(bank(0)[r, cols(hd)], qd_b[:, hd, r], st_b[:, hd], start=True, stop=False)
                        ins = mm(bank(0)[r, cols(hd)], qkt[:, hd, r], vn[:, hd], start=False, stop=True)
                    ins.then_inc(GDN_PE.sem, GDN_PE.one(f"o{c}"))
                    for hd in range(HEADS):
                        ins = mm(bank(5)[:, cols(hd)], ku_b[:, c, hd], vn[:, hd], start=True, stop=True)
                    ins.then_inc(GDN_PE.sem, GDN_PE.one(f"up{c}"))
                pe.wait_ge(GDN_DVE.sem, GDN_DVE.at(t, "on"))
                for hd in range(HEADS):
                    ins = turn(bank(1)[:, cols(hd)], on_b[:, hd])
                ins.then_inc(GDN_PE.sem, GDN_PE.one("oT"))

            def project_out(l):
                key = ("abo", 0) if l == 0 else ("swo", 1)
                for n in range(2):
                    c = first[key] + n
                    pe.wait_ge(chunk_in[c % RING], loaded(c))
                    for t in range(TT):
                        j = 8 * l + 4 * n + t
                        if j >= 4:
                            pe.wait_ge(outp_dve.sem, outp_dve.at(j - 4, "tmp"))
                        for k in range(KD):
                            ins = mm(bank(t), oT[:, k, cols(t)], slot(c)[:, k], start=(k == 0), stop=(k == 7))
                        ins.then_inc(outp_pe.sem, outp_pe.one("job"))
                    pe.wait_ge(outp_pe.sem, outp_pe.at(j, "job"))
                    pe.sem_inc(chunk_used, 1)

            def project_swa():
                pe.wait_ge(norm_act.sem, norm_act.at(2, "ev3"))
                pe.wait_ge(norm_dve.sem, norm_dve.at(2, "ev3"))
                for jj, (n, t) in enumerate(swa_jobs):
                    j = NJ + jj
                    c = first[("swa", 1)] + n
                    if t == 0:
                        pe.wait_ge(chunk_in[c % RING], loaded(c))
                    if jj >= 4:
                        pe.wait_ge(*emptier(j - 4))
                    for k in range(KD):
                        ins = mm(bank(j % 4), hT[:, k, cols(t)], slot(c)[:, k], start=(k == 0), stop=(k == 7))
                    ins.then_inc(proj_pe.sem, proj_pe.one("job"))
                    if t == TT - 1:
                        pe.wait_ge(proj_pe.sem, proj_pe.at(j, "job"))
                        pe.sem_inc(chunk_used, 1)

            def swa():
                for t in range(TT):
                    pe.wait_ge(QK_DVE.sem, QK_DVE.at(0, f"rope{t}"))
                    if t:
                        pe.wait_ge(QT_ACT.sem, QT_ACT.at(t - 1, "q"))
                        pe.wait_ge(QK_DVE.sem, QK_DVE.at(0, f"k{t - 1}"))
                    for n in range(8):
                        ins = turn(bank(n // 4)[:, cols(n % 4)], p2[:, t, cols(n)])
                    ins.then_inc(QK_PE.sem, QK_PE.one(f"q{t}"))
                    for n in range(2):
                        ins = turn(bank(2)[:, cols(n)], p2[:, t, QW + P * n:QW + P * n + P])
                    ins.then_inc(QK_PE.sem, QK_PE.one(f"k{t}"))
                pe.wait_ge(QT_ACT.sem, QT_ACT.at(TT - 1, "q"))
                pe.wait_ge(QK_DVE.sem, QK_DVE.at(0, "q3"))
                for t in range(TT):
                    for n in range(8):
                        if n >= 4:
                            pe.wait_ge(SWA_DVE.sem, SWA_DVE.at(t, f"s{n - 4}"))
                        ins = mm(bank(n % 4)[:, 0:384], qT[:, n, cols(t)], kTz[:, n // 2, :, P * t:P * t + 192],
                                 start=True, stop=True)
                        ins.then_inc(SWA_PE.sem, SWA_PE.one(f"s{n}"))
                    pe.wait_ge(SWA_DVE.sem, SWA_DVE.at(t, "p"))
                    if t:
                        pe.wait_ge(SWA_ACT.sem, SWA_ACT.at(t - 1, "o"))
                    for n in range(9):
                        if n < 8:
                            if n >= 2:
                                pe.wait_ge(SWA_ACT.sem, SWA_ACT.at(t, f"t{n - 2}"))
                            for hh in range(2):
                                for own in range(0 if t else 1, 2):
                                    ins = turn(bank(4 + n % 2)[:, cols(2 * hh + own)], sm[:, 2 * n + hh, cols(own)])
                            ins.then_inc(SWA_PE.sem, SWA_PE.one(f"t{n}"))
                            pe.wait_ge(SWA_ACT.sem, SWA_ACT.at(t, f"t{n}"))
                            for hh in range(2):
                                o = bank(6 + n // 4)[64 * hh:64 * hh + 64, cols(n % 4)]
                                kv = 1280 + 64 * (n // 2)
                                if t:
                                    mm(o, p2[:, t - 1, kv:kv + 64], pT[:, n % 2, hh, 0], start=True, stop=False)
                                ins = mm(o, p2[:, t, kv:kv + 64], pT[:, n % 2, hh, 1], start=(t == 0), stop=True)
                            ins.then_inc(SWA_PE.sem, SWA_PE.one(f"v{n}"))

            def router(l):
                pe.wait_ge(norm_act.sem, norm_act.at(2 * l + 1, "ev3"))
                pe.wait_ge(norm_dve.sem, norm_dve.at(2 * l + 1, "ev3"))
                for t in range(TT):
                    for k in range(KD):
                        ins = mm(bank(0, TT, NE)[:, t], hT[:, k, cols(t)], router_w[:, k], start=(k == 0), stop=(k == 7))
                ins.then_inc(RT_PE.sem, RT_PE.one("logits"))
                pe.wait_ge(RT_DVE.sem, RT_DVE.at(l, "mk"))
                for t in range(TT):
                    for u in range(t + 1):
                        mm(bank(1, TT, NE)[:, t], cst("before") if u == t else cst("ones"), mk[:, u], start=(u == 0), stop=(u == t))
                for u in range(TT):
                    ins = mm(bank(1)[:, 64:64 + NE], cst("ones"), mk[:, u], start=(u == 0), stop=(u == TT - 1))
                ins.then_inc(RT_PE.sem, RT_PE.one("pos"))

            def expert_block(st, i, E, weights_ready, gate_used, chunk_done):
                S, SA, SV = st
                pe.wait_ge(SV.sem, SV.at(i, "disp"))
                for k in range(KD):
                    if k >= 4:
                        copier = SA if k % 2 == 0 else SV
                        pe.wait_ge(copier.sem, copier.at(i, f"hg{k - 4}"))
                    for t in range(TT):
                        ins = mm(bank(k % 4)[:, 0:E * P], h[:, t, cols(k)], pd[:, t, 0:E * P], start=(t == 0), stop=(t == 3))
                    ins.then_inc(S.sem, S.one(f"hg{k}"))
                for e in range(E):
                    if e >= 2:
                        copier = SA if e % 2 == 0 else SV
                        pe.wait_ge(copier.sem, copier.at(i, f"pT{e - 2}"))
                    for t in range(TT):
                        ins = turn(bank(6 + e % 2)[:, cols(t)], pd[:, t, cols(e)])
                    ins.then_inc(S.sem, S.one(f"pT{e}"))
                for e in range(E):
                    for t in range(TT):
                        ins = mm(bank(5)[:, e:e + 1], pd[:, t, cols(e)], wcol[:, t, e:e + 1], start=(t == 0), stop=(t == 3))
                ins.then_inc(S.sem, S.one("ws"))
                pe.wait_ge(SA.sem, SA.at(i, f"hg{KD - 2}"))
                pe.wait_ge(SV.sem, SV.at(i, "ws"))
                pe.wait_ge(SA.sem, SA.at(i, "pT2" if E > 2 else "pT0"))
                for e in range(E):
                    if e:
                        pe.wait_ge(SA.sem, SA.at(i, f"sg{e - 1}"))
                    gate, up, down = weights_ready(e, 0)
                    for k in range(KD):
                        ins = mm(bank(4), hgT[:, k, cols(e)], gate[:, k], start=(k == 0), stop=(k == 7))
                    ins.then_inc(S.sem, S.one(f"g{e}"))
                    if e:
                        pe.wait_ge(SV.sem, SV.at(i, f"he{e - 1}"))
                    weights_ready(e, 1)
                    for k in range(KD):
                        ins = mm(bank(5), hgT[:, k, cols(e)], up[:, k], start=(k == 0), stop=(k == 7))
                        if k == 0:
                            gate_used(ins)
                    ins.then_inc(S.sem, S.one(f"u{e}"))
                    pe.wait_ge(S.sem, S.at(i, f"u{e}"))
                    chunk_done(e, 1)
                    pe.wait_ge(SV.sem, SV.at(i, f"he{e}"))
                    for n in range(4):
                        ins = turn(bank(6)[:, cols(n)], he[:, cols(n)])
                    ins.then_inc(S.sem, S.one(f"hT{e}"))
                    weights_ready(e, 2)
                    pe.wait_ge(SA.sem, SA.at(i, f"hT{e}"))
                    if e:
                        pe.wait_ge(SV.sem, SV.at(i, f"y1{e - 1}"))
                    for half, b in ((0, 7), (1, 3)):
                        for n in range(4):
                            ins = mm(bank(b), heT[:, n], down[:, n, 512 * half:512 * half + 512], start=(n == 0), stop=(n == 3))
                        ins.then_inc(S.sem, S.one(f"y{half}{e}"))
                    pe.wait_ge(S.sem, S.at(i, f"y1{e}"))
                    chunk_done(e, 2)
                pe.wait_ge(SV.sem, SV.at(i, f"y1{E - 1}"))
                for j in range(8):
                    if j >= 4:
                        pe.wait_ge(SV.sem, SV.at(i, f"x{j - 4}"))
                    t, half = j // 2, j % 2
                    for e in range(E):
                        ins = mm(bank(j % 4), pdT[:, e, cols(t)], ys[:, e, 512 * half:512 * half + 512], start=(e == 0), stop=(e == E - 1))
                    ins.then_inc(S.sem, S.one(f"c{j}"))

            def experts(l):
                c0 = first[("moe", l)]
                S = moe_steps[l][0]
                pe.sem_inc(S.sem, S.n)
                pe.sem_inc(over_steps[l][0].sem, over_steps[l][0].n)
                with pe.Fori(0, NE // EG) as i:
                    def ready(e, w):
                        c = c0 + 3 * e + w
                        pe.wait_ge(chunk_in[c % RING], 16 * (c // RING + 1) + 16 * (3 * EG // RING) * i)
                        cc = c - w
                        return expert_view(slot(cc), 0), expert_view(slot(cc + 1), 1), expert_view(slot(cc + 2), 2)

                    expert_block(moe_steps[l], i, EG, ready, lambda ins: ins.then_inc(chunk_used, 1),
                                 lambda e, w: pe.sem_inc(chunk_used, 1))
                pe.wait_ge(RT_DVE.sem, RT_DVE.at(l, "ovl"))
                n_over = pe.value_load(ovl_i[0:1, 8:9], min_val=0, max_val=MAXOVER)
                with pe.Fori(0, MAXOVER) as j:
                    with pe.If(n_over > j):
                        def ready(e, w):
                            pe.wait_ge(over_in[l], 48 * j + 48)
                            return tuple(expert_view(ring[:, n], n) for n in range(3))

                        expert_block(over_steps[l], j, 1, ready, lambda ins: None, lambda e, w: None)

            pe.wait_ge(params_in, 16 * NPARAMS)
            pe.wait_ge(const_in, 16)
            ada(0)
            norm(0)
            project_ab()
            nc.tensor.drain().then_inc(phase_done, 1)
            pe.wait_ge(phase_done, 3 * 1)
            pe.wait_ge(params_in, 16 * NPARAMS)
            for t in range(TT):
                gla(t)
            nc.tensor.drain().then_inc(phase_done, 1)
            pe.wait_ge(phase_done, 3 * 2)
            gdn_pre()
            for t in range(TT):
                gdn(t)
            nc.tensor.drain().then_inc(phase_done, 1)
            pe.wait_ge(phase_done, 3 * 3)
            project_out(0)
            nc.tensor.drain().then_inc(phase_done, 1)
            pe.wait_ge(phase_done, 3 * 4)
            norm(1)
            router(0)
            experts(0)
            nc.tensor.drain().then_inc(phase_done, 1)
            pe.wait_ge(phase_done, 3 * 5)
            ada(1)
            norm(2)
            project_swa()
            nc.tensor.drain().then_inc(phase_done, 1)
            pe.wait_ge(phase_done, 3 * 6)
            swa()
            nc.tensor.drain().then_inc(phase_done, 1)
            pe.wait_ge(phase_done, 3 * 7)
            project_out(1)
            nc.tensor.drain().then_inc(phase_done, 1)
            pe.wait_ge(phase_done, 3 * 8)
            norm(3)
            router(1)
            experts(1)
            nc.tensor.drain().then_inc(phase_done, 1)

        @block.scalar
        def _(act):
            def f(out, in_, fn=ACT.Copy, **kw):
                return nc.scalar.activation(out, in_, fn, **kw)

            def norm(s):
                for t in range(TT):
                    f(junk_wide, x[:, t], ACT.Square, accum_out=ss[:, t:t + 1]).then_inc(norm_act.sem, norm_act.one(f"ss{t}"))
                    act.wait_ge(norm_act.sem, norm_act.at(s, f"ss{t}"))
                act.wait_ge(norm_dve.sem, norm_dve.at(s, "var"))
                f(rstd[:], var[:], ACT.Ln).then_inc(norm_act.sem, norm_act.one("ln"))
                act.wait_ge(norm_act.sem, norm_act.at(s, "ln"))
                f(rstd[:], rstd[:], ACT.Exp, scale=-0.5).then_inc(norm_act.sem, norm_act.one("exp"))
                for t in range(TT):
                    act.wait_ge(norm_pe.sem, norm_pe.at(s, f"lo{t}"))
                    f(hT[:, 0:4, cols(t)], bank(4 + 2 * (t % 2), 4, P)).then_inc(norm_act.sem, norm_act.one(f"ev{t}"))

            def project_ab():
                for j, (n, t, kind) in enumerate(jobs):
                    if emptied[j][0] == "s":
                        act.wait_ge(proj_pe.sem, proj_pe.at(j, "job"))
                        src = bank(j % 4)
                        if kind == "qk":
                            ins = f(pqk[:, t], src)
                        elif kind == "v":
                            ins = f(pv[:, t], src)
                        elif kind == "small":
                            ins = f(psm[:, t], src[:, 0:24])
                        elif kind == "za":
                            ins = f(pz[:, t], src, ACT.Silu)
                        elif kind == "zb":
                            ins = f(pzb[:, t], src, ACT.Silu)
                        else:
                            ins = f(qkvT[:, j - 12, 3:3 + SEQ], src)
                        ins.then_inc(proj_act.sem, proj_act.one("ev"))
                    ct = j - 12
                    if 0 <= ct < 12:
                        act.wait_ge(conv_dve.sem, conv_dve.at(ct, "t3"))
                        f(qkvT[:, ct, 3:3 + SEQ], conv_t[:, ct % 2], ACT.Silu).then_inc(conv_act.sem, conv_act.one("silu"))
                        act.wait_ge(conv_act.sem, conv_act.at(ct, "silu"))
                        if 2 <= ct < 10:
                            act.wait_ge(conv_pe.sem, conv_pe.at(ct - 2, "ss"))
                        f(conv_sq[:, ct % 2], qkvT[:, ct, 3:3 + SEQ], ACT.Square).then_inc(conv_act.sem, conv_act.one("sq"))

            def gla(t):
                act.wait_ge(GLA_PE.sem, GLA_PE.at(t, "z"))
                f(az, bank(4)[:, P:P + 256], ACT.Abs).then_inc(GLA_ACT.sem, GLA_ACT.one("abs"))
                act.wait_ge(GLA_ACT.sem, GLA_ACT.at(t, "abs"))
                f(ee, az, ACT.Exp, scale=-1.0).then_inc(GLA_ACT.sem, GLA_ACT.one("e"))
                act.wait_ge(GLA_ACT.sem, GLA_ACT.at(t, "e"))
                f(ee, ee, ACT.Ln, bias=1.0).then_inc(GLA_ACT.sem, GLA_ACT.one("l"))
                act.wait_ge(GLA_PE.sem, GLA_PE.at(t, "cums"))
                bT = bank(5)[:, 0:256].rearrange("p (a b) -> p a b", a=2)
                f(eb, bT, ACT.Exp, scale=1.0 / 16).then_inc(GLA_ACT.sem, GLA_ACT.one("eb"))
                f(enb, bT, ACT.Exp, scale=-1.0 / 16).then_inc(GLA_ACT.sem, GLA_ACT.one("enb"))
                f(ekb, bank(5)[:, 256:512], ACT.Exp, scale=1.0 / 16).then_inc(GLA_ACT.sem, GLA_ACT.one("ekb"))
                act.wait_ge(GLA_PE.sem, GLA_PE.at(t, "int1"))
                for hd in range(HEADS):
                    ins = f(junk[:, cols(hd)], bank(2)[:, cols(hd)], ACT.Square, accum_out=sm_g[:, 0, hd:hd + 1])
                ins.then_inc(GLA_ACT.sem, GLA_ACT.one("ss"))
                act.wait_ge(GLA_DVE.sem, GLA_DVE.at(t, "var"))
                f(sm_g[:, 2], sm_g[:, 1], ACT.Ln).then_inc(GLA_ACT.sem, GLA_ACT.one("ln"))
                act.wait_ge(GLA_ACT.sem, GLA_ACT.at(t, "ln"))
                f(sm_g[:, 2], sm_g[:, 2], ACT.Exp, scale=-0.5).then_inc(GLA_ACT.sem, GLA_ACT.one("exp"))
                act.wait_ge(GLA_PE.sem, GLA_PE.at(t, "oT"))
                f(oT[:, 0:HEADS, cols(t)], bank(3, HEADS, P)).then_inc(GLA_ACT.sem, GLA_ACT.one("oT"))

            def gdn_pre():
                act.wait_ge(PRE_DVE.sem, PRE_DVE.at(0, "au"))
                f(pre_l, pre_a, ACT.Exp, scale=-1.0).then_inc(PRE_ACT.sem, PRE_ACT.one("e"))
                act.wait_ge(PRE_ACT.sem, PRE_ACT.at(0, "e"))
                f(pre_l, pre_l, ACT.Ln, bias=1.0).then_inc(PRE_ACT.sem, PRE_ACT.one("l"))
                f(nexpa, a_log, ACT.Exp).then_inc(PRE_ACT.sem, PRE_ACT.one("expa"))
                f(ssk, ssk, ACT.Ln).then_inc(PRE_ACT.sem, PRE_ACT.one("lnss"))
                act.wait_ge(PRE_DVE.sem, PRE_DVE.at(0, "pre"))
                f(pexp, pre, ACT.Exp).then_inc(PRE_ACT.sem, PRE_ACT.one("exp"))

            def gdn(t):
                act.wait_ge(GDN_DVE.sem, GDN_DVE.at(t, "d2"))
                f(ex, ex, ACT.Exp).then_inc(GDN_ACT.sem, GDN_ACT.one("exp"))
                f(eq, bank(1, HEADS, P), ACT.Exp).then_inc(GDN_ACT.sem, GDN_ACT.one("eq"))
                act.wait_ge(GDN_PE.sem, GDN_PE.at(t, "x0"))
                f(xx, bank(2, HEADS, P)).then_inc(GDN_ACT.sem, GDN_ACT.one("x0"))
                for l in range(1, 6):
                    act.wait_ge(GDN_PE.sem, GDN_PE.at(t, f"p{l}"))
                    f(pm, bank(6, HEADS, P)).then_inc(GDN_ACT.sem, GDN_ACT.one(f"p{l}"))
                act.wait_ge(GDN_PE.sem, GDN_PE.at(t, "uw"))
                f(wt_b, bank(6, HEADS, P)).then_inc(GDN_ACT.sem, GDN_ACT.one("wT"))
                act.wait_ge(GDN_PE.sem, GDN_PE.at(t, "o1"))
                for hd in range(HEADS):
                    ins = f(junk[:, cols(hd)], bank(0)[:, cols(hd)], ACT.Square, accum_out=sm_b[:, 0, hd:hd + 1])
                ins.then_inc(GDN_ACT.sem, GDN_ACT.one("ss"))
                act.wait_ge(GDN_DVE.sem, GDN_DVE.at(t, "var"))
                f(sm_b[:, 2], sm_b[:, 1], ACT.Ln).then_inc(GDN_ACT.sem, GDN_ACT.one("ln"))
                act.wait_ge(GDN_ACT.sem, GDN_ACT.at(t, "ln"))
                f(sm_b[:, 2], sm_b[:, 2], ACT.Exp, scale=-0.5).then_inc(GDN_ACT.sem, GDN_ACT.one("rs"))
                act.wait_ge(GDN_PE.sem, GDN_PE.at(t, "oT"))
                f(oT[:, HEADS:2 * HEADS, cols(t)], bank(1, HEADS, P)).then_inc(GDN_ACT.sem, GDN_ACT.one("oT"))

            def project_swa():
                for jj, (n, t) in enumerate(swa_jobs):
                    j = NJ + jj
                    if emptied[j][0] == "s":
                        act.wait_ge(proj_pe.sem, proj_pe.at(j, "job"))
                        f(p2[:, t, 512 * n:512 * n + 512], bank(j % 4)).then_inc(proj_act.sem, proj_act.one("ev"))

            def swa():
                act.wait_ge(ROPE_DVE.sem, ROPE_DVE.at(0, "c"))
                f(sn, rr, ACT.Sin).then_inc(ROPE_ACT.sem, ROPE_ACT.one("sin"))
                f(cs, rc, ACT.Sin).then_inc(ROPE_ACT.sem, ROPE_ACT.one("cos"))
                for t in range(TT):
                    if t:
                        act.wait_ge(QK_DVE.sem, QK_DVE.at(0, f"ss{t - 1}"))
                    f(sq2, p2[:, t, 0:1280], ACT.Square).then_inc(QK_ACT.sem, QK_ACT.one(f"sq{t}"))
                act.wait_ge(QK_DVE.sem, QK_DVE.at(0, "var"))
                f(qk_s[:, 2], qk_s[:, 1], ACT.Ln).then_inc(QK_ACT.sem, QK_ACT.one("ln"))
                act.wait_ge(QK_ACT.sem, QK_ACT.at(0, "ln"))
                f(qk_s[:, 2], qk_s[:, 2], ACT.Exp, scale=-0.5).then_inc(QK_ACT.sem, QK_ACT.one("exp"))
                for t in range(TT):
                    act.wait_ge(QK_PE.sem, QK_PE.at(0, f"q{t}"))
                    f(qT[:, 0:4, cols(t)], bank(0, 4, P))
                    f(qT[:, 4:8, cols(t)], bank(1, 4, P)).then_inc(QT_ACT.sem, QT_ACT.one("q"))
                for t in range(TT):
                    act.wait_ge(SWA_DVE.sem, SWA_DVE.at(t, "es"))
                    f(sw_s[:, 4], sw_s[:, 3], ACT.Exp).then_inc(SWA_ACT.sem, SWA_ACT.one("es"))
                    for hd in range(NQ):
                        ins = f(sm[:, hd, 64:256], sm[:, hd, 64:256], ACT.Exp, bias=sw_s[:, 2, hd:hd + 1],
                                accum_out=sw_s[:, 5, hd:hd + 1])
                    ins.then_inc(SWA_ACT.sem, SWA_ACT.one("exp"))
                    for n in range(8):
                        act.wait_ge(SWA_PE.sem, SWA_PE.at(t, f"t{n}"))
                        if n >= 2:
                            act.wait_ge(SWA_PE.sem, SWA_PE.at(t, f"v{n - 2}"))
                        lo = 0 if t else 1
                        f(pT[:, n % 2, :, lo:2], bank(4 + n % 2, 2, 2, P)[:, :, lo:2]).then_inc(SWA_ACT.sem, SWA_ACT.one(f"t{n}"))
                    act.wait_ge(SWA_PE.sem, SWA_PE.at(t, "v7"))
                    f(oT[:, 0:4, cols(t)], bank(6, 4, P))
                    f(oT[:, 4:8, cols(t)], bank(7, 4, P)).then_inc(SWA_ACT.sem, SWA_ACT.one("o"))

            def expert_block(st, i, E):
                S, SA, SV = st
                for k in range(0, KD, 2):
                    act.wait_ge(S.sem, S.at(i, f"hg{k}"))
                    f(hgT[:, k, 0:E * P], bank(k % 4)[:, 0:E * P]).then_inc(SA.sem, SA.one(f"hg{k}"))
                for e in range(0, E, 2):
                    act.wait_ge(S.sem, S.at(i, f"pT{e}"))
                    f(pdT[:, e], bank(6 + e % 2)).then_inc(SA.sem, SA.one(f"pT{e}"))
                for e in range(E):
                    act.wait_ge(S.sem, S.at(i, f"g{e}"))
                    if e:
                        act.wait_ge(SV.sem, SV.at(i, f"he{e - 1}"))
                    f(sg, bank(4), ACT.Silu).then_inc(SA.sem, SA.one(f"sg{e}"))
                    act.wait_ge(S.sem, S.at(i, f"hT{e}"))
                    if e:
                        act.wait_ge(S.sem, S.at(i, f"y1{e - 1}"))
                    f(heT, bank(6, 4, P)).then_inc(SA.sem, SA.one(f"hT{e}"))

            def experts(l):
                act.wait_ge(RT_PE.sem, RT_PE.at(l, "logits"))
                f(r_e, bank(0, TT, NE), ACT.Exp, scale=-1.0).then_inc(RT_ACT.sem, RT_ACT.one("exp"))
                act.sem_inc(moe_steps[l][1].sem, moe_steps[l][1].n)
                act.sem_inc(over_steps[l][1].sem, over_steps[l][1].n)
                with act.Fori(0, NE // EG) as i:
                    expert_block(moe_steps[l], i, EG)
                act.wait_ge(RT_DVE.sem, RT_DVE.at(l, "ovl"))
                n_over = act.value_load(ovl_i[0:1, 8:9], min_val=0, max_val=MAXOVER)
                with act.Fori(0, MAXOVER) as j:
                    with act.If(n_over > j):
                        expert_block(over_steps[l], j, 1)

            act.wait_ge(params_in, 16 * NPARAMS)
            f(junk_wide[:, 0:KD], cond, ACT.Exp, scale=-1.0).then_inc(cond_act.sem, cond_act.one("exp"))
            act.wait_ge(x_in, 16)
            act.wait_ge(cond_dve.sem, cond_dve.at(0, "silu"))
            norm(0)
            project_ab()
            nc.scalar.drain().then_inc(phase_done, 1)
            act.wait_ge(phase_done, 3 * 1)
            for t in range(TT):
                gla(t)
            nc.scalar.drain().then_inc(phase_done, 1)
            act.wait_ge(phase_done, 3 * 2)
            gdn_pre()
            for t in range(TT):
                gdn(t)
            nc.scalar.drain().then_inc(phase_done, 1)
            act.wait_ge(phase_done, 3 * 3)
            nc.scalar.drain().then_inc(phase_done, 1)
            act.wait_ge(phase_done, 3 * 4)
            norm(1)
            experts(0)
            nc.scalar.drain().then_inc(phase_done, 1)
            act.wait_ge(phase_done, 3 * 5)
            norm(2)
            project_swa()
            nc.scalar.drain().then_inc(phase_done, 1)
            act.wait_ge(phase_done, 3 * 6)
            swa()
            nc.scalar.drain().then_inc(phase_done, 1)
            act.wait_ge(phase_done, 3 * 7)
            nc.scalar.drain().then_inc(phase_done, 1)
            act.wait_ge(phase_done, 3 * 8)
            norm(3)
            experts(1)
            nc.scalar.drain().then_inc(phase_done, 1)

        @block.vector
        def _(dve):
            v = nc.vector

            def newton(st, r, y, vr, t1, last="rstd"):
                v.tensor_tensor(t1, y, y, ALU.mult).then_inc(st.sem, st.one("n1"))
                dve.wait_ge(st.sem, st.at(r, "n1"))
                v.tensor_tensor(t1, t1, vr, ALU.mult).then_inc(st.sem, st.one("n2"))
                dve.wait_ge(st.sem, st.at(r, "n2"))
                v.tensor_scalar(t1, t1, -0.5, 1.5, ALU.mult, ALU.add).then_inc(st.sem, st.one("n3"))
                dve.wait_ge(st.sem, st.at(r, "n3"))
                v.tensor_tensor(y, y, t1, ALU.mult).then_inc(st.sem, st.one(last))
                dve.wait_ge(st.sem, st.at(r, last))

            def ada(l):
                if l == 0:
                    dve.wait_ge(cond_act.sem, cond_act.at(0, "exp"))
                    v.tensor_scalar(junk_wide[:, KD:2 * KD], junk_wide[:, 0:KD], 1.0, None, ALU.add).then_inc(cond_dve.sem, cond_dve.one("e1"))
                    dve.wait_ge(cond_dve.sem, cond_dve.at(0, "e1"))
                    v.reciprocal(junk_wide[:, 2 * KD:3 * KD], junk_wide[:, KD:2 * KD]).then_inc(cond_dve.sem, cond_dve.one("rec"))
                    dve.wait_ge(cond_dve.sem, cond_dve.at(0, "rec"))
                    v.tensor_tensor(cond, cond, junk_wide[:, 2 * KD:3 * KD], ALU.mult).then_inc(cond_dve.sem, cond_dve.one("silu"))
                    dve.wait_ge(cond_dve.sem, cond_dve.at(0, "silu"))
                v.tensor_copy(cond_rep, cond.unsqueeze(2).to_broadcast([P, KD, P])).then_inc(rep_dve.sem, rep_dve.one("rep"))
                dve.wait_ge(bias_in[l], 48)
                for n in range(12):
                    r = 12 * l + n
                    dve.wait_ge(ada_pe.sem, ada_pe.at(r, "mod"))
                    m = mod[:, 512 * n:512 * n + 512]
                    v.tensor_tensor(m, bank(n % 4), m, ALU.add).then_inc(ada_dve.sem, ada_dve.one("mod"))
                dve.wait_ge(ada_dve.sem, ada_dve.at(r, "mod"))
                for name, lo, g in (("a1", D, gain1), ("a2", 4 * D, gain2)):
                    s = mod[:, lo:lo + D]
                    v.scalar_tensor_tensor(out=s, in0=s, scalar=1.0, in1=g, op0=ALU.add, op1=ALU.mult).then_inc(amod_dve.sem, amod_dve.one(name))
                    dve.wait_ge(amod_dve.sem, amod_dve.at(l, name))

            def norm(s):
                lo = 3 * D * (s % 2)
                shift, scale = mod[:, lo:lo + D], mod[:, lo + D:lo + 2 * D]
                dve.wait_ge(norm_act.sem, norm_act.at(s, "ss3"))
                v.tensor_scalar(var[:], ss[:], 1.0 / D, EPS, ALU.mult, ALU.add).then_inc(norm_dve.sem, norm_dve.one("var"))
                dve.wait_ge(norm_act.sem, norm_act.at(s, "exp"))
                dve.wait_ge(norm_dve.sem, norm_dve.at(s, "var"))
                newton(norm_dve, s, rstd[:], var[:], nt1[:])
                for t in range(TT):
                    v.scalar_tensor_tensor(out=h[:, t], in0=x[:, t], scalar=rstd[:, t:t + 1], in1=scale,
                                                                 op0=ALU.mult, op1=ALU.mult).then_inc(norm_dve.sem, norm_dve.one(f"hx{t}"))
                    dve.wait_ge(norm_dve.sem, norm_dve.at(s, f"hx{t}"))
                    v.tensor_tensor(h[:, t], h[:, t], shift, ALU.add).then_inc(norm_dve.sem, norm_dve.one(f"h{t}"))
                for t in range(TT):
                    dve.wait_ge(norm_pe.sem, norm_pe.at(s, f"hi{t}"))
                    v.tensor_copy(hT[:, 4:8, cols(t)], bank(5 + 2 * (t % 2), 4, P)).then_inc(norm_dve.sem, norm_dve.one(f"ev{t}"))

            def project_ab():
                dve.wait_ge(norm_pe.sem, norm_pe.at(0, "hi3"))
                v.memset(qkvT[:, :, 0:3], 0.0).then_inc(init_dve, 1)
                dve.wait_ge(init_dve, 1)
                for j, (n, t, kind) in enumerate(jobs):
                    if emptied[j][0] == "v":
                        dve.wait_ge(proj_pe.sem, proj_pe.at(j, "job"))
                        src = bank(j % 4)
                        dst = {"qk": pqk[:, t], "v": pv[:, t]}.get(kind)
                        if kind == "small":
                            dst, src = psm[:, t], src[:, 0:24]
                        elif kind[0] == "f":
                            dst = qkvT[:, j - 12, 3:3 + SEQ]
                        v.tensor_copy(dst, src).then_inc(proj_dve.sem, proj_dve.one("ev"))
                    ct = j - 12
                    if 0 <= ct < 12:
                        dve.wait_ge(*emptier(j))
                        if ct >= 2:
                            dve.wait_ge(conv_act.sem, conv_act.at(ct - 2, "silu"))
                        acc = conv_t[:, ct % 2]
                        v.tensor_scalar(acc, qkvT[:, ct, 0:SEQ], conv_w[:, ct, 0:1], None, ALU.mult).then_inc(conv_dve.sem, conv_dve.one("t0"))
                        dve.wait_ge(conv_dve.sem, conv_dve.at(ct, "t0"))
                        for k in range(1, 4):
                            ins = v.scalar_tensor_tensor(out=acc, in0=qkvT[:, ct, k:k + SEQ], scalar=conv_w[:, ct, k:k + 1],
                                                         in1=acc, op0=ALU.mult, op1=ALU.add)
                            ins.then_inc(conv_dve.sem, conv_dve.one(f"t{k}"))
                            dve.wait_ge(conv_dve.sem, conv_dve.at(ct, f"t{k}"))
                dve.wait_ge(conv_pe.sem, conv_pe.at(7, "ss"))
                v.tensor_scalar(ssk, bank(5, TT, 8), EPS, None, ALU.add)

            def gla(t):
                dve.wait_ge(GLA_PE.sem, GLA_PE.at(t, "gaT"))
                v.tensor_copy(gaT[0:RANK, :], bank(4)[0:RANK, 0:P]).then_inc(GLA_DVE.sem, GLA_DVE.one("gaT"))
                dve.wait_ge(GLA_PE.sem, GLA_PE.at(t, "z"))
                z = bank(4)[:, P:P + 256]
                dve.wait_ge(GLA_ACT.sem, GLA_ACT.at(t, "l"))
                v.scalar_tensor_tensor(out=gg, in0=z, scalar=0.0, in1=ee, op0=ALU.min, op1=ALU.subtract).then_inc(GLA_DVE.sem, GLA_DVE.one("g"))
                dve.wait_ge(GLA_ACT.sem, GLA_ACT.at(t, "ekb"))
                v.scalar_tensor_tensor(out=qd, in0=bank(6, 4, P)[:, 0:2], scalar=GLA_DK ** -0.5, in1=eb,
                                                    op0=ALU.mult, op1=ALU.mult).then_inc(GLA_DVE.sem, GLA_DVE.one("qd"))
                for par_ in range(2):
                    r = slice(64 * par_, 64 * par_ + 64)
                    ins = v.tensor_tensor(kz[r, par_], bank(6, 4, P)[r, 2:4], enb[r], ALU.mult)
                ins.then_inc(GLA_DVE.sem, GLA_DVE.one("kz"))
                for c in range(2):
                    r = slice(CHUNK * c, CHUNK * c + CHUNK)
                    ins = v.tensor_tensor(ku[r, c], pqk[r, t, 256:512], ekb[r], ALU.mult)
                ins.then_inc(GLA_DVE.sem, GLA_DVE.one("ku"))
                dve.wait_ge(GLA_PE.sem, GLA_PE.at(t, "A"))
                mask = cst("tri").bitcast(U32).unsqueeze(1).to_broadcast([P, HEADS, P])
                v.copy_predicated(at_g, mask, bank(7, HEADS, P)).then_inc(GLA_DVE.sem, GLA_DVE.one("A"))
                for c in range(2):
                    dve.wait_ge(GLA_PE.sem, GLA_PE.at(t, f"int{c}"))
                    for hd in range(HEADS):
                        f, r = hd // 2, slice(64 * (hd % 2), 64 * (hd % 2) + 64)
                        s = st_g[r, f, cols(hd % 2)]
                        ins = v.scalar_tensor_tensor(out=s, in0=s, scalar=eb[r, f, 64 * c + 63:64 * c + 64],
                                                     in1=bank(c)[r, 256 * f + P * (hd % 2):256 * f + P * (hd % 2) + P],
                                                     op0=ALU.mult, op1=ALU.add)
                    ins.then_inc(GLA_DVE.sem, GLA_DVE.one(f"s{c}"))
                    dve.wait_ge(GLA_DVE.sem, GLA_DVE.at(t, f"s{c}"))
                if t:
                    dve.wait_ge(GLA_PE.sem, GLA_PE.at(t - 1, "oT"))
                v.tensor_tensor(on_g, pz[:, t].rearrange("p (a b) -> p a b", a=HEADS),
                                             gla_gain.unsqueeze(1).to_broadcast([P, HEADS, P]), ALU.mult).then_inc(GLA_DVE.sem, GLA_DVE.one("zg"))
                head_norm(GLA_DVE, GLA_ACT, t, sm_g, bank(2), on_g, on_g, "exp")

            def head_norm(st, st_act, t, sm, o, zg, on, exp_name):
                dve.wait_ge(st_act.sem, st_act.at(t, "ss"))
                v.tensor_scalar(sm[:, 1], sm[:, 0], 1.0 / DV, EPS, ALU.mult, ALU.add).then_inc(st.sem, st.one("var"))
                dve.wait_ge(st_act.sem, st_act.at(t, exp_name))
                dve.wait_ge(st.sem, st.at(t, "var"))
                newton(st, t, sm[:, 2], sm[:, 1], sm[:, 3])
                for hd in range(HEADS):
                    ins = v.scalar_tensor_tensor(out=on[:, hd], in0=o[:, cols(hd)], scalar=sm[:, 2, hd:hd + 1],
                                                 in1=zg[:, hd], op0=ALU.mult, op1=ALU.mult)
                ins.then_inc(st.sem, st.one("on"))

            def gdn_pre():
                D_ = PRE_DVE
                v.tensor_tensor(pre_u[:, :, 0:4], psm[:, :, 16:20], dt_bias.unsqueeze(1).to_broadcast([P, TT, HEADS]), ALU.add)
                v.tensor_copy(pre_u[:, :, 4:8], psm[:, :, 20:24]).then_inc(D_.sem, D_.one("u"))
                dve.wait_ge(D_.sem, D_.at(0, "u"))
                v.scalar_tensor_tensor(out=pre_a, in0=pre_u, scalar=-1.0, in1=pre_u, op0=ALU.mult, op1=ALU.max).then_inc(D_.sem, D_.one("au"))
                dve.wait_ge(PRE_ACT.sem, PRE_ACT.at(0, "expa"))
                v.scalar_tensor_tensor(out=pre_a[:, :, 0:4], in0=pre_u[:, :, 0:4], scalar=0.0, in1=pre_l[:, :, 0:4],
                                                       op0=ALU.max, op1=ALU.add).then_inc(D_.sem, D_.one("mx"))
                dve.wait_ge(D_.sem, D_.at(0, "mx"))
                v.scalar_tensor_tensor(out=g_b, in0=pre_a[:, :, 0:4], scalar=-1.0,
                                               in1=nexpa.unsqueeze(1).to_broadcast([P, TT, HEADS]), op0=ALU.mult, op1=ALU.mult).then_inc(D_.sem, D_.one("g"))
                v.scalar_tensor_tensor(out=lnb, in0=pre_u[:, :, 4:8], scalar=0.0, in1=pre_l[:, :, 4:8],
                                               op0=ALU.min, op1=ALU.subtract).then_inc(D_.sem, D_.one("lnb"))
                dve.wait_ge(PRE_ACT.sem, PRE_ACT.at(0, "lnss"))
                v.tensor_scalar(lk, ssk[:, :, 4:8], -0.5, None, ALU.mult).then_inc(D_.sem, D_.one("lk"))
                v.tensor_scalar(lq, ssk[:, :, 0:4], -0.5, float(-0.5 * np.log(DV)), ALU.mult, ALU.add).then_inc(D_.sem, D_.one("lq"))
                dve.wait_ge(D_.sem, D_.at(0, "lq"))
                v.tensor_tensor(lbk, lnb, lk, ALU.add).then_inc(D_.sem, D_.one("lbk"))
                dve.wait_ge(D_.sem, D_.at(0, "lbk"))
                dve.wait_ge(PRE_PE.sem, PRE_PE.at(0, "cum"))
                cum = bank(4)[:, 0:64].rearrange("p (n t h) -> p n t h", n=4, t=TT)
                v.tensor_copy(pre[:, 0], lnb)
                v.tensor_tensor(pre[:, 1], cum[:, 0], lbk, ALU.add)
                v.tensor_tensor(pre[:, 2], cum[:, 1], lk, ALU.add)
                v.tensor_copy(pre[:, 3:5], cum[:, 2:4]).then_inc(D_.sem, D_.one("pre"))
                v.tensor_tensor(colj, lk, cum[:, 0], ALU.subtract).then_inc(D_.sem, D_.one("colj"))
                dve.wait_ge(D_.sem, D_.at(0, "colj"))
                dve.wait_ge(PRE_ACT.sem, PRE_ACT.at(0, "exp"))

            def gdn(t):
                S = GDN_DVE
                for n, src in enumerate((g_b, lbk, lq)):
                    ins = v.tensor_copy(rep[:, n], src[:, t].unsqueeze(2).to_broadcast([P, HEADS, P]))
                ins.then_inc(S.sem, S.one("rep"))
                dve.wait_ge(GDN_PE.sem, GDN_PE.at(t, "rows"))
                for n, (name, m) in enumerate((("d1", "strict_bias"), ("d2", "incl_bias"))):
                    for hd in range(HEADS):
                        ins = v.scalar_tensor_tensor(out=ex[:, n, hd], in0=bank(n)[:, cols(hd)], scalar=colj[:, t, hd:hd + 1],
                                                     in1=cst(m), op0=ALU.add, op1=ALU.add)
                    ins.then_inc(S.sem, S.one(name))
                dve.wait_ge(GDN_PE.sem, GDN_PE.at(t, "kk"))
                dve.wait_ge(GDN_ACT.sem, GDN_ACT.at(t, "exp"))
                v.tensor_tensor(atb, bank(2, HEADS, P), ex[:, 0], ALU.mult).then_inc(S.sem, S.one("at"))
                v.tensor_tensor(qkt, bank(3, HEADS, P), ex[:, 1], ALU.mult).then_inc(S.sem, S.one("qk"))
                dve.wait_ge(GDN_ACT.sem, GDN_ACT.at(t, "eq"))
                v.tensor_tensor(qd_b, qkvT[:, 0:4, 3 + P * t:3 + P * t + P], eq, ALU.mult).then_inc(S.sem, S.one("qd"))
                dve.wait_ge(GDN_PE.sem, GDN_PE.at(t, "kv"))

                def by_token(n, r):
                    return pexp[r, n, t].unsqueeze(2).to_broadcast([r.stop - r.start, HEADS, P])

                for c in range(2):
                    r = slice(CHUNK * c, CHUNK * c + CHUNK)
                    ins = v.tensor_tensor(ku_b[r, c], bank(6, HEADS, P)[r], by_token(2, r), ALU.mult)
                ins.then_inc(S.sem, S.one("ku"))
                every = slice(0, P)
                v.tensor_tensor(kb_b, bank(6, HEADS, P), by_token(1, every), ALU.mult).then_inc(S.sem, S.one("kb"))
                v.tensor_tensor(vb_b, bank(7, HEADS, P), by_token(0, every), ALU.mult).then_inc(S.sem, S.one("vb"))

                def level(l):
                    return cst("lev", P * l, P).unsqueeze(1).to_broadcast([P, HEADS, P])

                dve.wait_ge(S.sem, S.at(t, "at"))
                v.tensor_tensor(atm, atb, level(0), ALU.mult).then_inc(S.sem, S.one("atm0"))
                dve.wait_ge(S.sem, S.at(t, "atm0"))
                v.tensor_tensor(xt, ident.unsqueeze(1).to_broadcast([P, HEADS, P]), atm, ALU.subtract).then_inc(S.sem, S.one("xt0"))
                for l in range(1, 6):
                    if l > 1:
                        dve.wait_ge(GDN_PE.sem, GDN_PE.at(t, f"p{l - 1}"))
                    else:
                        dve.wait_ge(S.sem, S.at(t, "xt0"))
                    v.tensor_tensor(atm, atb, level(l), ALU.mult).then_inc(S.sem, S.one(f"atm{l}"))
                    dve.wait_ge(GDN_PE.sem, GDN_PE.at(t, f"y{l}"))
                    v.tensor_tensor(xt, xt, bank(7, HEADS, P), ALU.subtract).then_inc(S.sem, S.one(f"xt{l}"))
                    if l < 5:
                        v.tensor_tensor(xx, xx, bank(2, HEADS, P), ALU.subtract).then_inc(S.sem, S.one(f"x{l}"))
                dve.wait_ge(GDN_PE.sem, GDN_PE.at(t, "uw"))
                v.tensor_copy(u_b, bank(3, HEADS, P)).then_inc(S.sem, S.one("u"))
                dve.wait_ge(S.sem, S.at(t, "u"))
                for c in range(2):
                    r = slice(CHUNK * c, CHUNK * c + CHUNK)
                    dve.wait_ge(GDN_PE.sem, GDN_PE.at(t, f"ws{c}"))
                    v.tensor_tensor(vn[r], u_b[r], bank(4, HEADS, P)[r], ALU.subtract).then_inc(S.sem, S.one(f"vn{c}"))
                    dve.wait_ge(GDN_PE.sem, GDN_PE.at(t, f"up{c}"))
                    for hd in range(HEADS):
                        ins = v.scalar_tensor_tensor(out=st_b[:, hd], in0=st_b[:, hd], scalar=pexp[:, 3 + c, t, hd:hd + 1],
                                                     in1=bank(5)[:, cols(hd)], op0=ALU.mult, op1=ALU.add)
                    ins.then_inc(S.sem, S.one(f"s{c}"))
                    dve.wait_ge(S.sem, S.at(t, f"s{c}"))
                v.tensor_tensor(zg_b, pzb[:, t].rearrange("p (a b) -> p a b", a=HEADS),
                                               gdn_gain.unsqueeze(1).to_broadcast([P, HEADS, P]), ALU.mult).then_inc(S.sem, S.one("zg"))
                dve.wait_ge(S.sem, S.at(t, "zg"))
                head_norm(S, GDN_ACT, t, sm_b, bank(0), zg_b, on_b, "rs")

            def project_out(l):
                for n in range(2):
                    g = mod[:, 2 * D + 512 * n:2 * D + 512 * n + 512]
                    for t in range(TT):
                        j = 8 * l + 4 * n + t
                        dve.wait_ge(outp_pe.sem, outp_pe.at(j, "job"))
                        v.tensor_tensor(res_tmp, bank(t), g, ALU.mult).then_inc(outp_dve.sem, outp_dve.one("tmp"))
                        dve.wait_ge(outp_dve.sem, outp_dve.at(j, "tmp"))
                        xs = x[:, t, 512 * n:512 * n + 512]
                        v.tensor_tensor(xs, xs, res_tmp, ALU.add).then_inc(outp_dve.sem, outp_dve.one("x"))
                        dve.wait_ge(outp_dve.sem, outp_dve.at(j, "x"))

            def project_swa():
                for jj, (n, t) in enumerate(swa_jobs):
                    j = NJ + jj
                    if emptied[j][0] == "v":
                        dve.wait_ge(proj_pe.sem, proj_pe.at(j, "job"))
                        v.tensor_copy(p2[:, t, 512 * n:512 * n + 512], bank(j % 4)).then_inc(proj_dve.sem, proj_dve.one("ev"))

            def rope_angles():
                R = ROPE_DVE


                def turns(out, k, part, base):
                    return v.scalar_tensor_tensor(out=out, in0=k, scalar=-part, in1=base, op0=ALU.mult, op1=ALU.add)

                v.tensor_copy(posf, pos_i[:]).then_inc(R.sem, R.one("pos"))
                dve.wait_ge(R.sem, R.at(0, "pos"))
                v.tensor_tensor(rang, posf.unsqueeze(2).to_broadcast([P, TT, 32]),
                                   cst("inv_freq").unsqueeze(1).to_broadcast([P, TT, 32]), ALU.mult).then_inc(R.sem, R.one("ang"))
                dve.wait_ge(R.sem, R.at(0, "ang"))
                v.tensor_scalar(rk, rang, float(1 / (2 * np.pi)), ROUND, ALU.mult, ALU.add).then_inc(R.sem, R.one("k1"))
                dve.wait_ge(R.sem, R.at(0, "k1"))
                v.tensor_scalar(rk, rk, ROUND, None, ALU.subtract).then_inc(R.sem, R.one("k2"))
                dve.wait_ge(R.sem, R.at(0, "k2"))
                turns(rr, rk, TURN[0], rang).then_inc(R.sem, R.one("r1"))
                dve.wait_ge(R.sem, R.at(0, "r1"))
                turns(rr, rk, TURN[1], rr).then_inc(R.sem, R.one("r2"))
                dve.wait_ge(R.sem, R.at(0, "r2"))
                turns(rr, rk, TURN[2], rr).then_inc(R.sem, R.one("r3"))
                dve.wait_ge(R.sem, R.at(0, "r3"))
                v.tensor_scalar(rr, rr, PI_BELOW, -PI_BELOW, ALU.min, ALU.max).then_inc(R.sem, R.one("r"))
                dve.wait_ge(R.sem, R.at(0, "r"))
                v.tensor_scalar(rc, rr, float(np.pi / 2), None, ALU.add).then_inc(R.sem, R.one("c1"))
                dve.wait_ge(R.sem, R.at(0, "c1"))
                v.tensor_scalar(rk, rc, PI_BELOW, -float(2 * np.pi), ALU.is_gt, ALU.mult).then_inc(R.sem, R.one("c2"))
                dve.wait_ge(R.sem, R.at(0, "c2"))
                v.tensor_tensor(rc, rc, rk, ALU.add).then_inc(R.sem, R.one("c3"))
                dve.wait_ge(R.sem, R.at(0, "c3"))
                v.tensor_scalar(rc, rc, PI_BELOW, -PI_BELOW, ALU.min, ALU.max).then_inc(R.sem, R.one("c"))
                dve.wait_ge(R.sem, R.at(0, "c"))

            def swa():
                Q = QK_DVE
                v.memset(kTz, 0.0).then_inc(init_dve, 1)
                rope_angles()
                for t in range(TT):
                    dve.wait_ge(QK_ACT.sem, QK_ACT.at(0, f"sq{t}"))
                    v.tensor_reduce(qk_s[:, 0, t], sq2.rearrange("p (a b) -> p a b", a=20), AX.X, ALU.add).then_inc(Q.sem, Q.one(f"ss{t}"))
                dve.wait_ge(Q.sem, Q.at(0, "ss3"))
                v.tensor_scalar(qk_s[:, 1], qk_s[:, 0], 1.0 / HD, EPS, ALU.mult, ALU.add).then_inc(Q.sem, Q.one("var"))
                dve.wait_ge(Q.sem, Q.at(0, "var"))
                dve.wait_ge(QK_ACT.sem, QK_ACT.at(0, "exp"))
                newton(Q, 0, qk_s[:, 2], qk_s[:, 1], qk_s[:, 3])
                dve.wait_ge(ROPE_ACT.sem, ROPE_ACT.at(0, "cos"))

                def keys(t):
                    dve.wait_ge(QK_PE.sem, QK_PE.at(0, f"k{t}"))
                    if t == 0:
                        dve.wait_ge(init_dve, 4)
                    for kv in range(NKV):
                        src = bank(2)[64 * (kv % 2):64 * (kv % 2) + 64, cols(kv // 2)]
                        for p_ in range(2):
                            ins = v.tensor_copy(kTz[64 * p_:64 * p_ + 64, kv, p_, CHUNK + P * t:CHUNK + P * t + P], src)
                    ins.then_inc(Q.sem, Q.one(f"k{t}"))

                for t in range(TT):
                    xh = p2[:, t, 0:1280].rearrange("p (a b) -> p a b", a=20)
                    v.tensor_tensor(xh, xh, qk_s[:, 2, t].unsqueeze(2).to_broadcast([P, 20, HD]), ALU.mult).then_inc(Q.sem, Q.one(f"a{t}"))
                    dve.wait_ge(Q.sem, Q.at(0, f"a{t}"))
                    v.tensor_tensor(xh[:, 0:NQ], xh[:, 0:NQ], q_gain.unsqueeze(1).to_broadcast([P, NQ, HD]), ALU.mult)
                    v.tensor_tensor(xh[:, NQ:20], xh[:, NQ:20], k_gain.unsqueeze(1).to_broadcast([P, NKV, HD]), ALU.mult).then_inc(Q.sem, Q.one(f"b{t}"))
                    dve.wait_ge(Q.sem, Q.at(0, f"b{t}"))
                    c_, s_ = (w[:, t].unsqueeze(1).to_broadcast([P, 20, 32]) for w in (cs, sn))
                    x1, x2 = xh[:, :, 0:32], xh[:, :, 32:64]
                    v.tensor_tensor(rope_t[0], x1, c_, ALU.mult)
                    v.tensor_tensor(rope_t[1], x2, s_, ALU.mult)
                    v.tensor_tensor(rope_t[2], x2, c_, ALU.mult)
                    v.tensor_tensor(rope_t[3], x1, s_, ALU.mult).then_inc(Q.sem, Q.one(f"c{t}"))
                    dve.wait_ge(Q.sem, Q.at(0, f"c{t}"))
                    v.tensor_tensor(x1, rope_t[0], rope_t[1], ALU.subtract)
                    v.tensor_tensor(x2, rope_t[2], rope_t[3], ALU.add).then_inc(Q.sem, Q.one(f"rope{t}"))
                    dve.wait_ge(Q.sem, Q.at(0, f"rope{t}"))
                    keys(t)
                v.memset(sm[:, :, 0:64], 0.0).then_inc(Q.sem, Q.one("q3"))
                dve.wait_ge(Q.sem, Q.at(0, "q3"))
                W = SWA_DVE
                for t in range(TT):
                    if t:
                        dve.wait_ge(SWA_PE.sem, SWA_PE.at(t - 1, "t7"))
                    bias = cst("swa_bias", 192 if t else 0, 192).unsqueeze(1).to_broadcast([P, 2, 192])
                    for n in range(8):
                        dve.wait_ge(SWA_PE.sem, SWA_PE.at(t, f"s{n}"))
                        v.scalar_tensor_tensor(out=sm[:, 2 * n:2 * n + 2, 64:256], in0=bank(n % 4)[:, 0:384].rearrange("p (a b) -> p a b", a=2),
                                                      scalar=HD ** -0.5, in1=bias, op0=ALU.mult, op1=ALU.add).then_inc(W.sem, W.one(f"s{n}"))
                    dve.wait_ge(W.sem, W.at(t, "s7"))
                    pr = sm[:, :, 64:256]
                    v.tensor_reduce(sw_s[:, 0], pr, AX.X, ALU.max).then_inc(W.sem, W.one("max"))
                    dve.wait_ge(W.sem, W.at(t, "max"))
                    v.tensor_tensor(sw_s[:, 1], sw_s[:, 0], sink, ALU.max).then_inc(W.sem, W.one("m"))
                    dve.wait_ge(W.sem, W.at(t, "m"))
                    v.tensor_scalar(sw_s[:, 2], sw_s[:, 1], -1.0, None, ALU.mult).then_inc(W.sem, W.one("nm"))
                    v.tensor_tensor(sw_s[:, 3], sink, sw_s[:, 1], ALU.subtract).then_inc(W.sem, W.one("es"))
                    dve.wait_ge(SWA_ACT.sem, SWA_ACT.at(t, "exp"))
                    v.tensor_tensor(sw_s[:, 5], sw_s[:, 5], sw_s[:, 4], ALU.add).then_inc(W.sem, W.one("den"))
                    dve.wait_ge(W.sem, W.at(t, "den"))
                    v.reciprocal(sw_s[:, 5], sw_s[:, 5]).then_inc(W.sem, W.one("rec"))
                    dve.wait_ge(W.sem, W.at(t, "rec"))
                    v.tensor_tensor(pr, pr, sw_s[:, 5].unsqueeze(2).to_broadcast([P, NQ, 192]), ALU.mult).then_inc(W.sem, W.one("p"))

            def router(l):
                R = RT_DVE


                def e4(w):
                    return w.rearrange("p t (g e) -> p t g e", g=NGRP)

                def over(w, n):
                    return w.unsqueeze(2).to_broadcast([P, TT, n])

                def first_of_max(src, n, names, mask):
                    mx, eqn, wn, mwn, mn = names
                    tmp = r_b[:, :, 0:n]
                    v.tensor_reduce(r_t, src, AX.X, ALU.max).then_inc(R.sem, R.one(mx))
                    dve.wait_ge(R.sem, R.at(l, mx))
                    v.tensor_tensor(tmp, src, over(r_t, n), ALU.is_equal).then_inc(R.sem, R.one(eqn))
                    dve.wait_ge(R.sem, R.at(l, eqn))
                    v.tensor_tensor(tmp, tmp, cst("desc16", 0, n).unsqueeze(1).to_broadcast([P, TT, n]), ALU.mult).then_inc(R.sem, R.one(wn))
                    dve.wait_ge(R.sem, R.at(l, wn))
                    v.tensor_reduce(r_u, tmp, AX.X, ALU.max).then_inc(R.sem, R.one(mwn))
                    dve.wait_ge(R.sem, R.at(l, mwn))
                    v.tensor_tensor(mask, tmp, over(r_u, n), ALU.is_equal).then_inc(R.sem, R.one(mn))
                    dve.wait_ge(R.sem, R.at(l, mn))

                dve.wait_ge(RT_ACT.sem, RT_ACT.at(l, "exp"))
                v.tensor_scalar(r_e, r_e, 1.0, None, ALU.add).then_inc(R.sem, R.one("e1"))
                dve.wait_ge(R.sem, R.at(l, "e1"))
                v.reciprocal(r_sc, r_e).then_inc(R.sem, R.one("sc"))
                dve.wait_ge(R.sem, R.at(l, "sc"))
                v.tensor_tensor(r_sel, r_sc, router_b.unsqueeze(1).to_broadcast([P, TT, NE]), ALU.add).then_inc(R.sem, R.one("sel"))
                dve.wait_ge(R.sem, R.at(l, "sel"))
                s4 = e4(r_sel)
                g0, g1, g2, g3, g4, g5, gm, go_ = r_g
                v.tensor_tensor(g0, s4[:, :, :, 0], s4[:, :, :, 1], ALU.max)
                v.tensor_tensor(g1, s4[:, :, :, 0], s4[:, :, :, 1], ALU.min)
                v.tensor_tensor(g2, s4[:, :, :, 2], s4[:, :, :, 3], ALU.max)
                v.tensor_tensor(g3, s4[:, :, :, 2], s4[:, :, :, 3], ALU.min).then_inc(R.sem, R.one("pairs"))
                dve.wait_ge(R.sem, R.at(l, "pairs"))
                v.tensor_tensor(g4, g0, g2, ALU.max).then_inc(R.sem, R.one("top"))
                dve.wait_ge(R.sem, R.at(l, "top"))
                v.tensor_tensor(g5, g0, g2, ALU.min)
                v.tensor_tensor(gm, g1, g3, ALU.max).then_inc(R.sem, R.one("low"))
                dve.wait_ge(R.sem, R.at(l, "low"))
                v.tensor_tensor(g5, g5, gm, ALU.max).then_inc(R.sem, R.one("second"))
                dve.wait_ge(R.sem, R.at(l, "second"))
                v.tensor_tensor(g4, g4, g5, ALU.add).then_inc(R.sem, R.one("gs"))
                dve.wait_ge(R.sem, R.at(l, "gs"))
                first_of_max(g4, NGRP, ("gmax", "geq", "gw", "gmw", "gmask"), gm)
                v.tensor_scalar(go_, gm, -1.0, -NEG, ALU.add, ALU.mult).then_inc(R.sem, R.one("goff"))
                dve.wait_ge(R.sem, R.at(l, "goff"))
                v.tensor_tensor(e4(r_a), s4, go_.unsqueeze(3).to_broadcast([P, TT, NGRP, 4]), ALU.add).then_inc(R.sem, R.one("selm"))
                dve.wait_ge(R.sem, R.at(l, "selm"))
                first_of_max(r_a, NE, ("max1", "eq1", "w1", "mw1", "mk1"), mk1)
                v.scalar_tensor_tensor(out=r_a, in0=mk1, scalar=3 * NEG, in1=r_a, op0=ALU.mult, op1=ALU.add).then_inc(R.sem, R.one("selm2"))
                dve.wait_ge(R.sem, R.at(l, "selm2"))
                first_of_max(r_a, NE, ("max2", "eq2", "w2", "mw2", "mk2"), mk)
                v.tensor_tensor(mk, mk, mk1, ALU.add).then_inc(R.sem, R.one("mk"))
                dve.wait_ge(R.sem, R.at(l, "mk"))
                v.tensor_tensor(r_a, r_sc, mk, ALU.mult).then_inc(R.sem, R.one("wr"))
                dve.wait_ge(R.sem, R.at(l, "wr"))
                v.tensor_reduce(r_t, r_a, AX.X, ALU.add).then_inc(R.sem, R.one("wsum"))
                dve.wait_ge(R.sem, R.at(l, "wsum"))
                v.reciprocal(r_u, r_t).then_inc(R.sem, R.one("wrec"))
                dve.wait_ge(R.sem, R.at(l, "wrec"))
                v.tensor_tensor(wgt, r_a, over(r_u, NE), ALU.mult).then_inc(R.sem, R.one("wgt"))
                dve.wait_ge(R.sem, R.at(l, "wgt"))
                v.tensor_scalar(r_a, mk, -1e4, 1e4, ALU.mult, ALU.add).then_inc(R.sem, R.one("off"))
                dve.wait_ge(R.sem, R.at(l, "off"))
                dve.wait_ge(RT_PE.sem, RT_PE.at(l, "pos"))
                v.tensor_tensor(posm, bank(1, TT, NE), r_a, ALU.add).then_inc(R.sem, R.one("posm"))
                dve.wait_ge(R.sem, R.at(l, "posm"))
                for s_ in range(3):
                    ins = v.tensor_scalar(fl[:, s_], bank(1)[:, 64:64 + NE], float(SLOTS * (s_ + 1)), None, ALU.is_gt)
                ins.then_inc(R.sem, R.one("fl"))
                dve.wait_ge(R.sem, R.at(l, "fl"))
                flf, keyf = (w.rearrange("p s e -> p (s e)") for w in (fl, key))
                v.tensor_tensor(keyf, flf, cst("desc48"), ALU.mult).then_inc(R.sem, R.one("key"))
                dve.wait_ge(R.sem, R.at(l, "key"))
                v.max(top8, keyf).then_inc(R.sem, R.one("top8"))
                dve.wait_ge(R.sem, R.at(l, "top8"))
                v.tensor_reduce(nov, flf, AX.X, ALU.add).then_inc(R.sem, R.one("nov"))
                dve.wait_ge(R.sem, R.at(l, "nov"))
                v.tensor_scalar(ent, top8, -1.0, DESC_TOP, ALU.mult, ALU.add).then_inc(R.sem, R.one("ent"))
                dve.wait_ge(R.sem, R.at(l, "ent"))
                v.tensor_copy(ovl_i[:, 16:24], ent).then_inc(R.sem, R.one("enti"))
                dve.wait_ge(R.sem, R.at(l, "enti"))
                v.tensor_scalar(ovl_i[:, 24:32], ovl_i[:, 16:24], 4, None, ALU.logical_shift_right).then_inc(R.sem, R.one("sh"))
                dve.wait_ge(R.sem, R.at(l, "sh"))
                v.tensor_scalar(ovl_i[:, 0:8], ovl_i[:, 16:24], 15, None, ALU.bitwise_and).then_inc(R.sem, R.one("ei"))
                dve.wait_ge(R.sem, R.at(l, "ei"))
                v.tensor_copy(basef, ovl_i[:, 24:32]).then_inc(R.sem, R.one("base"))
                dve.wait_ge(R.sem, R.at(l, "base"))
                v.tensor_copy(ovl_i[:, 8:9], nov).then_inc(R.sem, R.one("ovl"))
                dve.wait_ge(R.sem, R.at(l, "ovl"))

            def expert_block(st, i, E, columns):
                S, SA, SV = st
                dve.wait_ge(S.sem, S.at(i - 1, "c7"))
                columns()
                for e in range(E):
                    for t in range(TT):
                        ins = v.tensor_scalar(pd[:, t, cols(e)], cst("iota"), pcol[:, t, e:e + 1], None, ALU.is_equal)
                ins.then_inc(SV.sem, SV.one("disp"))
                for k in range(1, KD, 2):
                    dve.wait_ge(S.sem, S.at(i, f"hg{k}"))
                    v.tensor_copy(hgT[:, k, 0:E * P], bank(k % 4)[:, 0:E * P]).then_inc(SV.sem, SV.one(f"hg{k}"))
                for e in range(1, E, 2):
                    dve.wait_ge(S.sem, S.at(i, f"pT{e}"))
                    v.tensor_copy(pdT[:, e], bank(6 + e % 2)).then_inc(SV.sem, SV.one(f"pT{e}"))
                dve.wait_ge(S.sem, S.at(i, "ws"))
                v.tensor_copy(ws[:, 0:E], bank(5)[:, 0:E]).then_inc(SV.sem, SV.one("ws"))
                dve.wait_ge(SV.sem, SV.at(i, "ws"))
                for e in range(E):
                    dve.wait_ge(S.sem, S.at(i, f"u{e}"))
                    dve.wait_ge(SA.sem, SA.at(i, f"sg{e}"))
                    if e:
                        dve.wait_ge(S.sem, S.at(i, f"hT{e - 1}"))
                    v.tensor_tensor(he, bank(5), sg, ALU.mult).then_inc(SV.sem, SV.one(f"he{e}"))
                    for half, b in ((0, 7), (1, 3)):
                        dve.wait_ge(S.sem, S.at(i, f"y{half}{e}"))
                        g2 = mod[:, 5 * D + 512 * half:5 * D + 512 * half + 512]
                        v.scalar_tensor_tensor(out=ys[:, e, 512 * half:512 * half + 512], in0=bank(b), scalar=ws[:, e:e + 1],
                                                       in1=g2, op0=ALU.mult, op1=ALU.mult).then_inc(SV.sem, SV.one(f"y{half}{e}"))
                for j in range(8):
                    t, half = j // 2, j % 2
                    dve.wait_ge(S.sem, S.at(i, f"c{j}"))
                    xs = x[:, t, 512 * half:512 * half + 512]
                    v.tensor_tensor(xs, xs, bank(j % 4), ALU.add).then_inc(SV.sem, SV.one(f"x{j}"))

            def experts(l):
                router(l)
                st, so = moe_steps[l], over_steps[l]
                dve.sem_inc(st[2].sem, st[2].n)
                dve.sem_inc(so[2].sem, so[2].n)
                with dve.Fori(0, NE // EG) as i:
                    def columns():
                        dve.wait_ge(st[2].sem, st[2].at(i - 1, "x7"))
                        v.tensor_copy(pcol, posm[:, :, bass.ds(EG * i, EG)])
                        v.tensor_copy(wcol, wgt[:, :, bass.ds(EG * i, EG)]).then_inc(st[2].sem, st[2].one("pw"))
                        dve.wait_ge(st[2].sem, st[2].at(i, "pw"))

                    expert_block(st, i, EG, columns)
                dve.wait_ge(st[2].sem, st[2].at(NE // EG - 1, "x7"))
                n_over = dve.value_load(ovl_i[0:1, 8:9], min_val=0, max_val=MAXOVER)
                with dve.Fori(0, MAXOVER) as j:
                    e = dve.value_load(ovl_i[0:1, bass.ds(j, 1)], min_val=0, max_val=NE - 1)
                    with dve.If(n_over > j):
                        def columns():
                            dve.wait_ge(so[2].sem, so[2].at(j - 1, "x7"))
                            v.tensor_copy(wcol[:, :, 0:1], wgt[:, :, bass.ds(e, 1)])
                            v.tensor_scalar(nov, basef[:, bass.ds(j, 1)], float(SLOTS), float(SLOTS), ALU.mult, ALU.add).then_inc(over_col[l], 1)
                            dve.wait_ge(over_col[l], j + 1)
                            v.tensor_scalar(pcol[:, :, 0:1], posm[:, :, bass.ds(e, 1)], nov[:, 0:1], None, ALU.subtract).then_inc(so[2].sem, so[2].one("pw"))
                            dve.wait_ge(so[2].sem, so[2].at(j, "pw"))

                        expert_block(so, j, 1, columns)

            dve.wait_ge(params_in, 16 * NPARAMS)
            ada(0)
            norm(0)
            project_ab()
            v.drain().then_inc(phase_done, 1)
            dve.wait_ge(phase_done, 3 * 1)
            v.memset(gaT[0:32, :], 1.0)
            for z_ in (kz, ku, at_g):
                v.memset(z_, 0.0)
            v.memset(st_g, 0.0).then_inc(init_dve, 1)
            dve.wait_ge(init_dve, 2)
            for t in range(TT):
                gla(t)
            v.drain().then_inc(phase_done, 1)
            dve.wait_ge(phase_done, 3 * 2)
            v.memset(ku_b, 0.0)
            v.memset(vn, 0.0)
            v.memset(st_b, 0.0).then_inc(init_dve, 1)
            dve.wait_ge(init_dve, 3)
            gdn_pre()
            for t in range(TT):
                gdn(t)
            v.drain().then_inc(phase_done, 1)
            dve.wait_ge(phase_done, 3 * 3)
            project_out(0)
            v.drain().then_inc(phase_done, 1)
            dve.wait_ge(phase_done, 3 * 4)
            norm(1)
            experts(0)
            v.drain().then_inc(phase_done, 1)
            dve.wait_ge(phase_done, 3 * 5)
            ada(1)
            norm(2)
            project_swa()
            v.drain().then_inc(phase_done, 1)
            dve.wait_ge(phase_done, 3 * 6)
            swa()
            v.drain().then_inc(phase_done, 1)
            dve.wait_ge(phase_done, 3 * 7)
            project_out(1)
            v.drain().then_inc(phase_done, 1)
            dve.wait_ge(phase_done, 3 * 8)
            norm(3)
            experts(1)
            v.drain().then_inc(phase_done, 1)


def laid_out(inputs):
    r = {k: np.ascontiguousarray(v) for k, v in inputs.items()}
    r["c_cols"] = np.ascontiguousarray(r.pop("c").reshape(KD, P).T)
    r["conv_cols"] = np.ascontiguousarray(r.pop("gdn_conv").reshape(4, 12, P).transpose(2, 1, 0).reshape(P, 48))
    r["pos_cols"] = np.ascontiguousarray(r.pop("positions").reshape(TT, P).T)
    r["consts"] = constants()
    return r


def kernel(**inputs):
    import concourse.bacc as bacc
    from concourse.bass_utils import run_bass_kernel_spmd

    nc = bacc.Bacc("TRN2", target_bir_lowering=False, num_devices=1)
    arrays, a = {}, {}
    for name, v in laid_out(inputs).items():
        arrays[f"in_{name}_dram"] = v
        a[name] = nc.dram_tensor(f"in_{name}_dram", v.shape, mybir.dt.from_np(v.dtype), kind="ExternalInput").ap()
    out = nc.dram_tensor("out_0_dram", (1, SEQ, D), F32, kind="ExternalOutput").ap()
    build_block(nc, a, out)
    return run_bass_kernel_spmd(nc, [arrays], core_ids=[0]).results[0]["out_0_dram"]
```

```python
from contextlib import ExitStack

import concourse.bass as bass
import numpy as np
from concourse import mybir

P = 128
SEQ, D = 512, 1024
TT = SEQ // P
KD = D // P
CHUNK = 64
EPS = 1e-6
HEADS = 4
GLA_DK, DV = 64, 128
RANK = 16
QW, NQ, NKV, HD = 1024, 16, 4, 64
NE, NGRP, FF = 16, 4, 512
EG = 2
NPAIRS = NE // EG // 2
RING = 4
SLOTS = 128
HIGHS = 3
MAXOVER = (2 * SEQ - 1) // SLOTS
NEG = -1e30
NWORK = 18700
NPAR = 1088

F32 = mybir.dt.float32
I32 = mybir.dt.int32
U32 = mybir.dt.uint32
F32R = mybir.dt.float32r
ALU = mybir.AluOpType
ACT = mybir.ActivationFunctionType
AX = mybir.AxisListType

C_GA = 2 * HEADS * GLA_DK + HEADS * DV
C_ZA = C_GA + RANK
C_QKVB = C_ZA + HEADS * DV
C_AB = C_QKVB + 3 * HEADS * DV
C_ZB = C_AB + 2 * HEADS

DESC_TOP = 1000.0
ROUND = 1.5 * 2.0 ** 23
TURN = (6.28125, 0.0019340515136718750, float(2 * np.pi - 6.28125 - 0.0019340515136718750))
PI_BELOW = 3.1415925

CONST_WIDTHS = [
    ("tri", P), ("later", P), ("strict_bias", P), ("incl_bias", P), ("lev", 6 * P), ("in_chunk", 2 * P),
    ("ident", P), ("ones", P), ("before", P), ("iota", P), ("swa_bias", 2 * 192),
    ("inv_freq", 32), ("desc16", 16), ("desc48", 48),
]
CONST_AT, _n = {}, 0
for _name, _w in CONST_WIDTHS:
    CONST_AT[_name] = (_n, _w)
    _n += _w
NCONST = _n
NEARLY = CONST_AT["ident"][0]


def constants():
    j, i = np.arange(P)[:, None], np.arange(P)[None, :]
    same = (j // CHUNK) == (i // CHUNK)
    c = {
        "ident": j == i, "tri": same & (j <= i), "later": same & (j > i),
        "strict_bias": np.where(same & (j < i), 0.0, NEG), "incl_bias": np.where(same & (j <= i), 0.0, NEG),
        "ones": np.ones((P, P)), "before": j < i, "iota": np.broadcast_to(i, (P, P)),
        "inv_freq": np.broadcast_to((10000.0 ** (-np.arange(32) / 32))[None, :], (P, 32)),
        "desc16": np.broadcast_to(16.0 - np.arange(16)[None, :], (P, 16)),
        "desc48": np.broadcast_to(DESC_TOP - np.arange(48)[None, :], (P, 48)),
    }
    lev = []
    for n in range(6):
        s = 1 << n
        lev.append(((i // (2 * s)) == (j // (2 * s))) & ((i // s) % 2 == 1) & ((j // s) % 2 == 0))
    c["lev"] = np.concatenate(lev, axis=1)
    c["in_chunk"] = np.concatenate([np.broadcast_to(j // CHUNK == n, (P, P)) for n in range(2)], axis=1)
    q, k = np.arange(P)[:, None], np.arange(192)[None, :]
    seen = (k // CHUNK == q // CHUNK) | (k // CHUNK == q // CHUNK + 1)
    c["swa_bias"] = np.concatenate([np.where(seen & (k >= CHUNK), 0.0, NEG), np.where(seen, 0.0, NEG)], axis=1)
    out = np.zeros((P, NCONST), np.float32)
    for name, (a, w) in CONST_AT.items():
        out[:, a:a + w] = c[name].astype(np.float32)
    return out


class Steps:

    def __init__(self, sem, names, credit=0):
        self.sem, self.names, self.n, self.credit, self.k = sem, list(names), len(names), credit, 0

    def at(self, t, name):
        return (t + self.credit) * self.n + self.names.index(name) + 1

    def one(self, name):
        assert self.names[self.k % self.n] == name, (self.names[self.k % self.n], name)
        self.k += 1
        return 1


def build_block(nc, a, out):
    ctx = ExitStack()
    with ctx:
        def sem(name):
            return ctx.enter_context(nc.semaphore(name))

        def sb(name, shape, dt=F32):
            return ctx.enter_context(nc.sbuf_tensor(name, shape, dt))

        AREAS = [("ring", [P, RING, KD, 512]), ("x", [P, TT, D]), ("hT", [P, KD, SEQ]), ("early_mod", [P, NEARLY + 6 * D]),
                 ("const", [P, NCONST - NEARLY]), ("par", [P, NPAR]), ("work", [P, NWORK])]
        start = (nc.sbuf_base + 63) // 64 * 64
        sb("slab", [P, sum(int(np.prod(shape[1:])) for _, shape in AREAS) + 16])
        area, area_r = {}, {}
        for name, shape in AREAS:
            area[name] = nc.alloc_sbuf_tensor_at(name, shape, F32, offset=start)
            area_r[name] = nc.alloc_sbuf_tensor_at(name + "_r", shape, F32R, offset=start)
            start += 4 * int(np.prod(shape[1:]))
        ring, x, hT, early_mod, const, par, work = (area[name] for name, _ in AREAS)
        mod = early_mod[:, NEARLY:NEARLY + 6 * D]
        ovl_i = sb("ovl_i", [P, 32], I32)
        pos_i = sb("pos_i", [P, TT], I32)
        ps = ctx.enter_context(nc.psum_tensor("ps", [P, 8, 512], F32))

        def cst(name, lo=0, n=None):
            o, w = CONST_AT[name]
            n = w if n is None else n
            if o < NEARLY:
                return early_mod[:, o + lo:o + lo + n]
            return const[:, o - NEARLY + lo:o - NEARLY + lo + n]

        top = {"par": 0, "work": 0}

        def carve(which, *shape, rounded=False):
            n = int(np.prod(shape))
            t = (area_r if rounded else area)[which]
            o = top[which]
            top[which] = o + n
            assert top[which] <= (NPAR if which == "par" else NWORK), (which, top[which])
            v = t[:, o:o + n]
            if len(shape) == 2:
                v = v.rearrange("p (a b) -> p a b", a=shape[0])
            elif len(shape) == 3:
                v = v.rearrange("p (a b c) -> p a b c", a=shape[0], b=shape[1])
            elif len(shape) == 4:
                v = v.rearrange("p (a b c d) -> p a b c d", a=shape[0], b=shape[1], c=shape[2])
            return v

        def bank(b, *shape):
            v = ps[:, b, :]
            if len(shape) == 2:
                v = v[:, 0:shape[0] * shape[1]].rearrange("p (a b) -> p a b", a=shape[0])
            elif len(shape) == 3:
                v = v[:, 0:shape[0] * shape[1] * shape[2]].rearrange("p (a b c) -> p a b c", a=shape[0], b=shape[1])
            return v

        ident = cst("ident")

        cond = carve("par", KD)
        w2aug = carve("par", HEADS * GLA_DK)
        conv_w = carve("par", 12, 4)
        gla_gain = carve("par", DV)
        gdn_gain = carve("par", DV)
        q_gain = carve("par", HD)
        k_gain = carve("par", HD)
        sink = carve("par", NQ)
        router_w = carve("par", KD, NE)
        router_b = carve("par", NE)
        a_log = carve("par", HEADS)
        dt_bias = carve("par", HEADS)
        ident_r = carve("par", P, rounded=True)
        ss = carve("par", TT)
        var = carve("par", TT)
        rstd = carve("par", TT)
        nt1 = carve("par", TT)
        nt2 = carve("par", TT)

        const_in = sem("const_in")
        early_in = sem("early_in")
        cond_in = sem("cond_in")
        params_in = sem("params_in")
        x_in = sem("x_in")
        x_again = sem("x_again")
        small_in = sem("small_in")
        gains_in = [sem(f"gains_in{l}") for l in range(2)]
        bias_in = [sem(f"bias_in{l}") for l in range(2)]
        chunk_in = [sem(f"chunk_in{s}") for s in range(RING)]
        chunk_used = sem("chunk_used")
        phase_done = sem("phase_done")
        out_written = sem("out_written")
        cond_dve = Steps(sem("cond_dve"), ["e1", "rec", "silu"])
        rep_dve = Steps(sem("rep_dve"), ["high", "rep"])
        Q_ACT = Steps(sem("quarter_act"), ["high"])
        Q_DVE = Steps(sem("quarter_dve"), ["low"])
        Q_PE = Steps(sem("quarter_pe"), ["used"])
        cond_act = Steps(sem("cond_act"), ["exp"])
        ada_pe = Steps(sem("ada_pe"), ["mod"])
        ada_dve = Steps(sem("ada_dve"), ["mod"])
        amod_dve = Steps(sem("amod_dve"), ["a1", "a2"])
        norm_pool = Steps(sem("norm_pool"), ["h1", "h3"])
        norm_act = Steps(sem("norm_act"), ["ss0", "ss1", "ss2", "ss3", "ln", "exp", "ev0", "ev1", "ev2", "ev3"])
        norm_dve = Steps(sem("norm_dve"), ["var", "n1", "n2", "n3", "rstd", "hx0", "h0", "hx1", "hx2", "h2",
                                           "hx3", "ev0", "ev1", "ev2", "ev3"])
        TN_ACT = Steps(sem("tile_norm_act"), ["ss", "ln", "exp"])
        TN_ACT_EV = Steps(sem("tile_norm_ev_act"), ["ev"])
        TN_DVE = Steps(sem("tile_norm_dve"), ["var", "n1", "n2", "n3", "rstd", "hx", "h"])
        TN_DVE_EV = Steps(sem("tile_norm_ev_dve"), ["ev"])
        TN_PE = Steps(sem("tile_norm_pe"), ["lo", "hi"])
        norm_pe = Steps(sem("norm_pe"), [f"{n}{t}" for t in range(TT) for n in ("lo", "hi")])
        proj_pe = Steps(sem("proj_pe"), ["job"])
        proj_act = Steps(sem("proj_act"), ["ev"])
        proj_dve = Steps(sem("proj_dve"), ["ev"])
        conv_dve = Steps(sem("conv_dve"), ["t0", "t1", "t2", "t3"])
        conv_act = Steps(sem("conv_act"), ["silu", "sq"])
        conv_pe = Steps(sem("conv_pe"), ["ss"])
        init_dve = sem("init_dve")

        GATE_PE = Steps(sem("gla_gate_pe"), ["gaT", "z", "cums"])
        GATE_ACT = Steps(sem("gla_gate_act"), ["abs", "e", "l", "eb", "enb", "ekb"])
        GATE_DVE = Steps(sem("gla_gate_dve"), ["gaT", "g", "zg"])
        GLP_PE = Steps(sem("gla_prep_pe"), ["qkT", "A", "u0", "u1"])
        GLP_DVE = Steps(sem("gla_prep_dve"), ["qd", "kz", "ku"])
        GLA_PE = Steps(sem("gla_pe"), ["o", "int0", "int1"])
        GLA_DVE = Steps(sem("gla_dve"), ["A", "s0", "s1"])
        GLN_PE = Steps(sem("gla_norm_pe"), ["oT"])
        GLN_ACT = Steps(sem("gla_norm_act"), ["ss0", "ss1", "ss2", "ss3", "ln", "exp", "oT0", "oT1", "oT2", "oT3"])
        GLN_DVE = Steps(sem("gla_norm_dve"), ["var", "n1", "n2", "n3", "rstd", "on0", "on1", "on2", "on3"])
        PRE_DVE = Steps(sem("gdn_pre_dve"), ["u", "au", "mx", "g", "lnb", "lk", "lq", "lbk", "pre", "colj"])
        PRE_ACT = Steps(sem("gdn_pre_act"), ["e", "l", "expa", "lnss", "exp"])
        PRE_PE = Steps(sem("gdn_pre_pe"), ["cum"])
        tiles, levels = range(TT), range(1, 6)
        MAT_PE = Steps(sem("gdn_mat_pe"), [f"{n}{t}" for t in tiles for n in ("rows", "kk")] + [f"x0{t}" for t in tiles])
        MAT_ACT = Steps(sem("gdn_mat_act"), [f"{n}{t}" for n in ("exp", "x0") for t in tiles])
        MAT_DVE = Steps(sem("gdn_mat_dve"), [f"{n}{t}" for n in ("rep", "d", "at", "level0", "xt0", "level1") for t in tiles])
        INV_PE = Steps(sem("gdn_inv_pe"), [f"{n}{l}{t}" for l in levels for n in ("p", "y") for t in tiles])
        INV_ACT = Steps(sem("gdn_inv_act"), [f"p{l}{t}" for l in levels for t in tiles])
        INV_DVE = Steps(sem("gdn_inv_dve"), [f"{n}{l}{t}" for l in levels for t in tiles
                                             for n in (("xt", "x", "level") if l < 5 else ("xt", ))])
        GDP_PE = Steps(sem("gdn_prep_pe"), ["rows", "kq", "kv", "uw"])
        GDP_ACT = Steps(sem("gdn_prep_act"), ["exp", "eq", "wT"])
        GDP_DVE = Steps(sem("gdn_prep_dve"), ["rep", "d", "qk", "qd", "ku", "kb", "vb", "u"])
        GDN_DVE = Steps(sem("gdn_dve"), ["vn0", "s0", "vn1", "s1", "zg", "var", "n1", "n2", "n3", "rstd", "on"])
        GDN_ACT = Steps(sem("gdn_act"), ["ss", "ln", "rs"])
        GDO_ACT = Steps(sem("gdn_out_act"), ["oT"])
        GDN_PE = Steps(sem("gdn_pe"), ["ws0", "o0", "up0", "ws1", "o1", "up1"])
        GDO_PE = Steps(sem("gdn_out_pe"), ["oT"])
        outp_pe = Steps(sem("outp_pe"), ["job"])
        outp_dve = Steps(sem("outp_dve"), ["tmp", "x"])

        ROPE_DVE = Steps(sem("rope_dve"), ["pos", "ang", "k1", "k2", "r1", "r2", "r3", "r", "c1", "c2", "c3", "c"])
        ROPE_ACT = Steps(sem("rope_act"), ["sin", "cos"])
        QK_ACT = Steps(sem("qk_act"), ["sq", "ln", "exp"])
        QT_ACT = Steps(sem("qt_act"), ["q"])
        QK_DVE = Steps(sem("qk_dve"), ["ss", "var", "n1", "n2", "n3", "rstd", "a", "b", "c", "rope"])
        QT_DVE = Steps(sem("kt_dve"), ["k"])
        QK_POOL = Steps(sem("qk_pool"), ["c"])
        QK_PE = Steps(sem("qk_pe"), ["q", "k"])
        SCO_PE = Steps(sem("scores_pe"), [f"s{n}" for n in range(8)])
        SCO_DVE = Steps(sem("scores_dve"), [f"s{n}" for n in range(8)] + ["max", "m", "nm", "es"])
        SCO_ACT = Steps(sem("scores_act"), ["es", "exp"])
        VAL_PE = Steps(sem("values_pe"), ["t0"] + [x_ for n in range(1, 8) for x_ in (f"t{n}", f"v{n - 1}")] + ["v7", "oT"])
        VAL_DVE = Steps(sem("values_dve"), ["den", "rec", "o"])
        VAL_ACT = Steps(sem("values_act"), [f"t{n}" for n in range(8)] + ["oT"])

        RT_DVE = Steps(sem("router_dve"), ["e1", "sc", "sel", "pairs", "top", "low", "second", "gs", "gmax", "geq", "gw",
                                           "gmw", "gmask", "goff", "selm", "max1", "eq1", "w1", "mw1", "mk1", "selm2",
                                           "max2", "eq2", "w2", "mw2", "mk2", "mk", "wr", "wsum", "wrec", "wgt", "off",
                                           "posm", "fl", "key", "top8", "nov", "ent", "enti", "sh", "ei", "base", "ovl"])
        RT_PE = Steps(sem("router_pe"), ["logits", "pos"])
        RT_ACT = Steps(sem("router_act"), ["exp"])

        def use_order(E):
            return [(e, w) for e in range(E) for w in range(2)] + [(e, 2) for e in range(E)]

        def expert_steps(tag, E):
            def halves(n, ms):
                return [f"{n}{m}{h_}" for m in ms for h_ in "ab"]

            if E == 1:
                pe_ = halves("w", (0, )) + ["ws"] + halves("w", (1, )) + ["hT0", "pT0"] + halves("w", (2, ))
                act_ = halves("hi", (1, )) + ["hi2a", "sg0", "hi2b"] + ["hT0", "y0"]
                dve_ = halves("lo", (0, 1)) + ["ws", "he0"] + halves("lo", (2, )) + ["hT0", "pT0", "y0"]
            else:
                pe_ = (halves("w", (0, )) + ["ws"] + halves("w", (1, 2)) + ["w3a", "hT0", "w3b", "w4a", "hT1", "w4b", "pT0", "pT1"]
                       + halves("w", (5, )))
                act_ = (halves("hi", (1, )) + ["hi2a", "sg0", "hi2b"] + halves("hi", (3, ))
                        + ["sg1", "hi4a", "hT0", "hi4b", "hi5a", "hT1", "hi5b", "y0", "y1"])
                dve_ = (halves("lo", (0, 1, 2)) + ["ws", "he0"] + halves("lo", (3, )) + ["lo4a", "hT0", "lo4b", "he1", "lo5a", "hT1",
                        "lo5b", "y0", "pT0", "pT1", "pw", "disp", "y1"])
            hg = [f"hg{k}" for k in range(KD)]
            return (
                Steps(sem(f"{tag}_pe"), hg + pe_ + [f"c{j}" for j in range(8)], credit=1),
                Steps(sem(f"{tag}_act"), halves("hi", (0, )) + hg + act_, credit=1),
                Steps(sem(f"{tag}_dve"), (["pw", "disp"] if E == 1 else []) + dve_ + [f"m{j}" for j in range(8)], credit=1),
                Steps(sem(f"{tag}_pool"), [f"x{j}" for j in range(8)], credit=1),
            )

        moe_steps = [expert_steps(f"moe{l}", EG) for l in range(2)]
        over_steps = [expert_steps(f"over{l}", 1) for l in range(2)]
        split_act = Steps(sem("split_act"), [f"hi{t}" for t in range(TT)])
        split_dve = Steps(sem("split_dve"), [f"lo{t}" for t in range(TT)])
        first_disp = [sem(f"first_disp{l}") for l in range(2)]
        x_added = sem("x_added")
        experts_through = sem("experts_through")
        over_in = [sem(f"over_in{l}") for l in range(2)]
        over_col = [sem(f"over_col{l}") for l in range(2)]

        n_chunks = {"ada": 12, "ab": 8, "abo": 2, "moe": 48, "swa": 3, "swo": 2}
        order = [("ada", 0), ("ab", 0), ("abo", 0), ("moe", 0), ("ada", 1), ("swa", 1), ("swo", 1), ("moe", 1)]
        first, n = {}, 0
        for o in order:
            first[o] = n
            n += n_chunks[o[0]]

        def loaded(c):
            return 16 * (c // RING + 1)

        def slot(c):
            return ring[:, c % RING]

        def expert_view(v, w):
            return v if w < 2 else v.rearrange("p (k a) f -> p k (a f)", a=2)

        def half_view(v, w):
            return v.rearrange("p (k f) -> p k f", k=4 if w < 2 else 2)

        def half_of(c, half, rounded=False):
            return (area_r if rounded else area)["ring"][:, c % RING, 4 * half:4 * half + 4].rearrange("p k f -> p (k f)")

        def high_of(q):
            return area_r["early_mod"][:, 2048 * (q % HIGHS):2048 * (q % HIGHS) + 2048]

        def high_free(st, i, m, half, E):
            q = 2 * m + half - HIGHS
            if q < 0:
                i, q = i - 1, q + 6 * E
            return st.at(i, f"w{q // 2}{'ab'[q % 2]}")

        def rows(w, n):
            return w.rearrange("(k p) f -> p k f", p=P)[:, :, n]


        h = carve("work", TT, D)
        cond_high, cond_low = (area_r["work"][:, o:o + D].rearrange("p (k m) -> p k m", k=KD) for o in (0, 3 * D))
        gain1, gain2 = h[:, 1], h[:, 2]
        junk_wide = work[:, NWORK - D:NWORK]

        top["work"] = 0
        pqk = carve("work", TT, 512)
        pv = carve("work", TT, 512)
        pz = carve("work", TT, 512)
        gaT = carve("work", SEQ)
        gla_spare = ring[:, 2:4].rearrange("p s k f -> p (s k f)")
        gate_e, gate_a, gate_g = (gla_spare[:, 1024 * n:1024 * n + 1024] for n in range(3))
        eb_all, enb_all, ekb_all = (gla_spare[:, 1024 * n:1024 * n + 1024].rearrange("p (t b) -> p t b", t=TT) for n in (3, 4, 5))
        gla_sq = gla_spare[:, 0:2048].rearrange("p (t b) -> p t b", t=TT)
        on_g = gla_spare[:, 6144:8192].rearrange("p (t a b) -> p t a b", t=TT, a=HEADS)
        kz = mod[:, 512:1536].rearrange("p (s c a b) -> p s c a b", s=2, c=2, a=2)
        qd = carve("work", 2, 2, P)
        ku = carve("work", 2, 2, 256)
        at_g = carve("work", HEADS, P)
        st_g = carve("work", 2, 256)
        sm_g = carve("work", 4, TT * HEADS)
        gla_end = top["work"]
        top["work"] = 0
        rep = carve("work", 2, HEADS, P)
        ex = carve("work", HEADS, P)
        xt = carve("work", TT, HEADS, P)
        kb_b = carve("work", HEADS, P)
        vb_b = carve("work", HEADS, P)
        vn = carve("work", HEADS, P)
        st_b = carve("work", HEADS, P)
        zg_b = carve("work", HEADS, P)
        on_b = carve("work", HEADS, P)
        sm_b = carve("work", 5, HEADS)
        spare = ring[:, 2:4].rearrange("p s k f -> p (s k f)")
        at, lev_at, xx, pm = (spare[:, 2048 * n:2048 * n + 2048].rearrange("p (t a b) -> p t a b", t=TT, a=HEADS) for n in range(4))
        prep = spare[:, 0:6144].rearrange("p (n s a b) -> p n s a b", n=6, s=2, a=HEADS)
        u_b, wt_b, qd_b, qkt = (prep[:, n] for n in range(4))
        ku_b = spare[:, 4096:6144].rearrange("p (s c a b) -> p s c a b", s=2, c=2, a=HEADS)
        top["work"] = max(gla_end, top["work"])
        pzb = carve("work", TT, 512)
        psm = carve("work", TT, 24)
        qkvT = carve("work", 12, 3 + SEQ)
        pre_u = carve("work", TT, 8)
        pre_a = carve("work", TT, 8)
        pre_l = carve("work", TT, 8)
        g_b = carve("work", TT, HEADS)
        lnb = carve("work", TT, HEADS)
        nexpa = carve("work", HEADS)
        ssk = carve("work", TT, 2 * HEADS)
        lk = carve("work", TT, HEADS)
        lq = carve("work", TT, HEADS)
        lbk = carve("work", TT, HEADS)
        pre = carve("work", 5, TT, HEADS)
        pexp = carve("work", 5, TT, HEADS)
        colj = carve("work", TT, HEADS)
        conv_t = mod[:, 0:1024].rearrange("p (a b) -> p a b", a=2)
        conv_sq = mod[:, 1024:2048].rearrange("p (a b) -> p a b", a=2)
        junk = mod[:, 1536:2048]
        res_tmp = mod[:, 0:512]
        oT = hT

        top["work"] = 0
        pq = carve("work", TT, QW)
        pkv = carve("work", TT, 512)
        kTz = carve("work", NKV, 2, CHUNK + SEQ)
        sm = [carve("work", NQ, 256), pq.rearrange("p t (a b) -> p (t a) b", b=256)]
        pT = carve("work", 2, 2, 2, P)
        o_sb = carve("work", NQ, HD)
        posf = carve("work", TT)
        qk_s = carve("work", 4, TT, 20)
        sw_s = carve("work", 2, 6, NQ)
        cs, sn = (w2aug[:, 128 * n:128 * n + 128].rearrange("p (t a) -> p t a", t=TT) for n in range(2))
        rang, rk, rr, rc = (hT[:, 0, 128 * n:128 * n + 128].rearrange("p (t a) -> p t a", t=TT) for n in range(4))
        smf = sm[0].rearrange("p a b -> p (a b)")
        rope_t = [smf[:, 640 * i:640 * i + 640].rearrange("p (a b) -> p a b", a=20) for i in range(4)]
        sq2 = smf[:, 2560:2560 + 1280]
        qT = hT

        top["work"] = TT * D
        h_high = carve("work", TT, D, rounded=True)
        h_low = area_r["work"][:, 0:TT * D].rearrange("p (t d) -> p t d", t=TT)
        pd = carve("work", TT, EG * P, rounded=True)
        pdT = carve("work", EG, SEQ, rounded=True)
        ys = carve("work", EG, 2, D, rounded=True)
        moe_tmp = carve("work", 2, 512)
        sg = carve("work", FF)
        he = carve("work", FF)
        heT = carve("work", EG, 2, 4, P, rounded=True)
        ws = carve("work", EG)
        pcol = carve("work", TT, EG)
        wcol = carve("work", TT, EG, 2, rounded=True)
        posm = carve("work", TT, NE + EG)
        wgt_parts = carve("work", TT, NE + EG, 2, rounded=True)
        basef = carve("work", 8)
        nov = carve("work", 1)
        top["work"] = 2 * TT * D + TT * EG * P + EG * SEQ
        wgt = carve("work", TT, NE + EG)
        r_e = carve("work", TT, NE)
        r_sc = carve("work", TT, NE)
        r_sel = carve("work", TT, NE)
        r_a = carve("work", TT, NE)
        r_b = carve("work", TT, NE)
        mk1 = carve("work", TT, NE)
        mk = carve("work", TT, NE)
        r_g = [carve("work", TT, NGRP) for _ in range(8)]
        r_t = carve("work", TT)
        r_u = carve("work", TT)
        fl = carve("work", 3, NE)
        key = carve("work", 3, NE)
        top8 = carve("work", 8)
        ent = carve("work", 8)
        hT_high = area_r["hT"][:]
        hT_low = area_r["x"].rearrange("p t (a f) -> p (t a) f", a=2)

        split_chunks = [(first[("ada", 0)] + n, 512, 10752) for n in range(12)]
        split_chunks += [(first[("ab", 0)] + n, 24 if n == 1 else 512, 3 * 2048) for n in range(8)]
        split_chunks += [(first[("ada", 1)] + n, 512, 10752) for n in range(12)]
        SPLIT_AB, SPLIT_ADA1 = 12, 20

        def quarter(i):
            c, w, at_ = split_chunks[i // 4]
            k = slice(2 * (i % 4), 2 * (i % 4) + 2)
            high = area_r["work"][:, at_ + D * (i % 3):at_ + D * (i % 3) + D].rearrange("p (k f) -> p k f", k=2)
            return ring[:, c % RING, k, 0:w], high[:, :, 0:w], area_r["ring"][:, c % RING, k, 0:w]

        def quarter_used(i):
            chunk, q = i // 4, i % 4
            if q < 3:
                return Q_PE.sem, Q_PE.at(3 * chunk + q, "used")
            if SPLIT_AB <= chunk < SPLIT_ADA1:
                return proj_pe.sem, proj_pe.at(4 * (chunk - SPLIT_AB) + 3, "job")
            return ada_pe.sem, ada_pe.at(chunk - (SPLIT_ADA1 - 12 if chunk >= SPLIT_ADA1 else 0), "mod")

        hgT = area_r["hT"].rearrange("p k (s n) -> p k s n", s=2)
        GATHER_BANKS, COMBINE_BANKS = (1, 2, 4, 5), (0, 6, 7, 3)
        GATE_BANK, UP_BANK, TURN_BANK, WS_BANK = 7, 3, 6, 0
        Y_BANK, PT_BANK = (4, 1), (0, 7)

        def cols(t):
            return slice(P * t, P * t + P)

        AB_COLS = [0, C_GA, 512, C_QKVB, C_QKVB + 512, C_QKVB + 1024, C_ZA, C_ZB]
        AB_KIND = ["qk", "small", "v", "f0", "f1", "f2", "za", "zb"]
        jobs = [(n, t, AB_KIND[n]) for n in range(8) for t in range(TT)]
        emptied, counts = [], {"s": 0, "v": 0}
        for j, (n, t, kind) in enumerate(jobs):
            e = "s" if kind in ("za", "zb") or j % 2 else "v"
            emptied.append((e, counts[e]))
            counts[e] += 1

        swa_jobs = [(n, t) for n in range(3) for t in range(TT)]

        def swa_dst(n, t):
            return pkv[:, t] if n == 0 else pq[:, t, 512 * (n - 1):512 * n]

        for j, _ in enumerate(swa_jobs):
            e = "s" if j % 2 else "v"
            emptied.append((e, counts[e]))
            counts[e] += 1
        NJ = len(jobs)

        def emptier(j):
            e, k = emptied[j]
            st = proj_act if e == "s" else proj_dve
            return st.sem, st.at(k, "ev")

        def head_parts(t):
            return ((pq[:, t].rearrange("p (a b) -> p a b", a=NQ), slice(0, NQ)),
                    (pkv[:, t, 0:256].rearrange("p (a b) -> p a b", a=NKV), slice(NQ, 20)))

        def rotations(multiply, t, which):
            for n in which:
                for xh, at_ in head_parts(t):
                    src = xh[:, :, 0:32] if n in (0, 3) else xh[:, :, 32:64]
                    w = (cs if n in (0, 2) else sn)[:, t].unsqueeze(1).to_broadcast([P, at_.stop - at_.start, 32])
                    ins = multiply(rope_t[n][:, at_], src, w)
            return ins

        block = ctx.enter_context(nc.Block())

        @block.sync
        def _(sp):

            def load(c, dst, src):
                if c >= RING:
                    sp.wait_ge(chunk_used, c - RING + 1)
                sp.dma_start(dst, src).then_inc(chunk_in[c % RING], 16)

            def load_columns(key, w, starts):
                for n, lo in enumerate(starts):
                    c = first[key] + n
                    load(c, slot(c), rows(w, slice(lo, lo + 512)))

            sp.dma_start(cond, a["c_cols"]).then_inc(cond_in, 16)
            load_columns(("ada", 0), a["ada_w"][0], range(0, 6 * D, 512))
            for n, lo in enumerate(AB_COLS):
                c = first[("ab", 0)] + n
                if n == 1:
                    if c >= RING:
                        sp.wait_ge(chunk_used, c - RING + 1)
                    sp.dma_start(slot(c)[:, :, 0:RANK], rows(a["ab_w_in"][0], slice(C_GA, C_GA + RANK))
                                 ).then_inc(small_in, 16)
                    load(c, slot(c)[:, :, RANK:RANK + 8], rows(a["ab_w_in"][0], slice(C_AB, C_AB + 8)))
                else:
                    load(c, slot(c), rows(a["ab_w_in"][0], slice(lo, lo + 512)))
            load_columns(("abo", 0), a["ab_w_out"][0], range(0, D, 512))
            def experts(l):
                c0 = first[("moe", l)]
                ws_ = [a["moe_w_gate"][l], a["moe_w_up"][l], a["moe_w_down"][l]]
                use = use_order(EG)
                S = moe_steps[l][0]

                def weights(e, w):
                    return ws_[w][e].rearrange("(k p) f -> p k f", p=P)

                last = 3 * EG - RING

                def used_before(i, m):
                    return S.at(i, f"w{m - RING}b") if m >= RING else S.at(i - 1, f"w{m + last}b")

                def load_chunk(i, group, m):
                    e, w = use[m]
                    c = c0 + 3 * EG * group + m
                    sp.dma_start(expert_view(slot(c), w), weights(EG * i + e, w)).then_inc(chunk_in[c % RING], 16)

                for m in range(RING):
                    sp.wait_ge(chunk_used, c0 + m - RING + 1)
                    if l == 0 and m == 0:
                        sp.wait_ge(phase_done, 9)
                    load_chunk(0, 0, m)
                for m in range(RING, 3 * EG):
                    sp.wait_ge(S.sem, used_before(0, m))
                    load_chunk(0, 0, m)
                with sp.Fori(0, NPAIRS - 1) as i:
                    for g in (1, 2):
                        for m in range(3 * EG):
                            sp.wait_ge(S.sem, used_before(2 * i + g, m))
                            load_chunk(2 * i + g, g, m)
                for m in range(3 * EG):
                    sp.wait_ge(S.sem, used_before(NE // EG - 1, m))
                    load_chunk(NE // EG - 1, 1, m)
                sp.wait_ge(RT_DVE.sem, RT_DVE.at(l, "ovl"))
                n_over = sp.value_load(ovl_i[0:1, 8:9], min_val=0, max_val=MAXOVER)
                over_pe = over_steps[l][0]
                with sp.Fori(0, MAXOVER) as j:
                    e = sp.value_load(ovl_i[0:1, bass.ds(j, 1)], min_val=0, max_val=NE - 1)
                    with sp.If(n_over > j):
                        sp.wait_ge(S.sem, S.at(NE // EG - 1, "c7"))
                        sp.wait_ge(over_pe.sem, over_pe.at(j - 1, "c7"))
                        for w in range(3):
                            sp.dma_start(expert_view(ring[:, w], w), weights(e, w)).then_inc(over_in[l], 16)


            experts(0)
            sp.wait_ge(experts_through, 1)
            load_columns(("ada", 1), a["ada_w"][1], range(0, 6 * D, 512))
            load_columns(("swa", 1), a["swa_w_in"][0], (QW, 0, 512))
            load_columns(("swo", 1), a["swa_w_out"][0], range(0, D, 512))
            experts(1)
            sp.wait_ge(phase_done, 3 * 9)
            sp.dma_start(out[0].rearrange("(t p) d -> p t d", p=P), x[:]).then_inc(out_written, 16)
            sp.wait_ge(out_written, 16)

        @block.gpsimd
        def _(pool):
            def param(dst, src):
                nc.gpsimd.dma_start(dst, src).then_inc(params_in, 16)

            def bc(v):
                return v.partition_broadcast(P)

            def pool_tt(out, in0, in1):
                return nc.gpsimd.tensor_tensor(out, in0, in1, ALU.mult)

            def residual(st, i):
                SV, SG = st[2], st[3]
                for j in range(8):
                    xs = x[:, j // 2, 512 * (j % 2):512 * (j % 2) + 512]
                    pool.wait_ge(SV.sem, SV.at(i, f"m{j}"))
                    nc.gpsimd.tensor_tensor(xs, xs, moe_tmp[:, j % 2], ALU.add).then_inc(SG.sem, SG.one(f"x{j}"))

            def experts(l):
                st, so = moe_steps[l], over_steps[l]
                pool.sem_inc(st[3].sem, st[3].n)
                pool.sem_inc(so[3].sem, so[3].n)
                with pool.Fori(0, NPAIRS) as i:
                    for g in range(2):
                        residual(st, 2 * i + g)
                pool.wait_ge(RT_DVE.sem, RT_DVE.at(l, "ovl"))
                n_over = pool.value_load(ovl_i[0:1, 8:9], min_val=0, max_val=MAXOVER)
                with pool.Fori(0, MAXOVER) as j:
                    with pool.If(n_over > j):
                        residual(so, j)
                pool.drain().then_inc(x_added, 1)

            def norm_shift(s):
                for t in (1, 3):
                    pool.wait_ge(norm_dve.sem, norm_dve.at(s, f"hx{t}"))
                    nc.gpsimd.tensor_tensor(h[:, t], h[:, t], mod[:, 0:D], ALU.add).then_inc(norm_pool.sem, norm_pool.one(f"h{t}"))

            for l in range(2):
                if l == 1:
                    pool.wait_ge(phase_done, 3 * 5)
                nc.gpsimd.dma_start(mod[0:1, :], a["ada_b"][l:l + 1]).then_inc(bias_in[l], 16)
                if l == 0:
                    pool.wait_ge(chunk_in[0], 16)
                nc.gpsimd.dma_start(gain1, bc(a["norm_mix"][l])).then_inc(gains_in[l], 16)
                nc.gpsimd.dma_start(gain2, bc(a["norm_ffn"][l])).then_inc(gains_in[l], 16)
                if l == 0:
                    param(w2aug[0:RANK, :], a["gla_gate_w2"][0])
                    param(w2aug[RANK:RANK + 1, :], a["gla_gate_b"][0:1])
                    param(conv_w.rearrange("p c k -> p (c k)"), a["conv_cols"])
                    param(gla_gain, bc(a["gla_norm"][0]))
                    param(gdn_gain, bc(a["gdn_norm"][0]))
                    param(q_gain, bc(a["swa_q_norm"][0]))
                    param(k_gain, bc(a["swa_k_norm"][0]))
                    param(sink, bc(a["swa_sinks"][0]))
                    param(router_w, a["router_w"].rearrange("(k p) e -> p k e", p=P))
                    param(router_b, bc(a["router_bias"]))
                    param(a_log, bc(a["gdn_a_log"][0]))
                    param(dt_bias, bc(a["gdn_dt_bias"][0]))
                    param(pos_i[:], a["pos_cols"])
                    norm_shift(0)
                    pool.wait_ge(phase_done, 3)
                    nc.gpsimd.dma_start(x[:], a["x"][0].rearrange("(t p) d -> p t d", p=P)).then_inc(x_again, 16)
                else:
                    norm_shift(1)
                    for t in range(TT):
                        pool.wait_ge(QK_DVE.sem, QK_DVE.at(t, "b"))
                        rotations(pool_tt, t, (2, 3)).then_inc(QK_POOL.sem, QK_POOL.one("c"))
                experts(l)

        NPARAMS = 13

        @block.tensor
        def _(pe):
            mm = nc.tensor.matmul

            def turn(dst, src, k=P):
                return nc.tensor.transpose(dst, src, ident[0:k, 0:k])

            def used(ins):
                ins.then_inc(chunk_used, 1)

            def parts_mm(out, a, w, start, stop):
                mm(out, a[1], w[0], start=start, stop=False)
                mm(out, a[0], w[0], start=False, stop=False)
                return mm(out, a[0], w[1], start=False, stop=stop)

            def ada(l):
                pe.wait_ge(rep_dve.sem, rep_dve.at(l, "rep"))
                for n in range(12):
                    r = 12 * l + n
                    if r >= 4:
                        pe.wait_ge(ada_dve.sem, ada_dve.at(r - 4, "mod"))
                    for q in range(4):
                        qi = 4 * (SPLIT_ADA1 * l + n) + q
                        pe.wait_ge(Q_DVE.sem, Q_DVE.at(qi, "low"))
                        _, high, low = quarter(qi)
                        for k in range(2):
                            kk = 2 * q + k
                            ins = parts_mm(bank(n % 4), (cond_high[:, kk], cond_low[:, kk]), (high[:, k], low[:, k]), kk == 0, False)
                        if q < 3:
                            ins.then_inc(Q_PE.sem, Q_PE.one("used"))
                        else:
                            if n == 0:
                                pe.wait_ge(bias_in[l], 16)
                                pe.wait_ge(const_in, 16)
                            ins = mm(bank(n % 4), cst("ones")[0:1, :], mod[0:1, 512 * n:512 * n + 512], start=False, stop=True)
                            ins.then_inc(ada_pe.sem, ada_pe.one("mod"))
                        if q == 0 and n:
                            pe.wait_ge(ada_pe.sem, ada_pe.at(r - 1, "mod"))
                            pe.sem_inc(chunk_used, 1)
                pe.wait_ge(ada_pe.sem, ada_pe.at(r, "mod"))
                pe.sem_inc(chunk_used, 1)

            def norm(s):
                for t in range(TT):
                    if t % 2:
                        pe.wait_ge(norm_pool.sem, norm_pool.at(s, f"h{t}"))
                    else:
                        pe.wait_ge(norm_dve.sem, norm_dve.at(s, f"h{t}"))
                    if t >= 2:
                        pe.wait_ge(norm_act.sem, norm_act.at(s, f"ev{t - 2}"))
                        pe.wait_ge(norm_dve.sem, norm_dve.at(s, f"ev{t - 2}"))
                    for half, name in enumerate(("lo", "hi")):
                        for k in range(4):
                            kk = 4 * half + k
                            ins = turn(bank(4 + 2 * (t % 2) + half)[:, cols(k)], h[:, t, kk * P:kk * P + P])
                        ins.then_inc(norm_pe.sem, norm_pe.one(f"{name}{t}"))

            def project_ab():
                pe.wait_ge(norm_act.sem, norm_act.at(0, "ev3"))
                pe.wait_ge(norm_dve.sem, norm_dve.at(0, "ev3"))

                def sums(ct):
                    pe.wait_ge(conv_act.sem, conv_act.at(ct, "sq"))
                    for t in range(TT):
                        ins = mm(bank(5, TT, 8)[:, t, ct:ct + 1], conv_sq[:, ct % 2, cols(t)], cst("ones", 0, 1),
                                 start=True, stop=True)
                    ins.then_inc(conv_pe.sem, conv_pe.one("ss"))

                for n in range(8):
                    kind = AB_KIND[n]
                    for q in range(4):
                        qi = 4 * (SPLIT_AB + n) + q
                        pe.wait_ge(Q_DVE.sem, Q_DVE.at(qi, "low"))
                        _, high, low = quarter(qi)
                        for t in range(TT):
                            j = 4 * n + t
                            if q == 0 and n:
                                pe.wait_ge(*emptier(j - 4))
                            for k in range(2):
                                kk = 2 * q + k
                                first_, last_ = kk == 0, kk == KD - 1
                                if kind[0] == "f":
                                    ins = parts_mm(bank(t), (high[:, k, cols(t)], low[:, k, cols(t)]), (hT_high[:, kk], hT_low[:, kk]), first_, last_)
                                else:
                                    w = 24 if kind == "small" else 512
                                    ins = parts_mm(bank(t)[:, 0:w], (hT_high[:, kk, cols(t)], hT_low[:, kk, cols(t)]), (high[:, k], low[:, k]), first_, last_)
                            if q == 3:
                                ins.then_inc(proj_pe.sem, proj_pe.one("job"))
                        if q < 3:
                            ins.then_inc(Q_PE.sem, Q_PE.one("used"))
                        if q == 0 and n:
                            pe.wait_ge(proj_pe.sem, proj_pe.at(4 * n - 1, "job"))
                            pe.sem_inc(chunk_used, 1)
                        ct = 4 * (n - 4) + q - 1
                        if 0 <= ct < 8:
                            sums(ct)
                pe.wait_ge(proj_pe.sem, proj_pe.at(31, "job"))
                pe.sem_inc(chunk_used, 1)

            def gla_gates():
                for t in range(TT):
                    ins = turn(bank(0)[0:RANK, cols(t)], psm[:, t, 0:RANK])
                ins.then_inc(GATE_PE.sem, GATE_PE.one("gaT"))
                pe.wait_ge(GATE_DVE.sem, GATE_DVE.at(0, "gaT"))
                for t in range(TT):
                    o = 256 * (t % 2)
                    ins = mm(bank(2 + t // 2)[:, o:o + 256], gaT[0:RANK + 1, cols(t)], w2aug[0:RANK + 1, :], start=True, stop=True)
                ins.then_inc(GATE_PE.sem, GATE_PE.one("z"))
                pe.wait_ge(GATE_DVE.sem, GATE_DVE.at(0, "g"))
                for t in range(TT):
                    g = gate_g[:, 256 * t:256 * t + 256]
                    for f in range(2):
                        mm(bank(4 + t)[:, cols(f)], g[:, cols(f)], cst("tri"), start=True, stop=True)
                    ins = mm(bank(4 + t)[:, 256:512], cst("later"), g, start=True, stop=True)
                ins.then_inc(GATE_PE.sem, GATE_PE.one("cums"))

            def gla_turn(t):
                if t:
                    pe.wait_ge(GLP_DVE.sem, GLP_DVE.at(t - 1, "kz"))
                else:
                    pe.wait_ge(GATE_ACT.sem, GATE_ACT.at(0, "ekb"))
                for n in range(4):
                    ins = turn(bank(6)[:, cols(n)], pqk[:, t, cols(n)])
                ins.then_inc(GLP_PE.sem, GLP_PE.one("qkT"))

            def gla_scores(t):
                pe.wait_ge(GLP_DVE.sem, GLP_DVE.at(t, "kz"))
                for hd in range(HEADS):
                    ins = mm(bank(7)[:, cols(hd)], kz[:, t % 2, hd % 2, hd // 2], qd[:, t % 2, hd // 2], start=True, stop=True)
                ins.then_inc(GLP_PE.sem, GLP_PE.one("A"))

            def gla_updates(t):
                pe.wait_ge(GLP_DVE.sem, GLP_DVE.at(t, "ku"))
                for c in range(2):
                    if t:
                        pe.wait_ge(GLA_DVE.sem, GLA_DVE.at(t - 1, f"s{c}"))
                    for f in range(2):
                        ins = mm(bank(4 + c)[:, 256 * f:256 * f + 256], ku[:, t % 2, c, cols(f)], pv[:, t, 256 * f:256 * f + 256],
                                 start=True, stop=True)
                    ins.then_inc(GLP_PE.sem, GLP_PE.one(f"u{c}"))

            def gla():
                gla_gates()
                gla_turn(0)
                gla_scores(0)
                gla_updates(0)
                for t in range(TT):
                    if t + 1 < TT:
                        gla_turn(t + 1)
                    pe.wait_ge(GLA_DVE.sem, GLA_DVE.at(t, "A"))
                    for hd in range(HEADS):
                        ins = mm(bank(t)[:, cols(hd)], at_g[:, hd], pv[:, t, cols(hd)], start=(hd == 0), stop=False,
                                 skip_group_check=True)
                    ins.then_inc(GLA_PE.sem, GLA_PE.one("o"))
                    for c in range(2):
                        if c:
                            if t + 1 < TT:
                                gla_scores(t + 1)
                            pe.wait_ge(GLA_DVE.sem, GLA_DVE.at(t, "s0"))
                        r = slice(CHUNK * c, CHUNK * c + CHUNK)
                        for f in range(2):
                            ins = mm(bank(t)[r, 256 * f:256 * f + 256], qd[:, t % 2, f, r], st_g[:, f], start=False, stop=(f == 1),
                                     skip_group_check=True)
                        ins.then_inc(GLA_PE.sem, GLA_PE.one(f"int{c}"))
                    if t + 1 < TT:
                        gla_updates(t + 1)
                for t in range(TT):
                    pe.wait_ge(GLN_DVE.sem, GLN_DVE.at(0, f"on{t}"))
                    for hd in range(HEADS):
                        ins = turn(bank(4 + t)[:, cols(hd)], on_g[:, t, hd])
                    ins.then_inc(GLN_PE.sem, GLN_PE.one("oT"))

            def gdn_pre():
                pe.wait_ge(PRE_DVE.sem, PRE_DVE.at(0, "g"))
                gf = g_b.rearrange("p t h -> p (t h)")
                for n, m in enumerate((cst("tri"), cst("later"), cst("in_chunk", 0, P), cst("in_chunk", P, P))):
                    ins = mm(bank(4)[:, 16 * n:16 * n + 16], m, gf, start=True, stop=True)
                ins.then_inc(PRE_PE.sem, PRE_PE.one("cum"))

            def tok(t):
                return slice(3 + P * t, 3 + P * t + P)

            def gdn_inverses():
                for t in range(TT):
                    pe.wait_ge(MAT_DVE.sem, MAT_DVE.at(0, f"rep{t}"))
                    for hd in range(HEADS):
                        mm(bank(t)[:, cols(hd)], xx[:, t, hd], cst("tri"), start=True, stop=False)
                        ins = mm(bank(t)[:, cols(hd)], xt[:, t, hd], ident, start=False, stop=True)
                    ins.then_inc(MAT_PE.sem, MAT_PE.one(f"rows{t}"))
                    for hd in range(HEADS):
                        ins = mm(bank(4 + t)[:, cols(hd)], qkvT[:, 4 + hd, tok(t)], qkvT[:, 4 + hd, tok(t)], start=True, stop=True)
                    ins.then_inc(MAT_PE.sem, MAT_PE.one(f"kk{t}"))
                for t in range(TT):
                    pe.wait_ge(MAT_DVE.sem, MAT_DVE.at(0, f"xt0{t}"))
                    for hd in range(HEADS):
                        ins = turn(bank(t)[:, cols(hd)], xt[:, t, hd])
                    ins.then_inc(MAT_PE.sem, MAT_PE.one(f"x0{t}"))
                for l in range(1, 6):
                    for t in range(TT):
                        if l == 1:
                            pe.wait_ge(MAT_ACT.sem, MAT_ACT.at(0, f"x0{t}"))
                            pe.wait_ge(MAT_DVE.sem, MAT_DVE.at(0, f"level1{t}"))
                        else:
                            pe.wait_ge(INV_DVE.sem, INV_DVE.at(0, f"level{l - 1}{t}"))
                        for hd in range(HEADS):
                            ins = mm(bank(t)[:, cols(hd)], lev_at[:, t, hd], xx[:, t, hd], start=True, stop=True)
                        ins.then_inc(INV_PE.sem, INV_PE.one(f"p{l}{t}"))
                    for t in range(TT):
                        pe.wait_ge(INV_ACT.sem, INV_ACT.at(0, f"p{l}{t}"))
                        for hd in range(HEADS):
                            ins = mm(bank(4 + t)[:, cols(hd)], pm[:, t, hd], xt[:, t, hd], start=True, stop=True)
                        if l < 5:
                            for hd in range(HEADS):
                                ins = mm(bank(t)[:, cols(hd)], xt[:, t, hd], pm[:, t, hd], start=True, stop=True)
                        ins.then_inc(INV_PE.sem, INV_PE.one(f"y{l}{t}"))
                pe.wait_ge(INV_DVE.sem, INV_DVE.at(0, f"xt5{TT - 1}"))

            def gdn_prep(t):
                pe.wait_ge(GDP_DVE.sem, GDP_DVE.at(t, "rep"))
                if t:
                    pe.wait_ge(GDP_ACT.sem, GDP_ACT.at(t - 1, "eq"))
                for hd in range(HEADS):
                    mm(bank(1)[:, cols(hd)], rep[:, 0, hd], cst("tri"), start=True, stop=False)
                    ins = mm(bank(1)[:, cols(hd)], rep[:, 1, hd], ident, start=False, stop=True)
                ins.then_inc(GDP_PE.sem, GDP_PE.one("rows"))
                if t:
                    pe.wait_ge(GDP_DVE.sem, GDP_DVE.at(t - 1, "u"))
                for hd in range(HEADS):
                    ins = mm(bank(3)[:, cols(hd)], qkvT[:, 4 + hd, tok(t)], qkvT[:, hd, tok(t)], start=True, stop=True)
                ins.then_inc(GDP_PE.sem, GDP_PE.one("kq"))
                if t:
                    pe.wait_ge(GDP_ACT.sem, GDP_ACT.at(t - 1, "wT"))
                for b, f in ((6, 4), (7, 8)):
                    for hd in range(HEADS):
                        ins = turn(bank(b)[:, cols(hd)], qkvT[:, f + hd, tok(t)])
                ins.then_inc(GDP_PE.sem, GDP_PE.one("kv"))

            def gdn_solve(t):
                pe.wait_ge(GDP_DVE.sem, GDP_DVE.at(t, "vb"))
                for hd in range(HEADS):
                    mm(bank(3)[:, cols(hd)], xt[:, t, hd], vb_b[:, hd], start=True, stop=True)
                for hd in range(HEADS):
                    ins = mm(bank(6)[:, cols(hd)], kb_b[:, hd], xt[:, t, hd], start=True, stop=True)
                ins.then_inc(GDP_PE.sem, GDP_PE.one("uw"))

            def turn_output_b(t):
                pe.wait_ge(GDN_DVE.sem, GDN_DVE.at(t, "on"))
                if t:
                    pe.wait_ge(GDO_ACT.sem, GDO_ACT.at(t - 1, "oT"))
                for hd in range(HEADS):
                    ins = turn(bank(2)[:, cols(hd)], on_b[:, hd])
                ins.then_inc(GDO_PE.sem, GDO_PE.one("oT"))

            def gdn(t):
                b = t % 2
                if t + 1 < TT:
                    gdn_prep(t + 1)
                if t:
                    turn_output_b(t - 1)
                pe.wait_ge(GDP_ACT.sem, GDP_ACT.at(t, "wT"))
                if t:
                    pe.wait_ge(GDN_DVE.sem, GDN_DVE.at(t - 1, "on"))
                    pe.wait_ge(GDN_ACT.sem, GDN_ACT.at(t - 1, "ss"))
                for c in range(2):
                    r = slice(CHUNK * c, CHUNK * c + CHUNK)
                    if c:
                        pe.wait_ge(GDN_DVE.sem, GDN_DVE.at(t, "s0"))
                    for hd in range(HEADS):
                        ins = mm(bank(4)[r, cols(hd)], wt_b[:, b, hd, r], st_b[:, hd], start=True, stop=True)
                    ins.then_inc(GDN_PE.sem, GDN_PE.one(f"ws{c}"))
                    pe.wait_ge(GDN_DVE.sem, GDN_DVE.at(t, f"vn{c}"))
                    for hd in range(HEADS):
                        mm(bank(0)[r, cols(hd)], qd_b[:, b, hd, r], st_b[:, hd], start=True, stop=False)
                        ins = mm(bank(0)[r, cols(hd)], qkt[:, b, hd, r], vn[:, hd], start=False, stop=True)
                    ins.then_inc(GDN_PE.sem, GDN_PE.one(f"o{c}"))
                    for hd in range(HEADS):
                        ins = mm(bank(5)[:, cols(hd)], ku_b[:, b, c, hd], vn[:, hd], start=True, stop=True)
                    ins.then_inc(GDN_PE.sem, GDN_PE.one(f"up{c}"))
                if t + 1 < TT:
                    gdn_solve(t + 1)

            def turn_tile(l, t):
                u = TT * l + t
                pe.wait_ge(TN_DVE.sem, TN_DVE.at(u, "h"))
                if t >= 2:
                    pe.wait_ge(TN_ACT_EV.sem, TN_ACT_EV.at(u - 2, "ev"))
                    pe.wait_ge(TN_DVE_EV.sem, TN_DVE_EV.at(u - 2, "ev"))
                for half, name in enumerate(("lo", "hi")):
                    for k in range(4):
                        kk = 4 * half + k
                        ins = turn(bank(4 + 2 * (t % 2) + half)[:, cols(k)], h[:, t, kk * P:kk * P + P])
                    ins.then_inc(TN_PE.sem, TN_PE.one(name))

            def project_out(l):
                c0 = first[("abo", 0) if l == 0 else ("swo", 1)]
                for t in range(TT):
                    for n in range(2):
                        j = 8 * l + 2 * t + n
                        if t == 0:
                            pe.wait_ge(chunk_in[(c0 + n) % RING], loaded(c0 + n))
                        if j >= 4:
                            pe.wait_ge(outp_dve.sem, outp_dve.at(j - 4, "tmp"))
                        for k in range(KD):
                            ins = mm(bank(j % 4), oT[:, k, cols(t)], slot(c0 + n)[:, k], start=(k == 0), stop=(k == 7))
                        ins.then_inc(outp_pe.sem, outp_pe.one("job"))
                    if t:
                        turn_tile(l, t - 1)
                pe.wait_ge(outp_pe.sem, outp_pe.at(j, "job"))
                pe.sem_inc(chunk_used, 2)
                turn_tile(l, TT - 1)

            def project_swa():
                pe.wait_ge(norm_act.sem, norm_act.at(1, "ev3"))
                pe.wait_ge(norm_dve.sem, norm_dve.at(1, "ev3"))
                for jj, (n, t) in enumerate(swa_jobs):
                    j = NJ + jj
                    c = first[("swa", 1)] + n
                    if t == 0:
                        pe.wait_ge(chunk_in[c % RING], loaded(c))
                    if jj >= 4:
                        pe.wait_ge(*emptier(j - 4))
                    for k in range(KD):
                        ins = mm(bank(j % 4), hT[:, k, cols(t)], slot(c)[:, k], start=(k == 0), stop=(k == 7))
                    ins.then_inc(proj_pe.sem, proj_pe.one("job"))
                    if t == TT - 1:
                        pe.wait_ge(proj_pe.sem, proj_pe.at(j, "job"))
                        pe.sem_inc(chunk_used, 1)
                    if n == 2 and t:
                        turn_qk(t - 1)
                turn_qk(TT - 1)

            def turn_qk(t):
                pe.wait_ge(QK_DVE.sem, QK_DVE.at(t, "rope"))
                if t:
                    pe.wait_ge(QT_ACT.sem, QT_ACT.at(t - 1, "q"))
                    pe.wait_ge(QT_DVE.sem, QT_DVE.at(t - 1, "k"))
                for n in range(8):
                    ins = turn(bank(4 + n // 4)[:, cols(n % 4)], pq[:, t, cols(n)])
                ins.then_inc(QK_PE.sem, QK_PE.one("q"))
                for n in range(2):
                    ins = turn(bank(6)[:, cols(n)], pkv[:, t, cols(n)])
                ins.then_inc(QK_PE.sem, QK_PE.one("k"))

            def scores(t):
                for n in range(8):
                    if n >= 4:
                        pe.wait_ge(SCO_DVE.sem, SCO_DVE.at(t, f"s{n - 4}"))
                    elif t:
                        pe.wait_ge(SCO_DVE.sem, SCO_DVE.at(t - 1, f"s{n + 4}"))
                    mm(bank(n % 4)[:, 0:384], qT[:, n, cols(t)], kTz[:, n // 2, :, P * t:P * t + 192],
                       start=True, stop=True).then_inc(SCO_PE.sem, SCO_PE.one(f"s{n}"))

            def values(t):
                def turn_pair(n):
                    if n >= 2:
                        pe.wait_ge(VAL_ACT.sem, VAL_ACT.at(t, f"t{n - 2}"))
                    elif t:
                        pe.wait_ge(VAL_ACT.sem, VAL_ACT.at(t - 1, "oT"))
                    for hh in range(2):
                        for own in range(0 if t else 1, 2):
                            ins = turn(bank(4 + n % 2)[:, cols(2 * hh + own)], sm[t % 2][:, 2 * n + hh, cols(own)])
                    ins.then_inc(VAL_PE.sem, VAL_PE.one(f"t{n}"))

                pe.wait_ge(SCO_ACT.sem, SCO_ACT.at(t, "exp"))
                if t:
                    pe.wait_ge(VAL_DVE.sem, VAL_DVE.at(t - 1, "o"))
                turn_pair(0)
                for n in range(8):
                    if n < 7:
                        turn_pair(n + 1)
                    pe.wait_ge(VAL_ACT.sem, VAL_ACT.at(t, f"t{n}"))
                    for hh in range(2):
                        hd = 2 * n + hh
                        o = bank(6 + hd // 8)[:, HD * (hd % 8):HD * (hd % 8) + HD]
                        kv = slice(256 + HD * (n // 2), 256 + HD * (n // 2) + HD)
                        if t:
                            mm(o, pT[:, n % 2, hh, 0], pkv[:, t - 1, kv], start=True, stop=False)
                        ins = mm(o, pT[:, n % 2, hh, 1], pkv[:, t, kv], start=(t == 0), stop=True)
                    ins.then_inc(VAL_PE.sem, VAL_PE.one(f"v{n}"))

            def turn_output(t):
                pe.wait_ge(VAL_DVE.sem, VAL_DVE.at(t, "o"))
                pe.wait_ge(VAL_ACT.sem, VAL_ACT.at(t, "t7"))
                of = o_sb.rearrange("p a b -> p (a b)")
                for n in range(8):
                    ins = turn(bank(4 + n // 4)[:, cols(n % 4)], of[:, cols(n)])
                ins.then_inc(VAL_PE.sem, VAL_PE.one("oT"))

            def swa():
                pe.wait_ge(QT_ACT.sem, QT_ACT.at(TT - 1, "q"))
                pe.wait_ge(QT_DVE.sem, QT_DVE.at(TT - 1, "k"))
                pe.wait_ge(init_dve, 6)
                scores(0)
                for t in range(TT):
                    if t + 1 < TT:
                        scores(t + 1)
                    values(t)
                    turn_output(t)

            def router(l):
                pe.wait_ge(TN_ACT_EV.sem, TN_ACT_EV.at(TT * l + TT - 1, "ev"))
                pe.wait_ge(TN_DVE_EV.sem, TN_DVE_EV.at(TT * l + TT - 1, "ev"))
                for t in range(TT):
                    for k in range(KD):
                        ins = mm(bank(0, TT, NE)[:, t], hT[:, k, cols(t)], router_w[:, k], start=(k == 0), stop=(k == 7))
                ins.then_inc(RT_PE.sem, RT_PE.one("logits"))
                pe.wait_ge(RT_DVE.sem, RT_DVE.at(l, "mk"))
                for t in range(TT):
                    for u in range(t + 1):
                        mm(bank(1, TT, NE)[:, t], cst("before") if u == t else cst("ones"), mk[:, u], start=(u == 0), stop=(u == t))
                for u in range(TT):
                    ins = mm(bank(1)[:, 64:64 + NE], cst("ones"), mk[:, u], start=(u == 0), stop=(u == TT - 1))
                ins.then_inc(RT_PE.sem, RT_PE.one("pos"))

            def expert_block(st, i, E, c0):
                S, SA, SV, SG = st
                use = use_order(E)

                def split_mm(out, a_hi, a_lo, w_hi, w_lo, first_, last_):
                    mm(out, a_lo, w_hi, start=first_, stop=False)
                    mm(out, a_hi, w_hi, start=False, stop=False)
                    return mm(out, a_hi, w_lo, start=False, stop=last_)

                def half_chunk(m, half):
                    w = use[m][1]
                    pe.wait_ge(SV.sem, SV.at(i, f"lo{m}{'ab'[half]}"))
                    return half_view(high_of(2 * m + half), w), half_view(half_of(c0 + m, half, True), w)

                def gate_up(m, which=(0, 1)):
                    e, w = use[m]
                    b = UP_BANK if w else GATE_BANK
                    for half in which:
                        hi, lo = half_chunk(m, half)
                        if m == 0:
                            pe.wait_ge(SA.sem, SA.at(i, f"hg{4 * half + 3}"))
                        for k in range(4):
                            kk = 4 * half + k
                            ins = split_mm(bank(b), hgT[:, kk, 0, cols(e)], hgT[:, kk, 1, cols(e)],
                                           hi[:, k], lo[:, k], kk == 0, kk == KD - 1)
                        ins.then_inc(S.sem, S.one(f"w{m}{'ab'[half]}"))

                def down(m, which=(0, 1)):
                    e, _ = use[m]
                    for half in which:
                        hi, lo = half_chunk(m, half)
                        for yh in range(2):
                            f = slice(512 * yh, 512 * yh + 512)
                            for n in range(2):
                                nn = 2 * half + n
                                ins = split_mm(bank(Y_BANK[e] + yh), heT[:, e, 0, nn], heT[:, e, 1, nn],
                                               hi[:, n, f], lo[:, n, f], nn == 0, nn == 3)
                        ins.then_inc(S.sem, S.one(f"w{m}{'ab'[half]}"))

                def turn_hidden(e):
                    pe.wait_ge(SV.sem, SV.at(i, f"he{e}"))
                    for n in range(4):
                        ins = turn(bank(TURN_BANK)[:, cols(n)], he[:, cols(n)])
                    ins.then_inc(S.sem, S.one(f"hT{e}"))

                pe.wait_ge(SV.sem, SV.at(i if E == 1 else i - 1, "disp"))
                for k in range(KD):
                    if k >= 4:
                        pe.wait_ge(SA.sem, SA.at(i, f"hg{k - 4}"))
                    for part, hp in enumerate((h_high, h_low)):
                        for t in range(TT):
                            ins = mm(bank(GATHER_BANKS[k % 4])[:, 256 * part:256 * part + E * P], hp[:, t, cols(k)],
                                     pd[:, t, 0:E * P], start=(t == 0), stop=(t == 3))
                    ins.then_inc(S.sem, S.one(f"hg{k}"))
                pe.wait_ge(SV.sem, SV.at(i - 1, "m7"))
                gate_up(0)
                for e in range(E):
                    for t in range(TT):
                        ins = mm(bank(WS_BANK)[:, 2 * e:2 * e + 2], pd[:, t, cols(e)], wcol[:, t, e], start=(t == 0), stop=(t == 3))
                ins.then_inc(S.sem, S.one("ws"))
                gate_up(1)
                if E == 2:
                    pe.wait_ge(SA.sem, SA.at(i, "sg0"))
                    gate_up(2)
                    pe.wait_ge(SV.sem, SV.at(i, "he0"))
                    gate_up(3, (0, ))
                turn_hidden(0)
                if E == 2:
                    gate_up(3, (1, ))
                    pe.wait_ge(SV.sem, SV.at(i, "hT0"))
                    down(4, (0, ))
                    turn_hidden(1)
                    down(4, (1, ))
                for e in range(E):
                    for t in range(TT):
                        ins = mm(bank(PT_BANK[e])[:, cols(t)], pd[:, t, cols(e)], ident_r, start=True, stop=True)
                    ins.then_inc(S.sem, S.one(f"pT{e}"))
                pe.wait_ge(SV.sem, SV.at(i, f"hT{E - 1}"))
                down(3 * E - 1)

                def combine(j, e):
                    t, f = j // 2, slice(512 * (j % 2), 512 * (j % 2) + 512)
                    for part in range(2):
                        ins = mm(bank(COMBINE_BANKS[j % 4]), pdT[:, e, cols(t)], ys[:, e, part, f],
                                 start=(e == 0 and part == 0), stop=(e == E - 1 and part == 1))
                    return ins

                if E == 2:
                    pe.wait_ge(SV.sem, SV.at(i, "pT1"))
                    for j in range(4):
                        combine(j, 0)
                pe.wait_ge(SV.sem, SV.at(i, f"y{E - 1}"))
                for j in range(8):
                    if j >= 4:
                        pe.wait_ge(SV.sem, SV.at(i, f"m{j - 4}"))
                    if E == 2 and j >= 4:
                        combine(j, 0)
                    combine(j, E - 1).then_inc(S.sem, S.one(f"c{j}"))

            def experts(l):
                S, so = moe_steps[l][0], over_steps[l][0]
                pe.sem_inc(S.sem, S.n)
                pe.sem_inc(so.sem, so.n)
                pe.wait_ge(split_dve.sem, split_dve.at(l, "lo3"))
                with pe.Fori(0, NPAIRS) as i:
                    for g in range(2):
                        expert_block(moe_steps[l], 2 * i + g, EG, first[("moe", l)] + 3 * EG * g)
                pe.wait_ge(S.sem, S.at(NE // EG - 1, "c7"))
                pe.sem_inc(chunk_used, 3 * NE)
                pe.wait_ge(RT_DVE.sem, RT_DVE.at(l, "ovl"))
                n_over = pe.value_load(ovl_i[0:1, 8:9], min_val=0, max_val=MAXOVER)
                with pe.Fori(0, MAXOVER) as j:
                    with pe.If(n_over > j):
                        expert_block(over_steps[l], j, 1, 0)

            ada(0)
            pe.wait_ge(const_in, 16)
            norm(0)
            project_ab()
            nc.tensor.drain().then_inc(phase_done, 1)
            pe.wait_ge(phase_done, 3 * 1)
            gla()
            nc.tensor.drain().then_inc(phase_done, 1)
            pe.wait_ge(phase_done, 3 * 2)
            gdn_pre()
            gdn_inverses()
            gdn_prep(0)
            gdn_solve(0)
            for t in range(TT):
                gdn(t)
            turn_output_b(TT - 1)
            nc.tensor.drain().then_inc(phase_done, 1)
            pe.wait_ge(phase_done, 3 * 3)
            project_out(0)
            nc.tensor.drain().then_inc(phase_done, 1)
            pe.wait_ge(phase_done, 3 * 4)
            router(0)
            experts(0)
            nc.tensor.drain().then_inc(experts_through, 1)
            nc.tensor.drain().then_inc(phase_done, 1)
            pe.wait_ge(phase_done, 3 * 5)
            ada(1)
            norm(1)
            project_swa()
            nc.tensor.drain().then_inc(phase_done, 1)
            pe.wait_ge(phase_done, 3 * 6)
            swa()
            nc.tensor.drain().then_inc(phase_done, 1)
            pe.wait_ge(phase_done, 3 * 7)
            project_out(1)
            nc.tensor.drain().then_inc(phase_done, 1)
            pe.wait_ge(phase_done, 3 * 8)
            router(1)
            experts(1)
            nc.tensor.drain().then_inc(phase_done, 1)

        @block.scalar
        def _(act):
            def f(out, in_, fn=ACT.Copy, **kw):
                return nc.scalar.activation(out, in_, fn, **kw)

            def square_sum(s, t):
                if t == 0 and s == 0:
                    act.wait_ge(x_in, 16)
                    act.wait_ge(cond_dve.sem, cond_dve.at(0, "silu"))
                if t:
                    act.wait_ge(norm_act.sem, norm_act.at(s, f"ss{t - 1}"))
                f(junk_wide, x[:, t], ACT.Square, accum_out=ss[:, t:t + 1]).then_inc(norm_act.sem, norm_act.one(f"ss{t}"))

            def first_rstd(s):
                act.wait_ge(norm_dve.sem, norm_dve.at(s, "var"))
                f(rstd[:], var[:], ACT.Ln).then_inc(norm_act.sem, norm_act.one("ln"))
                act.wait_ge(norm_act.sem, norm_act.at(s, "ln"))
                f(rstd[:], rstd[:], ACT.Exp, scale=-0.5).then_inc(norm_act.sem, norm_act.one("exp"))

            def high_part(qi):
                c, _, _ = split_chunks[qi // 4]
                if qi % 4 == 0:
                    act.wait_ge(chunk_in[c % RING], loaded(c))
                    if c == first[("ab", 0)] + 1:
                        act.wait_ge(small_in, 16)
                if qi >= 3:
                    act.wait_ge(*quarter_used(qi - 3))
                w, high, _ = quarter(qi)
                f(high, w).then_inc(Q_ACT.sem, Q_ACT.one("high"))

            def ada(l):
                for n in range(12):
                    if l == 0 and n == 2:
                        nc.scalar.dma_start(x[:], a["x"][0].rearrange("(t p) d -> p t d", p=P)).then_inc(x_in, 16)
                        nc.scalar.dma_start(early_mod[:, 0:NEARLY], a["consts"][:, 0:NEARLY]).then_inc(early_in, 16)
                    if l == 1 and n == 3:
                        act.wait_ge(ROPE_DVE.sem, ROPE_DVE.at(0, "c"))
                        f(sn, rr, ACT.Sin).then_inc(ROPE_ACT.sem, ROPE_ACT.one("sin"))
                        f(cs, rc, ACT.Sin).then_inc(ROPE_ACT.sem, ROPE_ACT.one("cos"))
                        act.wait_ge(ROPE_ACT.sem, ROPE_ACT.at(0, "cos"))
                    if 7 <= n < 7 + TT:
                        square_sum(l, n - 7)
                    for q in range(4):
                        high_part(4 * (SPLIT_ADA1 * l + n) + q)
                first_rstd(l)

            def norm(s):
                for t in range(TT):
                    act.wait_ge(norm_pe.sem, norm_pe.at(s, f"lo{t}"))
                    if s == 0:
                        act.wait_ge(norm_pe.sem, norm_pe.at(s, f"hi{t}"))
                        b = 4 + 2 * (t % 2)
                        ins = f(hT_high[:, :, cols(t)], ps[:, b:b + 2].rearrange("p b (k n) -> p (b k) n", k=4))
                    else:
                        ins = f(hT[:, 0:4, cols(t)], bank(4 + 2 * (t % 2), 4, P))
                    ins.then_inc(norm_act.sem, norm_act.one(f"ev{t}"))

            def norm_tiles(l):
                def put_away(t):
                    act.wait_ge(TN_PE.sem, TN_PE.at(TT * l + t, "lo"))
                    f(hT[:, 0:4, cols(t)], bank(4 + 2 * (t % 2), 4, P)).then_inc(TN_ACT_EV.sem, TN_ACT_EV.one("ev"))

                for t in range(TT):
                    u = TT * l + t
                    act.wait_ge(outp_dve.sem, outp_dve.at(2 * u + 1, "x"))
                    f(junk_wide, x[:, t], ACT.Square, accum_out=ss[:, t:t + 1]).then_inc(TN_ACT.sem, TN_ACT.one("ss"))
                    act.wait_ge(TN_DVE.sem, TN_DVE.at(u, "var"))
                    f(rstd[:, t:t + 1], var[:, t:t + 1], ACT.Ln).then_inc(TN_ACT.sem, TN_ACT.one("ln"))
                    act.wait_ge(TN_ACT.sem, TN_ACT.at(u, "ln"))
                    f(rstd[:, t:t + 1], rstd[:, t:t + 1], ACT.Exp, scale=-0.5).then_inc(TN_ACT.sem, TN_ACT.one("exp"))
                    if t:
                        put_away(t - 1)
                put_away(TT - 1)

            def project_ab():
                q0 = 4 * SPLIT_AB
                high_part(q0)
                high_part(q0 + 1)
                def conv(ct):
                    act.wait_ge(conv_dve.sem, conv_dve.at(ct, "t3"))
                    f(qkvT[:, ct, 3:3 + SEQ], conv_t[:, ct % 2], ACT.Silu).then_inc(conv_act.sem, conv_act.one("silu"))
                    act.wait_ge(conv_act.sem, conv_act.at(ct, "silu"))
                    if 2 <= ct < 10:
                        act.wait_ge(conv_pe.sem, conv_pe.at(ct - 2, "ss"))
                    f(conv_sq[:, ct % 2], qkvT[:, ct, 3:3 + SEQ], ACT.Square).then_inc(conv_act.sem, conv_act.one("sq"))

                for n in range(8):
                    for q in range(4):
                        if 4 * n + q + 2 < 32:
                            high_part(q0 + 4 * n + q + 2)
                        if q == 3:
                            for t in range(TT):
                                j, kind = 4 * n + t, AB_KIND[n]
                                if emptied[j][0] == "s":
                                    act.wait_ge(proj_pe.sem, proj_pe.at(j, "job"))
                                    src = bank(t)
                                    if kind == "qk":
                                        ins = f(pqk[:, t], src)
                                    elif kind == "v":
                                        ins = f(pv[:, t], src)
                                    elif kind == "small":
                                        ins = f(psm[:, t], src[:, 0:24])
                                    elif kind == "za":
                                        ins = f(pz[:, t], src, ACT.Silu)
                                    elif kind == "zb":
                                        ins = f(pzb[:, t], src, ACT.Silu)
                                    else:
                                        ins = f(qkvT[:, j - 12, 3:3 + SEQ], src)
                                    ins.then_inc(proj_act.sem, proj_act.one("ev"))
                        if 0 <= 4 * (n - 4) + q < 12:
                            conv(4 * (n - 4) + q)

            def gla():
                act.wait_ge(GATE_PE.sem, GATE_PE.at(0, "z"))
                f(gate_a, ps[:, 2:4].rearrange("p a b -> p (a b)"), ACT.Abs).then_inc(GATE_ACT.sem, GATE_ACT.one("abs"))
                act.wait_ge(GATE_ACT.sem, GATE_ACT.at(0, "abs"))
                f(gate_e, gate_a, ACT.Exp, scale=-1.0).then_inc(GATE_ACT.sem, GATE_ACT.one("e"))
                act.wait_ge(GATE_ACT.sem, GATE_ACT.at(0, "e"))
                f(gate_e, gate_e, ACT.Ln, bias=1.0).then_inc(GATE_ACT.sem, GATE_ACT.one("l"))
                act.wait_ge(GATE_PE.sem, GATE_PE.at(0, "cums"))
                f(eb_all, ps[:, 4:8, 0:256], ACT.Exp, scale=1.0 / 16).then_inc(GATE_ACT.sem, GATE_ACT.one("eb"))
                f(enb_all, ps[:, 4:8, 0:256], ACT.Exp, scale=-1.0 / 16).then_inc(GATE_ACT.sem, GATE_ACT.one("enb"))
                f(ekb_all, ps[:, 4:8, 256:512], ACT.Exp, scale=1.0 / 16).then_inc(GATE_ACT.sem, GATE_ACT.one("ekb"))
                for t in range(TT):
                    act.wait_ge(GLA_PE.sem, GLA_PE.at(t, "int1"))
                    for hd in range(HEADS):
                        ins = f(gla_sq[:, t, cols(hd)], bank(t)[:, cols(hd)], ACT.Square,
                                accum_out=sm_g[:, 0, HEADS * t + hd:HEADS * t + hd + 1])
                    ins.then_inc(GLN_ACT.sem, GLN_ACT.one(f"ss{t}"))
                act.wait_ge(GLN_DVE.sem, GLN_DVE.at(0, "var"))
                f(sm_g[:, 2], sm_g[:, 1], ACT.Ln).then_inc(GLN_ACT.sem, GLN_ACT.one("ln"))
                act.wait_ge(GLN_ACT.sem, GLN_ACT.at(0, "ln"))
                f(sm_g[:, 2], sm_g[:, 2], ACT.Exp, scale=-0.5).then_inc(GLN_ACT.sem, GLN_ACT.one("exp"))
                for t in range(TT):
                    act.wait_ge(GLN_PE.sem, GLN_PE.at(t, "oT"))
                    f(oT[:, 0:HEADS, cols(t)], bank(4 + t, HEADS, P)).then_inc(GLN_ACT.sem, GLN_ACT.one(f"oT{t}"))

            def gdn_pre():
                act.wait_ge(PRE_DVE.sem, PRE_DVE.at(0, "au"))
                f(pre_l, pre_a, ACT.Exp, scale=-1.0).then_inc(PRE_ACT.sem, PRE_ACT.one("e"))
                act.wait_ge(PRE_ACT.sem, PRE_ACT.at(0, "e"))
                f(pre_l, pre_l, ACT.Ln, bias=1.0).then_inc(PRE_ACT.sem, PRE_ACT.one("l"))
                f(nexpa, a_log, ACT.Exp).then_inc(PRE_ACT.sem, PRE_ACT.one("expa"))
                f(ssk, ssk, ACT.Ln).then_inc(PRE_ACT.sem, PRE_ACT.one("lnss"))
                act.wait_ge(PRE_DVE.sem, PRE_DVE.at(0, "pre"))
                f(pexp, pre, ACT.Exp).then_inc(PRE_ACT.sem, PRE_ACT.one("exp"))

            def gdn_inverses():
                for t in range(TT):
                    act.wait_ge(MAT_DVE.sem, MAT_DVE.at(0, f"d{t}"))
                    f(pm[:, t], pm[:, t], ACT.Exp).then_inc(MAT_ACT.sem, MAT_ACT.one(f"exp{t}"))
                for t in range(TT):
                    act.wait_ge(MAT_PE.sem, MAT_PE.at(0, f"x0{t}"))
                    f(xx[:, t], bank(t, HEADS, P)).then_inc(MAT_ACT.sem, MAT_ACT.one(f"x0{t}"))
                for l in range(1, 6):
                    for t in range(TT):
                        act.wait_ge(INV_PE.sem, INV_PE.at(0, f"p{l}{t}"))
                        if l > 1:
                            act.wait_ge(INV_PE.sem, INV_PE.at(0, f"y{l - 1}{t}"))
                        f(pm[:, t], bank(t, HEADS, P)).then_inc(INV_ACT.sem, INV_ACT.one(f"p{l}{t}"))

            def gdn_prep(t):
                b = t % 2
                act.wait_ge(GDP_DVE.sem, GDP_DVE.at(t, "d"))
                f(ex, ex, ACT.Exp).then_inc(GDP_ACT.sem, GDP_ACT.one("exp"))
                if t >= 2:
                    act.wait_ge(GDN_PE.sem, GDN_PE.at(t - 2, "up1"))
                f(qd_b[:, b], bank(1, HEADS, P), ACT.Exp).then_inc(GDP_ACT.sem, GDP_ACT.one("eq"))

            def gdn_solve(t):
                act.wait_ge(GDP_PE.sem, GDP_PE.at(t, "uw"))
                f(wt_b[:, t % 2], bank(6, HEADS, P)).then_inc(GDP_ACT.sem, GDP_ACT.one("wT"))

            def put_output_b(t):
                act.wait_ge(GDO_PE.sem, GDO_PE.at(t, "oT"))
                f(oT[:, HEADS:2 * HEADS, cols(t)], bank(2, HEADS, P)).then_inc(GDO_ACT.sem, GDO_ACT.one("oT"))

            def gdn(t):
                if t + 1 < TT:
                    gdn_prep(t + 1)
                if t:
                    put_output_b(t - 1)
                if t + 1 < TT:
                    gdn_solve(t + 1)
                act.wait_ge(GDN_PE.sem, GDN_PE.at(t, "o1"))
                for hd in range(HEADS):
                    ins = f(junk[:, cols(hd)], bank(0)[:, cols(hd)], ACT.Square, accum_out=sm_b[:, 0, hd:hd + 1])
                ins.then_inc(GDN_ACT.sem, GDN_ACT.one("ss"))
                act.wait_ge(GDN_DVE.sem, GDN_DVE.at(t, "var"))
                f(sm_b[:, 2], sm_b[:, 1], ACT.Ln).then_inc(GDN_ACT.sem, GDN_ACT.one("ln"))
                act.wait_ge(GDN_ACT.sem, GDN_ACT.at(t, "ln"))
                f(sm_b[:, 2], sm_b[:, 2], ACT.Exp, scale=-0.5).then_inc(GDN_ACT.sem, GDN_ACT.one("rs"))

            def project_swa():
                for jj, (n, t) in enumerate(swa_jobs):
                    j = NJ + jj
                    if emptied[j][0] == "s":
                        act.wait_ge(proj_pe.sem, proj_pe.at(j, "job"))
                        f(swa_dst(n, t), bank(j % 4)).then_inc(proj_act.sem, proj_act.one("ev"))
                    if n == 2:
                        qk_stats(t)
                        if t:
                            put_q(t - 1)
                put_q(TT - 1)

            def qk_stats(t):
                if t:
                    act.wait_ge(QK_DVE.sem, QK_DVE.at(t - 1, "ss"))
                for n in range(3):
                    act.wait_ge(*emptier(NJ + TT * n + t))
                f(sq2[:, 0:QW], pq[:, t], ACT.Square)
                f(sq2[:, QW:1280], pkv[:, t, 0:256], ACT.Square).then_inc(QK_ACT.sem, QK_ACT.one("sq"))
                act.wait_ge(QK_DVE.sem, QK_DVE.at(t, "var"))
                f(qk_s[:, 2, t], qk_s[:, 1, t], ACT.Ln).then_inc(QK_ACT.sem, QK_ACT.one("ln"))
                act.wait_ge(QK_ACT.sem, QK_ACT.at(t, "ln"))
                f(qk_s[:, 2, t], qk_s[:, 2, t], ACT.Exp, scale=-0.5).then_inc(QK_ACT.sem, QK_ACT.one("exp"))

            def put_q(t):
                act.wait_ge(QK_PE.sem, QK_PE.at(t, "q"))
                f(qT[:, :, cols(t)], ps[:, 4:6].rearrange("p b (k n) -> p (b k) n", k=4)).then_inc(QT_ACT.sem, QT_ACT.one("q"))

            def exps(t):
                act.wait_ge(SCO_DVE.sem, SCO_DVE.at(t, "es"))
                w = sw_s[:, t % 2]
                f(w[:, 4], w[:, 3], ACT.Exp).then_inc(SCO_ACT.sem, SCO_ACT.one("es"))
                for hd in range(NQ):
                    p_ = sm[t % 2][:, hd, 64:256]
                    ins = f(p_, p_, ACT.Exp, bias=w[:, 2, hd:hd + 1], accum_out=w[:, 5, hd:hd + 1])
                ins.then_inc(SCO_ACT.sem, SCO_ACT.one("exp"))

            def swa():
                exps(0)
                for t in range(TT):
                    for n in range(8):
                        act.wait_ge(VAL_PE.sem, VAL_PE.at(t, f"t{n}"))
                        if n >= 2:
                            act.wait_ge(VAL_PE.sem, VAL_PE.at(t, f"v{n - 2}"))
                        elif t:
                            act.wait_ge(VAL_PE.sem, VAL_PE.at(t - 1, "v7"))
                        lo = 0 if t else 1
                        f(pT[:, n % 2, :, lo:2], bank(4 + n % 2, 2, 2, P)[:, :, lo:2]).then_inc(VAL_ACT.sem, VAL_ACT.one(f"t{n}"))
                    if t + 1 < TT:
                        exps(t + 1)
                    act.wait_ge(VAL_PE.sem, VAL_PE.at(t, "oT"))
                    f(oT[:, :, cols(t)], ps[:, 4:6].rearrange("p b (k n) -> p (b k) n", k=4)).then_inc(VAL_ACT.sem, VAL_ACT.one("oT"))

            def split_h(l):
                for t in range(TT):
                    act.wait_ge(TN_DVE.sem, TN_DVE.at(TT * l + t, "h"))
                    f(h_high[:, t], h[:, t]).then_inc(split_act.sem, split_act.one(f"hi{t}"))

            def expert_block(st, i, E, c0, chunk_wait):
                S, SA, SV, _ = st

                def high_parts(m, which=(0, 1)):
                    chunk_wait(m)
                    for half in which:
                        act.wait_ge(S.sem, high_free(S, i, m, half, E))
                        f(high_of(2 * m + half), half_of(c0 + m, half)).then_inc(SA.sem, SA.one(f"hi{m}{'ab'[half]}"))

                def gate_silu(e):
                    act.wait_ge(S.sem, S.at(i, f"w{2 * e}b"))
                    if e:
                        act.wait_ge(SV.sem, SV.at(i, f"he{e - 1}"))
                    else:
                        act.wait_ge(SV.sem, SV.at(i - 1, "m7"))
                    f(sg, bank(GATE_BANK), ACT.Silu).then_inc(SA.sem, SA.one(f"sg{e}"))

                def hidden_high(e):
                    act.wait_ge(S.sem, S.at(i, f"hT{e}"))
                    f(heT[:, e, 0], bank(TURN_BANK, 4, P)).then_inc(SA.sem, SA.one(f"hT{e}"))

                def y_high(e):
                    act.wait_ge(S.sem, S.at(i, f"w{2 * E + e}b"))
                    f(ys[:, e, 0], ps[:, Y_BANK[e]:Y_BANK[e] + 2].rearrange("p a b -> p (a b)")
                      ).then_inc(SA.sem, SA.one(f"y{e}"))

                high_parts(0)
                for k in range(KD):
                    act.wait_ge(S.sem, S.at(i, f"hg{k}"))
                    f(hgT[:, k, :, 0:E * P], bank(GATHER_BANKS[k % 4], 2, 256)[:, :, 0:E * P]
                      ).then_inc(SA.sem, SA.one(f"hg{k}"))
                high_parts(1)
                high_parts(2, (0, ))
                gate_silu(0)
                high_parts(2, (1, ))
                if E == 2:
                    high_parts(3)
                    gate_silu(1)
                    high_parts(4, (0, ))
                hidden_high(0)
                if E == 2:
                    high_parts(4, (1, ))
                    high_parts(5, (0, ))
                    hidden_high(1)
                    high_parts(5, (1, ))
                    y_high(0)
                y_high(E - 1)

            def experts(l):
                act.wait_ge(RT_PE.sem, RT_PE.at(l, "logits"))
                f(r_e, bank(0, TT, NE), ACT.Exp, scale=-1.0).then_inc(RT_ACT.sem, RT_ACT.one("exp"))
                split_h(l)
                act.wait_ge(split_dve.sem, split_dve.at(l, "lo3"))
                act.sem_inc(moe_steps[l][1].sem, moe_steps[l][1].n)
                act.sem_inc(over_steps[l][1].sem, over_steps[l][1].n)
                c0 = first[("moe", l)]
                with act.Fori(0, NPAIRS) as i:
                    for g in range(2):
                        cg = c0 + 3 * EG * g

                        def chunk_wait(m):
                            act.wait_ge(chunk_in[(cg + m) % RING], loaded(cg + m) + 16 * (6 * EG // RING) * i)

                        expert_block(moe_steps[l], 2 * i + g, EG, cg, chunk_wait)
                act.wait_ge(RT_DVE.sem, RT_DVE.at(l, "ovl"))
                n_over = act.value_load(ovl_i[0:1, 8:9], min_val=0, max_val=MAXOVER)
                with act.Fori(0, MAXOVER) as j:
                    with act.If(n_over > j):
                        def chunk_wait(m):
                            act.wait_ge(over_in[l], 48 * j + 48)

                        expert_block(over_steps[l], j, 1, 0, chunk_wait)

            nc.scalar.dma_start(const[:], a["consts"][:, NEARLY:NCONST]).then_inc(const_in, 16)
            act.wait_ge(cond_in, 16)
            f(junk_wide[:, 0:KD], cond, ACT.Exp, scale=-1.0).then_inc(cond_act.sem, cond_act.one("exp"))
            ada(0)
            norm(0)
            project_ab()
            nc.scalar.drain().then_inc(phase_done, 1)
            act.wait_ge(phase_done, 3 * 1)
            gla()
            nc.scalar.drain().then_inc(phase_done, 1)
            act.wait_ge(phase_done, 3 * 2)
            gdn_pre()
            gdn_inverses()
            gdn_prep(0)
            gdn_solve(0)
            for t in range(TT):
                gdn(t)
            put_output_b(TT - 1)
            act.drain().then_inc(phase_done, 1)
            act.wait_ge(phase_done, 3 * 3)
            norm_tiles(0)
            nc.scalar.drain().then_inc(phase_done, 1)
            act.wait_ge(phase_done, 3 * 4)
            experts(0)
            nc.scalar.drain().then_inc(phase_done, 1)
            act.wait_ge(phase_done, 3 * 5)
            ada(1)
            norm(1)
            project_swa()
            nc.scalar.drain().then_inc(phase_done, 1)
            act.wait_ge(phase_done, 3 * 6)
            swa()
            nc.scalar.drain().then_inc(phase_done, 1)
            act.wait_ge(phase_done, 3 * 7)
            norm_tiles(1)
            nc.scalar.drain().then_inc(phase_done, 1)
            act.wait_ge(phase_done, 3 * 8)
            experts(1)
            nc.scalar.drain().then_inc(phase_done, 1)

        @block.vector
        def _(dve):
            v = nc.vector

            def newton(st, r, y, vr, t1, last="rstd"):
                v.tensor_tensor(t1, y, y, ALU.mult).then_inc(st.sem, st.one("n1"))
                dve.wait_ge(st.sem, st.at(r, "n1"))
                v.tensor_tensor(t1, t1, vr, ALU.mult).then_inc(st.sem, st.one("n2"))
                dve.wait_ge(st.sem, st.at(r, "n2"))
                v.tensor_scalar(t1, t1, -0.5, 1.5, ALU.mult, ALU.add).then_inc(st.sem, st.one("n3"))
                dve.wait_ge(st.sem, st.at(r, "n3"))
                v.tensor_tensor(y, y, t1, ALU.mult).then_inc(st.sem, st.one(last))
                dve.wait_ge(st.sem, st.at(r, last))

            def ada(l):
                if l == 0:
                    dve.wait_ge(cond_act.sem, cond_act.at(0, "exp"))
                    v.tensor_scalar(junk_wide[:, KD:2 * KD], junk_wide[:, 0:KD], 1.0, None, ALU.add).then_inc(cond_dve.sem, cond_dve.one("e1"))
                    dve.wait_ge(cond_dve.sem, cond_dve.at(0, "e1"))
                    v.reciprocal(junk_wide[:, 2 * KD:3 * KD], junk_wide[:, KD:2 * KD]).then_inc(cond_dve.sem, cond_dve.one("rec"))
                    dve.wait_ge(cond_dve.sem, cond_dve.at(0, "rec"))
                    v.tensor_tensor(cond, cond, junk_wide[:, 2 * KD:3 * KD], ALU.mult).then_inc(cond_dve.sem, cond_dve.one("silu"))
                    dve.wait_ge(cond_dve.sem, cond_dve.at(0, "silu"))
                wide = cond.unsqueeze(2).to_broadcast([P, KD, P])
                v.tensor_copy(cond_high, wide).then_inc(rep_dve.sem, rep_dve.one("high"))
                dve.wait_ge(rep_dve.sem, rep_dve.at(l, "high"))
                v.tensor_tensor(cond_low, wide, cond_high.bitcast(F32), ALU.subtract).then_inc(rep_dve.sem, rep_dve.one("rep"))

                def put_modulation(n):
                    r = 12 * l + n
                    dve.wait_ge(ada_pe.sem, ada_pe.at(r, "mod"))
                    m = mod[:, 512 * n:512 * n + 512]
                    v.tensor_copy(m, bank(n % 4)).then_inc(ada_dve.sem, ada_dve.one("mod"))

                def scale_rows(name, lo, g, n):
                    dve.wait_ge(ada_dve.sem, ada_dve.at(12 * l + n, "mod"))
                    s = mod[:, lo:lo + D]
                    v.scalar_tensor_tensor(out=s, in0=s, scalar=1.0, in1=g, op0=ALU.add, op1=ALU.mult).then_inc(amod_dve.sem, amod_dve.one(name))
                    dve.wait_ge(amod_dve.sem, amod_dve.at(l, name))

                for n in range(12):
                    if l == 1 and n == 3:
                        rope_angles()
                    if n == 7:
                        dve.wait_ge(gains_in[l], 32)
                        scale_rows("a1", D, gain1, 3)
                    if n == 11:
                        variance(l)
                    for q in range(4):
                        low_part(4 * (SPLIT_ADA1 * l + n) + q)
                    if n:
                        put_modulation(n - 1)
                    if n == 11:
                        scale_rows("a2", 4 * D, gain2, 9)
                refine_rstd(l)
                put_modulation(11)
                dve.wait_ge(ada_dve.sem, ada_dve.at(12 * l + 11, "mod"))

            def low_part(qi):
                w, high, low = quarter(qi)
                dve.wait_ge(Q_ACT.sem, Q_ACT.at(qi, "high"))
                v.tensor_tensor(low, w, high.bitcast(F32), ALU.subtract).then_inc(Q_DVE.sem, Q_DVE.one("low"))

            def variance(s):
                dve.wait_ge(norm_act.sem, norm_act.at(s, "ss3"))
                v.tensor_scalar(var[:], ss[:], 1.0 / D, EPS, ALU.mult, ALU.add).then_inc(norm_dve.sem, norm_dve.one("var"))
                dve.wait_ge(norm_dve.sem, norm_dve.at(s, "var"))

            def refine_rstd(s):
                dve.wait_ge(norm_act.sem, norm_act.at(s, "exp"))
                newton(norm_dve, s, rstd[:], var[:], nt1[:])

            def norm(s):
                shift, scale = mod[:, 0:D], mod[:, D:2 * D]
                for t in range(TT):
                    v.scalar_tensor_tensor(out=h[:, t], in0=x[:, t], scalar=rstd[:, t:t + 1], in1=scale,
                                           op0=ALU.mult, op1=ALU.mult).then_inc(norm_dve.sem, norm_dve.one(f"hx{t}"))
                    if t % 2 == 0:
                        dve.wait_ge(norm_dve.sem, norm_dve.at(s, f"hx{t}"))
                        v.tensor_tensor(h[:, t], h[:, t], shift, ALU.add).then_inc(norm_dve.sem, norm_dve.one(f"h{t}"))
                dve.wait_ge(norm_dve.sem, norm_dve.at(s, "hx3"))
                for t in range(TT):
                    if s == 0:
                        dve.wait_ge(norm_act.sem, norm_act.at(s, f"ev{t}"))
                        b = 4 + 2 * (t % 2)
                        ins = v.tensor_tensor(hT_low[:, :, cols(t)], ps[:, b:b + 2].rearrange("p b (k n) -> p (b k) n", k=4),
                                              hT_high[:, :, cols(t)].bitcast(F32), ALU.subtract)
                    else:
                        dve.wait_ge(norm_pe.sem, norm_pe.at(s, f"hi{t}"))
                        ins = v.tensor_copy(hT[:, 4:8, cols(t)], bank(5 + 2 * (t % 2), 4, P))
                    ins.then_inc(norm_dve.sem, norm_dve.one(f"ev{t}"))

            def project_ab():
                dve.wait_ge(norm_pe.sem, norm_pe.at(0, "hi3"))
                v.memset(qkvT[:, :, 0:3], 0.0).then_inc(init_dve, 1)
                dve.wait_ge(init_dve, 1)
                q0 = 4 * SPLIT_AB
                low_part(q0)
                low_part(q0 + 1)
                def conv(ct):
                    dve.wait_ge(*emptier(12 + ct))
                    if ct >= 2:
                        dve.wait_ge(conv_act.sem, conv_act.at(ct - 2, "silu"))
                    acc = conv_t[:, ct % 2]
                    v.tensor_scalar(acc, qkvT[:, ct, 0:SEQ], conv_w[:, ct, 0:1], None, ALU.mult).then_inc(conv_dve.sem, conv_dve.one("t0"))
                    dve.wait_ge(conv_dve.sem, conv_dve.at(ct, "t0"))
                    for k in range(1, 4):
                        v.scalar_tensor_tensor(out=acc, in0=qkvT[:, ct, k:k + SEQ], scalar=conv_w[:, ct, k:k + 1],
                                               in1=acc, op0=ALU.mult, op1=ALU.add).then_inc(conv_dve.sem, conv_dve.one(f"t{k}"))
                        dve.wait_ge(conv_dve.sem, conv_dve.at(ct, f"t{k}"))

                for n in range(8):
                    for q in range(4):
                        if 4 * n + q + 2 < 32:
                            low_part(q0 + 4 * n + q + 2)
                        if q == 3:
                            for t in range(TT):
                                j, kind = 4 * n + t, AB_KIND[n]
                                if emptied[j][0] == "v":
                                    dve.wait_ge(proj_pe.sem, proj_pe.at(j, "job"))
                                    src = bank(t)
                                    dst = {"qk": pqk[:, t], "v": pv[:, t]}.get(kind)
                                    if kind == "small":
                                        dst, src = psm[:, t], src[:, 0:24]
                                    elif kind[0] == "f":
                                        dst = qkvT[:, j - 12, 3:3 + SEQ]
                                    v.tensor_copy(dst, src).then_inc(proj_dve.sem, proj_dve.one("ev"))
                        if 0 <= 4 * (n - 4) + q < 12:
                            conv(4 * (n - 4) + q)
                dve.wait_ge(conv_pe.sem, conv_pe.at(7, "ss"))
                v.tensor_scalar(ssk, bank(5, TT, 8), EPS, None, ALU.add)

            def gla_gates():
                dve.wait_ge(GATE_PE.sem, GATE_PE.at(0, "gaT"))
                v.tensor_copy(gaT[0:RANK, :], bank(0)[0:RANK, :]).then_inc(GATE_DVE.sem, GATE_DVE.one("gaT"))
                dve.wait_ge(GATE_ACT.sem, GATE_ACT.at(0, "l"))
                v.scalar_tensor_tensor(out=gate_g, in0=ps[:, 2:4].rearrange("p a b -> p (a b)"), scalar=0.0, in1=gate_e,
                                       op0=ALU.min, op1=ALU.subtract).then_inc(GATE_DVE.sem, GATE_DVE.one("g"))
                for t in range(TT):
                    ins = v.tensor_tensor(on_g[:, t], pz[:, t].rearrange("p (a b) -> p a b", a=HEADS),
                                          gla_gain.unsqueeze(1).to_broadcast([P, HEADS, P]), ALU.mult)
                ins.then_inc(GATE_DVE.sem, GATE_DVE.one("zg"))

            def gla_qk(t):
                dve.wait_ge(GLP_PE.sem, GLP_PE.at(t, "qkT"))
                if t == 0:
                    dve.wait_ge(GATE_ACT.sem, GATE_ACT.at(0, "ekb"))
                e, ne = (w[:, t].rearrange("p (a b) -> p a b", a=2) for w in (eb_all, enb_all))
                v.scalar_tensor_tensor(out=qd[:, t % 2], in0=bank(6, 4, P)[:, 0:2], scalar=GLA_DK ** -0.5, in1=e,
                                       op0=ALU.mult, op1=ALU.mult).then_inc(GLP_DVE.sem, GLP_DVE.one("qd"))
                for par_ in range(2):
                    r = slice(64 * par_, 64 * par_ + 64)
                    ins = v.tensor_tensor(kz[r, t % 2, par_], bank(6, 4, P)[r, 2:4], ne[r], ALU.mult)
                ins.then_inc(GLP_DVE.sem, GLP_DVE.one("kz"))

            def gla_k_rows(t):
                for c in range(2):
                    r = slice(CHUNK * c, CHUNK * c + CHUNK)
                    ins = v.tensor_tensor(ku[r, t % 2, c], pqk[r, t, 256:512], ekb_all[r, t], ALU.mult)
                ins.then_inc(GLP_DVE.sem, GLP_DVE.one("ku"))

            def gla():
                gla_gates()
                gla_qk(0)
                gla_k_rows(0)
                mask = cst("tri").bitcast(U32).unsqueeze(1).to_broadcast([P, HEADS, P])
                for t in range(TT):
                    dve.wait_ge(GLP_PE.sem, GLP_PE.at(t, "A"))
                    v.copy_predicated(at_g, mask, bank(7, HEADS, P)).then_inc(GLA_DVE.sem, GLA_DVE.one("A"))
                    if t + 1 < TT:
                        gla_qk(t + 1)
                    for c in range(2):
                        dve.wait_ge(GLA_PE.sem, GLA_PE.at(t, f"int{c}"))
                        for hd in range(HEADS):
                            f, r = hd // 2, slice(64 * (hd % 2), 64 * (hd % 2) + 64)
                            s = st_g[r, f, cols(hd % 2)]
                            ins = v.scalar_tensor_tensor(out=s, in0=s, scalar=eb_all[r, t, P * f + 64 * c + 63:P * f + 64 * c + 64],
                                                         in1=bank(4 + c)[r, 256 * f + P * (hd % 2):256 * f + P * (hd % 2) + P],
                                                         op0=ALU.mult, op1=ALU.add)
                        ins.then_inc(GLA_DVE.sem, GLA_DVE.one(f"s{c}"))
                        if c == 0 and t + 1 < TT:
                            gla_k_rows(t + 1)
                        dve.wait_ge(GLA_DVE.sem, GLA_DVE.at(t, f"s{c}"))
                dve.wait_ge(GLN_ACT.sem, GLN_ACT.at(0, "ss3"))
                v.tensor_scalar(sm_g[:, 1], sm_g[:, 0], 1.0 / DV, EPS, ALU.mult, ALU.add).then_inc(GLN_DVE.sem, GLN_DVE.one("var"))
                dve.wait_ge(GLN_ACT.sem, GLN_ACT.at(0, "exp"))
                dve.wait_ge(GLN_DVE.sem, GLN_DVE.at(0, "var"))
                newton(GLN_DVE, 0, sm_g[:, 2], sm_g[:, 1], sm_g[:, 3])
                for t in range(TT):
                    for hd in range(HEADS):
                        n = HEADS * t + hd
                        ins = v.scalar_tensor_tensor(out=on_g[:, t, hd], in0=bank(t)[:, cols(hd)], scalar=sm_g[:, 2, n:n + 1],
                                                     in1=on_g[:, t, hd], op0=ALU.mult, op1=ALU.mult)
                    ins.then_inc(GLN_DVE.sem, GLN_DVE.one(f"on{t}"))

            def head_norm(st, st_act, t, sm, o, zg, on, exp_name):
                dve.wait_ge(st_act.sem, st_act.at(t, "ss"))
                v.tensor_scalar(sm[:, 1], sm[:, 0], 1.0 / DV, EPS, ALU.mult, ALU.add).then_inc(st.sem, st.one("var"))
                dve.wait_ge(st_act.sem, st_act.at(t, exp_name))
                dve.wait_ge(st.sem, st.at(t, "var"))
                newton(st, t, sm[:, 2], sm[:, 1], sm[:, 3])
                for hd in range(HEADS):
                    ins = v.scalar_tensor_tensor(out=on[:, hd], in0=o[:, cols(hd)], scalar=sm[:, 2, hd:hd + 1],
                                                 in1=zg[:, hd], op0=ALU.mult, op1=ALU.mult)
                ins.then_inc(st.sem, st.one("on"))

            def gdn_pre():
                D_ = PRE_DVE
                v.tensor_tensor(pre_u[:, :, 0:4], psm[:, :, 16:20], dt_bias.unsqueeze(1).to_broadcast([P, TT, HEADS]), ALU.add)
                v.tensor_copy(pre_u[:, :, 4:8], psm[:, :, 20:24]).then_inc(D_.sem, D_.one("u"))
                dve.wait_ge(D_.sem, D_.at(0, "u"))
                v.scalar_tensor_tensor(out=pre_a, in0=pre_u, scalar=-1.0, in1=pre_u, op0=ALU.mult, op1=ALU.max).then_inc(D_.sem, D_.one("au"))
                dve.wait_ge(PRE_ACT.sem, PRE_ACT.at(0, "expa"))
                v.scalar_tensor_tensor(out=pre_a[:, :, 0:4], in0=pre_u[:, :, 0:4], scalar=0.0, in1=pre_l[:, :, 0:4],
                                                       op0=ALU.max, op1=ALU.add).then_inc(D_.sem, D_.one("mx"))
                dve.wait_ge(D_.sem, D_.at(0, "mx"))
                v.scalar_tensor_tensor(out=g_b, in0=pre_a[:, :, 0:4], scalar=-1.0,
                                               in1=nexpa.unsqueeze(1).to_broadcast([P, TT, HEADS]), op0=ALU.mult, op1=ALU.mult).then_inc(D_.sem, D_.one("g"))
                v.scalar_tensor_tensor(out=lnb, in0=pre_u[:, :, 4:8], scalar=0.0, in1=pre_l[:, :, 4:8],
                                               op0=ALU.min, op1=ALU.subtract).then_inc(D_.sem, D_.one("lnb"))
                dve.wait_ge(PRE_ACT.sem, PRE_ACT.at(0, "lnss"))
                v.tensor_scalar(lk, ssk[:, :, 4:8], -0.5, None, ALU.mult).then_inc(D_.sem, D_.one("lk"))
                v.tensor_scalar(lq, ssk[:, :, 0:4], -0.5, float(-0.5 * np.log(DV)), ALU.mult, ALU.add).then_inc(D_.sem, D_.one("lq"))
                dve.wait_ge(D_.sem, D_.at(0, "lq"))
                v.tensor_tensor(lbk, lnb, lk, ALU.add).then_inc(D_.sem, D_.one("lbk"))
                dve.wait_ge(D_.sem, D_.at(0, "lbk"))
                dve.wait_ge(PRE_PE.sem, PRE_PE.at(0, "cum"))
                cum = bank(4)[:, 0:64].rearrange("p (n t h) -> p n t h", n=4, t=TT)
                v.tensor_copy(pre[:, 0], lnb)
                v.tensor_tensor(pre[:, 1], cum[:, 0], lbk, ALU.add)
                v.tensor_tensor(pre[:, 2], cum[:, 1], lk, ALU.add)
                v.tensor_copy(pre[:, 3:5], cum[:, 2:4]).then_inc(D_.sem, D_.one("pre"))
                v.tensor_tensor(colj, lk, cum[:, 0], ALU.subtract).then_inc(D_.sem, D_.one("colj"))
                dve.wait_ge(D_.sem, D_.at(0, "colj"))
                dve.wait_ge(PRE_ACT.sem, PRE_ACT.at(0, "exp"))

            def level(l):
                return cst("lev", P * l, P).unsqueeze(1).to_broadcast([P, HEADS, P])

            def gdn_inverses():
                for t in range(TT):
                    v.tensor_copy(xx[:, t], g_b[:, t].unsqueeze(2).to_broadcast([P, HEADS, P]))
                    v.tensor_copy(xt[:, t], lbk[:, t].unsqueeze(2).to_broadcast([P, HEADS, P])).then_inc(MAT_DVE.sem, MAT_DVE.one(f"rep{t}"))
                for t in range(TT):
                    dve.wait_ge(MAT_PE.sem, MAT_PE.at(0, f"rows{t}"))
                    for hd in range(HEADS):
                        ins = v.scalar_tensor_tensor(out=pm[:, t, hd], in0=bank(t)[:, cols(hd)], scalar=colj[:, t, hd:hd + 1],
                                                     in1=cst("strict_bias"), op0=ALU.add, op1=ALU.add)
                    ins.then_inc(MAT_DVE.sem, MAT_DVE.one(f"d{t}"))
                for t in range(TT):
                    dve.wait_ge(MAT_PE.sem, MAT_PE.at(0, f"kk{t}"))
                    dve.wait_ge(MAT_ACT.sem, MAT_ACT.at(0, f"exp{t}"))
                    v.tensor_tensor(at[:, t], bank(4 + t, HEADS, P), pm[:, t], ALU.mult).then_inc(MAT_DVE.sem, MAT_DVE.one(f"at{t}"))
                for t in range(TT):
                    dve.wait_ge(MAT_DVE.sem, MAT_DVE.at(0, f"at{t}"))
                    v.tensor_tensor(lev_at[:, t], at[:, t], level(0), ALU.mult).then_inc(MAT_DVE.sem, MAT_DVE.one(f"level0{t}"))
                for t in range(TT):
                    dve.wait_ge(MAT_DVE.sem, MAT_DVE.at(0, f"level0{t}"))
                    v.tensor_tensor(xt[:, t], ident.unsqueeze(1).to_broadcast([P, HEADS, P]), lev_at[:, t], ALU.subtract
                                    ).then_inc(MAT_DVE.sem, MAT_DVE.one(f"xt0{t}"))
                for t in range(TT):
                    dve.wait_ge(MAT_DVE.sem, MAT_DVE.at(0, f"xt0{t}"))
                    v.tensor_tensor(lev_at[:, t], at[:, t], level(1), ALU.mult).then_inc(MAT_DVE.sem, MAT_DVE.one(f"level1{t}"))
                dve.wait_ge(MAT_DVE.sem, MAT_DVE.at(0, f"level1{TT - 1}"))
                for l in range(1, 6):
                    for t in range(TT):
                        dve.wait_ge(INV_PE.sem, INV_PE.at(0, f"y{l}{t}"))
                        if l > 1:
                            dve.wait_ge(INV_DVE.sem, INV_DVE.at(0, f"x{l - 1}{t}"))
                        v.tensor_tensor(xt[:, t], xt[:, t], bank(4 + t, HEADS, P), ALU.subtract).then_inc(INV_DVE.sem, INV_DVE.one(f"xt{l}{t}"))
                        if l < 5:
                            v.tensor_tensor(xx[:, t], xx[:, t], bank(t, HEADS, P), ALU.subtract).then_inc(INV_DVE.sem, INV_DVE.one(f"x{l}{t}"))
                            v.tensor_tensor(lev_at[:, t], at[:, t], level(l + 1), ALU.mult).then_inc(INV_DVE.sem, INV_DVE.one(f"level{l}{t}"))

            def gdn_prep_decays(t):
                S, b = GDP_DVE, t % 2
                dve.wait_ge(GDP_PE.sem, GDP_PE.at(t, "rows"))
                for hd in range(HEADS):
                    ins = v.scalar_tensor_tensor(out=ex[:, hd], in0=bank(1)[:, cols(hd)], scalar=colj[:, t, hd:hd + 1],
                                                 in1=cst("incl_bias"), op0=ALU.add, op1=ALU.add)
                ins.then_inc(S.sem, S.one("d"))

            def gdn_prep_products(t):
                S, b = GDP_DVE, t % 2
                if t >= 2:
                    dve.wait_ge(GDN_PE.sem, GDN_PE.at(t - 2, "up1"))
                dve.wait_ge(GDP_PE.sem, GDP_PE.at(t, "kq"))
                dve.wait_ge(GDP_ACT.sem, GDP_ACT.at(t, "exp"))
                v.tensor_tensor(qkt[:, b], bank(3, HEADS, P), ex, ALU.mult).then_inc(S.sem, S.one("qk"))
                dve.wait_ge(GDP_ACT.sem, GDP_ACT.at(t, "eq"))
                v.tensor_tensor(qd_b[:, b], qkvT[:, 0:4, 3 + P * t:3 + P * t + P], qd_b[:, b], ALU.mult).then_inc(S.sem, S.one("qd"))
                dve.wait_ge(GDP_PE.sem, GDP_PE.at(t, "kv"))
                for c in range(2):
                    r = slice(CHUNK * c, CHUNK * c + CHUNK)
                    ins = v.tensor_tensor(ku_b[r, b, c], bank(6, HEADS, P)[r], by_token(2, t, r), ALU.mult)
                ins.then_inc(S.sem, S.one("ku"))

            def by_token(n, t, r=slice(0, P)):
                return pexp[r, n, t].unsqueeze(2).to_broadcast([r.stop - r.start, HEADS, P])

            def gdn_prep_solve(t):
                S = GDP_DVE
                v.tensor_tensor(kb_b, bank(6, HEADS, P), by_token(1, t), ALU.mult).then_inc(S.sem, S.one("kb"))
                v.tensor_tensor(vb_b, bank(7, HEADS, P), by_token(0, t), ALU.mult).then_inc(S.sem, S.one("vb"))

            def gdn_rep(t):
                for n, src in enumerate((g_b, lq)):
                    ins = v.tensor_copy(rep[:, n], src[:, t].unsqueeze(2).to_broadcast([P, HEADS, P]))
                ins.then_inc(GDP_DVE.sem, GDP_DVE.one("rep"))

            def gdn_u(t):
                dve.wait_ge(GDP_PE.sem, GDP_PE.at(t, "uw"))
                v.tensor_copy(u_b[:, t % 2], bank(3, HEADS, P)).then_inc(GDP_DVE.sem, GDP_DVE.one("u"))

            def gdn(t):
                S, b, ahead = GDN_DVE, t % 2, t + 1 < TT
                dve.wait_ge(GDP_DVE.sem, GDP_DVE.at(t, "u"))
                for c in range(2):
                    r = slice(CHUNK * c, CHUNK * c + CHUNK)
                    dve.wait_ge(GDN_PE.sem, GDN_PE.at(t, f"ws{c}"))
                    v.tensor_tensor(vn[r], u_b[r, b], bank(4, HEADS, P)[r], ALU.subtract).then_inc(S.sem, S.one(f"vn{c}"))
                    if ahead:
                        if c == 0:
                            gdn_prep_decays(t + 1)
                        else:
                            gdn_prep_solve(t + 1)
                    dve.wait_ge(GDN_PE.sem, GDN_PE.at(t, f"up{c}"))
                    for hd in range(HEADS):
                        ins = v.scalar_tensor_tensor(out=st_b[:, hd], in0=st_b[:, hd], scalar=pexp[:, 3 + c, t, hd:hd + 1],
                                                     in1=bank(5)[:, cols(hd)], op0=ALU.mult, op1=ALU.add)
                    ins.then_inc(S.sem, S.one(f"s{c}"))
                    dve.wait_ge(S.sem, S.at(t, f"s{c}"))
                    if ahead and c == 0:
                        gdn_prep_products(t + 1)
                if ahead:
                    gdn_u(t + 1)
                if t + 2 < TT:
                    gdn_rep(t + 2)
                v.tensor_tensor(zg_b, pzb[:, t].rearrange("p (a b) -> p a b", a=HEADS),
                                gdn_gain.unsqueeze(1).to_broadcast([P, HEADS, P]), ALU.mult).then_inc(S.sem, S.one("zg"))
                dve.wait_ge(S.sem, S.at(t, "zg"))
                if t:
                    dve.wait_ge(GDO_PE.sem, GDO_PE.at(t - 1, "oT"))
                head_norm(S, GDN_ACT, t, sm_b, bank(0), zg_b, on_b, "rs")

            def norm_tile(l, t):
                u = TT * l + t
                shift, scale = mod[:, 3 * D:4 * D], mod[:, 4 * D:5 * D]
                c = slice(t, t + 1)
                dve.wait_ge(TN_ACT.sem, TN_ACT.at(u, "ss"))
                v.tensor_scalar(var[:, c], ss[:, c], 1.0 / D, EPS, ALU.mult, ALU.add).then_inc(TN_DVE.sem, TN_DVE.one("var"))
                dve.wait_ge(TN_DVE.sem, TN_DVE.at(u, "var"))
                dve.wait_ge(TN_ACT.sem, TN_ACT.at(u, "exp"))
                newton(TN_DVE, u, rstd[:, c], var[:, c], nt1[:, c])
                v.scalar_tensor_tensor(out=h[:, t], in0=x[:, t], scalar=rstd[:, c], in1=scale,
                                       op0=ALU.mult, op1=ALU.mult).then_inc(TN_DVE.sem, TN_DVE.one("hx"))
                dve.wait_ge(TN_DVE.sem, TN_DVE.at(u, "hx"))
                v.tensor_tensor(h[:, t], h[:, t], shift, ALU.add).then_inc(TN_DVE.sem, TN_DVE.one("h"))

            def put_away(l, t):
                dve.wait_ge(TN_PE.sem, TN_PE.at(TT * l + t, "hi"))
                v.tensor_copy(hT[:, 4:8, cols(t)], bank(5 + 2 * (t % 2), 4, P)).then_inc(TN_DVE_EV.sem, TN_DVE_EV.one("ev"))

            def project_out(l):
                if l == 0:
                    dve.wait_ge(x_again, 16)
                for t in range(TT):
                    for n in range(2):
                        g = mod[:, 2 * D + 512 * n:2 * D + 512 * n + 512]
                        j = 8 * l + 2 * t + n
                        dve.wait_ge(outp_pe.sem, outp_pe.at(j, "job"))
                        v.tensor_tensor(res_tmp, bank(j % 4), g, ALU.mult).then_inc(outp_dve.sem, outp_dve.one("tmp"))
                        dve.wait_ge(outp_dve.sem, outp_dve.at(j, "tmp"))
                        xs = x[:, t, 512 * n:512 * n + 512]
                        v.tensor_tensor(xs, xs, res_tmp, ALU.add).then_inc(outp_dve.sem, outp_dve.one("x"))
                        dve.wait_ge(outp_dve.sem, outp_dve.at(j, "x"))
                    norm_tile(l, t)
                    if t:
                        put_away(l, t - 1)
                put_away(l, TT - 1)

            def project_swa():
                v.memset(kTz, 0.0).then_inc(init_dve, 1)
                dve.wait_ge(init_dve, 5)
                for jj, (n, t) in enumerate(swa_jobs):
                    j = NJ + jj
                    if emptied[j][0] == "v":
                        dve.wait_ge(proj_pe.sem, proj_pe.at(j, "job"))
                        v.tensor_copy(swa_dst(n, t), bank(j % 4)).then_inc(proj_dve.sem, proj_dve.one("ev"))
                    if n == 2:
                        qk_heads(t)
                        if t:
                            put_k(t - 1)
                put_k(TT - 1)

            def rope_angles():
                R = ROPE_DVE


                def turns(out, k, part, base):
                    return v.scalar_tensor_tensor(out=out, in0=k, scalar=-part, in1=base, op0=ALU.mult, op1=ALU.add)

                v.tensor_copy(posf, pos_i[:]).then_inc(R.sem, R.one("pos"))
                dve.wait_ge(R.sem, R.at(0, "pos"))
                v.tensor_tensor(rang, posf.unsqueeze(2).to_broadcast([P, TT, 32]),
                                   cst("inv_freq").unsqueeze(1).to_broadcast([P, TT, 32]), ALU.mult).then_inc(R.sem, R.one("ang"))
                dve.wait_ge(R.sem, R.at(0, "ang"))
                v.tensor_scalar(rk, rang, float(1 / (2 * np.pi)), ROUND, ALU.mult, ALU.add).then_inc(R.sem, R.one("k1"))
                dve.wait_ge(R.sem, R.at(0, "k1"))
                v.tensor_scalar(rk, rk, ROUND, None, ALU.subtract).then_inc(R.sem, R.one("k2"))
                dve.wait_ge(R.sem, R.at(0, "k2"))
                turns(rr, rk, TURN[0], rang).then_inc(R.sem, R.one("r1"))
                dve.wait_ge(R.sem, R.at(0, "r1"))
                turns(rr, rk, TURN[1], rr).then_inc(R.sem, R.one("r2"))
                dve.wait_ge(R.sem, R.at(0, "r2"))
                turns(rr, rk, TURN[2], rr).then_inc(R.sem, R.one("r3"))
                dve.wait_ge(R.sem, R.at(0, "r3"))
                v.tensor_scalar(rr, rr, PI_BELOW, -PI_BELOW, ALU.min, ALU.max).then_inc(R.sem, R.one("r"))
                dve.wait_ge(R.sem, R.at(0, "r"))
                v.tensor_scalar(rc, rr, float(np.pi / 2), None, ALU.add).then_inc(R.sem, R.one("c1"))
                dve.wait_ge(R.sem, R.at(0, "c1"))
                v.tensor_scalar(rk, rc, PI_BELOW, -float(2 * np.pi), ALU.is_gt, ALU.mult).then_inc(R.sem, R.one("c2"))
                dve.wait_ge(R.sem, R.at(0, "c2"))
                v.tensor_tensor(rc, rc, rk, ALU.add).then_inc(R.sem, R.one("c3"))
                dve.wait_ge(R.sem, R.at(0, "c3"))
                v.tensor_scalar(rc, rc, PI_BELOW, -PI_BELOW, ALU.min, ALU.max).then_inc(R.sem, R.one("c"))
                dve.wait_ge(R.sem, R.at(0, "c"))

            def qk_heads(t):
                Q = QK_DVE

                def multiply(out, in0, in1):
                    return v.tensor_tensor(out, in0, in1, ALU.mult)

                dve.wait_ge(QK_ACT.sem, QK_ACT.at(t, "sq"))
                v.tensor_reduce(qk_s[:, 0, t], sq2.rearrange("p (a b) -> p a b", a=20), AX.X, ALU.add).then_inc(Q.sem, Q.one("ss"))
                dve.wait_ge(Q.sem, Q.at(t, "ss"))
                v.tensor_scalar(qk_s[:, 1, t], qk_s[:, 0, t], 1.0 / HD, EPS, ALU.mult, ALU.add).then_inc(Q.sem, Q.one("var"))
                dve.wait_ge(Q.sem, Q.at(t, "var"))
                dve.wait_ge(QK_ACT.sem, QK_ACT.at(t, "exp"))
                newton(Q, t, qk_s[:, 2, t], qk_s[:, 1, t], qk_s[:, 3, t])
                for xh, at_ in head_parts(t):
                    ins = v.tensor_tensor(xh, xh, qk_s[:, 2, t, at_].unsqueeze(2).to_broadcast([P, at_.stop - at_.start, HD]), ALU.mult)
                ins.then_inc(Q.sem, Q.one("a"))
                dve.wait_ge(Q.sem, Q.at(t, "a"))
                for (xh, at_), gain in zip(head_parts(t), (q_gain, k_gain)):
                    ins = v.tensor_tensor(xh, xh, gain.unsqueeze(1).to_broadcast([P, at_.stop - at_.start, HD]), ALU.mult)
                ins.then_inc(Q.sem, Q.one("b"))
                dve.wait_ge(Q.sem, Q.at(t, "b"))
                dve.wait_ge(ROPE_ACT.sem, ROPE_ACT.at(0, "cos"))
                rotations(multiply, t, (0, 1)).then_inc(Q.sem, Q.one("c"))
                dve.wait_ge(Q.sem, Q.at(t, "c"))
                dve.wait_ge(QK_POOL.sem, QK_POOL.at(t, "c"))
                for xh, at_ in head_parts(t):
                    v.tensor_tensor(xh[:, :, 0:32], rope_t[0][:, at_], rope_t[1][:, at_], ALU.subtract)
                    ins = v.tensor_tensor(xh[:, :, 32:64], rope_t[2][:, at_], rope_t[3][:, at_], ALU.add)
                ins.then_inc(Q.sem, Q.one("rope"))

            def put_k(t):
                dve.wait_ge(QK_PE.sem, QK_PE.at(t, "k"))
                for kv in range(NKV):
                    src = bank(6)[64 * (kv % 2):64 * (kv % 2) + 64, cols(kv // 2)]
                    for p_ in range(2):
                        ins = v.tensor_copy(kTz[64 * p_:64 * p_ + 64, kv, p_, CHUNK + P * t:CHUNK + P * t + P], src)
                ins.then_inc(QT_DVE.sem, QT_DVE.one("k"))

            def weigh(t):
                W, w = SCO_DVE, sw_s[:, t % 2]
                if t >= 2:
                    dve.wait_ge(VAL_PE.sem, VAL_PE.at(t - 2, "t7"))
                bias = cst("swa_bias", 192 if t else 0, 192).unsqueeze(1).to_broadcast([P, 2, 192])
                for n in range(8):
                    dve.wait_ge(SCO_PE.sem, SCO_PE.at(t, f"s{n}"))
                    v.scalar_tensor_tensor(out=sm[t % 2][:, 2 * n:2 * n + 2, 64:256], in0=bank(n % 4)[:, 0:384].rearrange("p (a b) -> p a b", a=2),
                                           scalar=HD ** -0.5, in1=bias, op0=ALU.mult, op1=ALU.add).then_inc(W.sem, W.one(f"s{n}"))
                dve.wait_ge(W.sem, W.at(t, "s7"))
                v.tensor_reduce(w[:, 0], sm[t % 2][:, :, 64:256], AX.X, ALU.max).then_inc(W.sem, W.one("max"))
                dve.wait_ge(W.sem, W.at(t, "max"))
                v.tensor_tensor(w[:, 1], w[:, 0], sink, ALU.max).then_inc(W.sem, W.one("m"))
                dve.wait_ge(W.sem, W.at(t, "m"))
                v.tensor_scalar(w[:, 2], w[:, 1], -1.0, None, ALU.mult).then_inc(W.sem, W.one("nm"))
                v.tensor_tensor(w[:, 3], sink, w[:, 1], ALU.subtract).then_inc(W.sem, W.one("es"))

            def swa():
                dve.wait_ge(QK_PE.sem, QK_PE.at(TT - 1, "q"))
                for b in range(2):
                    ins = v.memset(sm[b][:, :, 0:64], 0.0)
                ins.then_inc(init_dve, 1)
                dve.wait_ge(init_dve, 6)
                weigh(0)
                for t in range(TT):
                    if t + 1 < TT:
                        weigh(t + 1)
                    V, w = VAL_DVE, sw_s[:, t % 2]
                    dve.wait_ge(SCO_ACT.sem, SCO_ACT.at(t, "exp"))
                    v.tensor_tensor(w[:, 5], w[:, 5], w[:, 4], ALU.add).then_inc(V.sem, V.one("den"))
                    dve.wait_ge(V.sem, V.at(t, "den"))
                    v.reciprocal(w[:, 5], w[:, 5]).then_inc(V.sem, V.one("rec"))
                    dve.wait_ge(V.sem, V.at(t, "rec"))
                    dve.wait_ge(VAL_PE.sem, VAL_PE.at(t, "v7"))
                    if t:
                        dve.wait_ge(VAL_PE.sem, VAL_PE.at(t - 1, "oT"))
                    v.tensor_tensor(o_sb, ps[:, 6:8].rearrange("p b (a d) -> p (b a) d", d=HD), w[:, 5].unsqueeze(2).to_broadcast([P, NQ, HD]),
                                    ALU.mult).then_inc(V.sem, V.one("o"))

            def router(l):
                R = RT_DVE


                def e4(w):
                    return w.rearrange("p t (g e) -> p t g e", g=NGRP)

                def over(w, n):
                    return w.unsqueeze(2).to_broadcast([P, TT, n])

                def first_of_max(src, n, names, mask):
                    mx, eqn, wn, mwn, mn = names
                    tmp = r_b[:, :, 0:n]
                    v.tensor_reduce(r_t, src, AX.X, ALU.max).then_inc(R.sem, R.one(mx))
                    dve.wait_ge(R.sem, R.at(l, mx))
                    v.tensor_tensor(tmp, src, over(r_t, n), ALU.is_equal).then_inc(R.sem, R.one(eqn))
                    dve.wait_ge(R.sem, R.at(l, eqn))
                    v.tensor_tensor(tmp, tmp, cst("desc16", 0, n).unsqueeze(1).to_broadcast([P, TT, n]), ALU.mult).then_inc(R.sem, R.one(wn))
                    dve.wait_ge(R.sem, R.at(l, wn))
                    v.tensor_reduce(r_u, tmp, AX.X, ALU.max).then_inc(R.sem, R.one(mwn))
                    dve.wait_ge(R.sem, R.at(l, mwn))
                    v.tensor_tensor(mask, tmp, over(r_u, n), ALU.is_equal).then_inc(R.sem, R.one(mn))
                    dve.wait_ge(R.sem, R.at(l, mn))

                dve.wait_ge(RT_ACT.sem, RT_ACT.at(l, "exp"))
                v.memset(posm, 0.0)
                v.memset(wgt, 0.0)
                v.tensor_scalar(r_e, r_e, 1.0, None, ALU.add).then_inc(R.sem, R.one("e1"))
                dve.wait_ge(R.sem, R.at(l, "e1"))
                v.reciprocal(r_sc, r_e).then_inc(R.sem, R.one("sc"))
                dve.wait_ge(R.sem, R.at(l, "sc"))
                v.tensor_tensor(r_sel, r_sc, router_b.unsqueeze(1).to_broadcast([P, TT, NE]), ALU.add).then_inc(R.sem, R.one("sel"))
                dve.wait_ge(R.sem, R.at(l, "sel"))
                s4 = e4(r_sel)
                g0, g1, g2, g3, g4, g5, gm, go_ = r_g
                v.tensor_tensor(g0, s4[:, :, :, 0], s4[:, :, :, 1], ALU.max)
                v.tensor_tensor(g1, s4[:, :, :, 0], s4[:, :, :, 1], ALU.min)
                v.tensor_tensor(g2, s4[:, :, :, 2], s4[:, :, :, 3], ALU.max)
                v.tensor_tensor(g3, s4[:, :, :, 2], s4[:, :, :, 3], ALU.min).then_inc(R.sem, R.one("pairs"))
                dve.wait_ge(R.sem, R.at(l, "pairs"))
                v.tensor_tensor(g4, g0, g2, ALU.max).then_inc(R.sem, R.one("top"))
                dve.wait_ge(R.sem, R.at(l, "top"))
                v.tensor_tensor(g5, g0, g2, ALU.min)
                v.tensor_tensor(gm, g1, g3, ALU.max).then_inc(R.sem, R.one("low"))
                dve.wait_ge(R.sem, R.at(l, "low"))
                v.tensor_tensor(g5, g5, gm, ALU.max).then_inc(R.sem, R.one("second"))
                dve.wait_ge(R.sem, R.at(l, "second"))
                v.tensor_tensor(g4, g4, g5, ALU.add).then_inc(R.sem, R.one("gs"))
                dve.wait_ge(R.sem, R.at(l, "gs"))
                first_of_max(g4, NGRP, ("gmax", "geq", "gw", "gmw", "gmask"), gm)
                v.tensor_scalar(go_, gm, -1.0, -NEG, ALU.add, ALU.mult).then_inc(R.sem, R.one("goff"))
                dve.wait_ge(R.sem, R.at(l, "goff"))
                v.tensor_tensor(e4(r_a), s4, go_.unsqueeze(3).to_broadcast([P, TT, NGRP, 4]), ALU.add).then_inc(R.sem, R.one("selm"))
                dve.wait_ge(R.sem, R.at(l, "selm"))
                first_of_max(r_a, NE, ("max1", "eq1", "w1", "mw1", "mk1"), mk1)
                v.scalar_tensor_tensor(out=r_a, in0=mk1, scalar=3 * NEG, in1=r_a, op0=ALU.mult, op1=ALU.add).then_inc(R.sem, R.one("selm2"))
                dve.wait_ge(R.sem, R.at(l, "selm2"))
                first_of_max(r_a, NE, ("max2", "eq2", "w2", "mw2", "mk2"), mk)
                v.tensor_tensor(mk, mk, mk1, ALU.add).then_inc(R.sem, R.one("mk"))
                dve.wait_ge(R.sem, R.at(l, "mk"))
                v.tensor_tensor(r_a, r_sc, mk, ALU.mult).then_inc(R.sem, R.one("wr"))
                dve.wait_ge(R.sem, R.at(l, "wr"))
                v.tensor_reduce(r_t, r_a, AX.X, ALU.add).then_inc(R.sem, R.one("wsum"))
                dve.wait_ge(R.sem, R.at(l, "wsum"))
                v.reciprocal(r_u, r_t).then_inc(R.sem, R.one("wrec"))
                dve.wait_ge(R.sem, R.at(l, "wrec"))
                v.tensor_tensor(wgt[:, :, 0:NE], r_a, over(r_u, NE), ALU.mult).then_inc(R.sem, R.one("wgt"))
                dve.wait_ge(R.sem, R.at(l, "wgt"))
                v.tensor_scalar(r_a, mk, -1e4, 1e4, ALU.mult, ALU.add).then_inc(R.sem, R.one("off"))
                dve.wait_ge(R.sem, R.at(l, "off"))
                dve.wait_ge(RT_PE.sem, RT_PE.at(l, "pos"))
                v.tensor_tensor(posm[:, :, 0:NE], bank(1, TT, NE), r_a, ALU.add).then_inc(R.sem, R.one("posm"))
                dve.wait_ge(R.sem, R.at(l, "posm"))
                for s_ in range(3):
                    ins = v.tensor_scalar(fl[:, s_], bank(1)[:, 64:64 + NE], float(SLOTS * (s_ + 1)), None, ALU.is_gt)
                ins.then_inc(R.sem, R.one("fl"))
                dve.wait_ge(R.sem, R.at(l, "fl"))
                flf, keyf = (w.rearrange("p s e -> p (s e)") for w in (fl, key))
                v.tensor_tensor(keyf, flf, cst("desc48"), ALU.mult).then_inc(R.sem, R.one("key"))
                dve.wait_ge(R.sem, R.at(l, "key"))
                v.max(top8, keyf).then_inc(R.sem, R.one("top8"))
                dve.wait_ge(R.sem, R.at(l, "top8"))
                v.tensor_reduce(nov, flf, AX.X, ALU.add).then_inc(R.sem, R.one("nov"))
                dve.wait_ge(R.sem, R.at(l, "nov"))
                v.tensor_scalar(ent, top8, -1.0, DESC_TOP, ALU.mult, ALU.add).then_inc(R.sem, R.one("ent"))
                dve.wait_ge(R.sem, R.at(l, "ent"))
                v.tensor_copy(ovl_i[:, 16:24], ent).then_inc(R.sem, R.one("enti"))
                dve.wait_ge(R.sem, R.at(l, "enti"))
                v.tensor_scalar(ovl_i[:, 24:32], ovl_i[:, 16:24], 4, None, ALU.logical_shift_right).then_inc(R.sem, R.one("sh"))
                dve.wait_ge(R.sem, R.at(l, "sh"))
                v.tensor_scalar(ovl_i[:, 0:8], ovl_i[:, 16:24], 15, None, ALU.bitwise_and).then_inc(R.sem, R.one("ei"))
                dve.wait_ge(R.sem, R.at(l, "ei"))
                v.tensor_copy(basef, ovl_i[:, 24:32]).then_inc(R.sem, R.one("base"))
                dve.wait_ge(R.sem, R.at(l, "base"))
                v.tensor_copy(ovl_i[:, 8:9], nov).then_inc(R.sem, R.one("ovl"))
                dve.wait_ge(R.sem, R.at(l, "ovl"))

            def split_h(l):
                for t in range(TT):
                    dve.wait_ge(split_act.sem, split_act.at(l, f"hi{t}"))
                    v.tensor_tensor(h_low[:, t], h[:, t], h_high[:, t].bitcast(F32), ALU.subtract).then_inc(split_dve.sem, split_dve.one(f"lo{t}"))

            def dispatch(E):
                for e in range(E):
                    for t in range(TT):
                        ins = v.tensor_scalar(pd[:, t, cols(e)], cst("iota"), pcol[:, t, e:e + 1], None, ALU.is_equal)
                return ins

            def expert_block(st, i, E, c0, columns):
                S, SA, SV, SG = st

                def low_parts(m, which=(0, 1)):
                    for half in which:
                        w = half_of(c0 + m, half)
                        dve.wait_ge(SA.sem, SA.at(i, f"hi{m}{'ab'[half]}"))
                        v.tensor_tensor(half_of(c0 + m, half, True), w, high_of(2 * m + half).bitcast(F32), ALU.subtract).then_inc(SV.sem, SV.one(f"lo{m}{'ab'[half]}"))

                def hidden(e):
                    dve.wait_ge(S.sem, S.at(i, f"w{2 * e + 1}b"))
                    dve.wait_ge(SA.sem, SA.at(i, f"sg{e}"))
                    if e:
                        dve.wait_ge(S.sem, S.at(i, f"hT{e - 1}"))
                    v.scalar_tensor_tensor(out=he, in0=bank(UP_BANK), scalar=ws[:, e:e + 1], in1=sg, op0=ALU.mult, op1=ALU.mult
                                           ).then_inc(SV.sem, SV.one(f"he{e}"))

                def hidden_low(e):
                    dve.wait_ge(SA.sem, SA.at(i, f"hT{e}"))
                    v.tensor_tensor(heT[:, e, 1], bank(TURN_BANK, 4, P), heT[:, e, 0].bitcast(F32), ALU.subtract).then_inc(SV.sem, SV.one(f"hT{e}"))

                def y_low(e):
                    dve.wait_ge(SA.sem, SA.at(i, f"y{e}"))
                    v.tensor_tensor(ys[:, e, 1], ps[:, Y_BANK[e]:Y_BANK[e] + 2].rearrange("p a b -> p (a b)"),
                                    ys[:, e, 0].bitcast(F32), ALU.subtract).then_inc(SV.sem, SV.one(f"y{e}"))

                if E == 1:
                    columns()
                    dispatch(E).then_inc(SV.sem, SV.one("disp"))
                low_parts(0)
                low_parts(1)
                if E == 2:
                    low_parts(2)
                dve.wait_ge(S.sem, S.at(i, "ws"))
                v.tensor_reduce(ws[:, 0:E], bank(WS_BANK)[:, 0:2 * E].rearrange("p (e s) -> p e s", s=2), AX.X, ALU.add).then_inc(SV.sem, SV.one("ws"))
                dve.wait_ge(SV.sem, SV.at(i, "ws"))
                hidden(0)
                if E == 2:
                    low_parts(3)
                    low_parts(4, (0, ))
                else:
                    low_parts(2)
                hidden_low(0)
                if E == 2:
                    low_parts(4, (1, ))
                    hidden(1)
                    low_parts(5, (0, ))
                    hidden_low(1)
                    low_parts(5, (1, ))
                    y_low(0)
                for e in range(E):
                    dve.wait_ge(S.sem, S.at(i, f"pT{e}"))
                    v.tensor_copy(pdT[:, e], bank(PT_BANK[e])).then_inc(SV.sem, SV.one(f"pT{e}"))
                if E == 2:
                    columns()
                    dispatch(E).then_inc(SV.sem, SV.one("disp"))
                y_low(E - 1)
                for j in range(8):
                    t, half = j // 2, j % 2
                    f = slice(512 * half, 512 * half + 512)
                    dve.wait_ge(S.sem, S.at(i, f"c{j}"))
                    dve.wait_ge(SG.sem, SG.at(i if j >= 2 else i - 1, f"x{(j - 2) % 8}"))
                    v.tensor_tensor(moe_tmp[:, j % 2], bank(COMBINE_BANKS[j % 4]), mod[:, 5 * D + 512 * half:5 * D + 512 * half + 512],
                                    ALU.mult).then_inc(SV.sem, SV.one(f"m{j}"))

            def experts(l):
                split_h(l)
                router(l)
                st, so = moe_steps[l], over_steps[l]
                SV, SO = st[2], so[2]
                v.tensor_copy(wgt_parts[:, :, :, 0], wgt).then_inc(first_disp[l], 1)
                dve.wait_ge(first_disp[l], 1)
                v.tensor_tensor(wgt_parts[:, :, :, 1], wgt, wgt_parts[:, :, :, 0].bitcast(F32), ALU.subtract).then_inc(first_disp[l], 1)
                dve.wait_ge(first_disp[l], 2)
                v.tensor_copy(wcol, wgt_parts[:, :, 0:EG])
                v.tensor_copy(pcol, posm[:, :, 0:EG]).then_inc(first_disp[l], 1)
                dve.wait_ge(first_disp[l], 3)
                dispatch(EG).then_inc(first_disp[l], 1)
                dve.wait_ge(first_disp[l], 4)
                dve.sem_inc(SV.sem, SV.n)
                dve.sem_inc(SO.sem, SO.n)
                with dve.Fori(0, NPAIRS) as i:
                    for g in range(2):
                        def columns():
                            v.tensor_copy(pcol, posm[:, :, bass.ds(2 * EG * i + EG * (g + 1), EG)])
                            v.tensor_copy(wcol, wgt_parts[:, :, bass.ds(2 * EG * i + EG * (g + 1), EG)]).then_inc(SV.sem, SV.one("pw"))
                            dve.wait_ge(SV.sem, SV.at(2 * i + g, "pw"))

                        expert_block(st, 2 * i + g, EG, first[("moe", l)] + 3 * EG * g, columns)
                dve.wait_ge(st[3].sem, st[3].at(NE // EG - 1, "x7"))
                n_over = dve.value_load(ovl_i[0:1, 8:9], min_val=0, max_val=MAXOVER)
                with dve.Fori(0, MAXOVER) as j:
                    e = dve.value_load(ovl_i[0:1, bass.ds(j, 1)], min_val=0, max_val=NE - 1)
                    with dve.If(n_over > j):
                        def columns():
                            dve.wait_ge(SO.sem, SO.at(j - 1, "m7"))
                            v.tensor_copy(wcol[:, :, 0:1], wgt_parts[:, :, bass.ds(e, 1)])
                            v.tensor_scalar(nov, basef[:, bass.ds(j, 1)], float(SLOTS), float(SLOTS), ALU.mult, ALU.add).then_inc(over_col[l], 1)
                            dve.wait_ge(over_col[l], j + 1)
                            v.tensor_scalar(pcol[:, :, 0:1], posm[:, :, bass.ds(e, 1)], nov[:, 0:1], None, ALU.subtract).then_inc(SO.sem, SO.one("pw"))
                            dve.wait_ge(SO.sem, SO.at(j, "pw"))

                        expert_block(so, j, 1, 0, columns)
                dve.wait_ge(x_added, l + 1)

            ada(0)
            norm(0)
            dve.wait_ge(const_in, 16)
            v.tensor_copy(ident_r, ident)
            dve.wait_ge(params_in, 16 * NPARAMS)
            dve.wait_ge(early_in, 16)
            project_ab()
            v.drain().then_inc(phase_done, 1)
            dve.wait_ge(phase_done, 3 * 1)
            v.memset(gaT[0:32, :], 1.0)
            for z_ in (kz, ku, at_g):
                v.memset(z_, 0.0)
            v.memset(st_g, 0.0).then_inc(init_dve, 1)
            dve.wait_ge(init_dve, 2)
            gla()
            v.drain().then_inc(phase_done, 1)
            dve.wait_ge(phase_done, 3 * 2)
            v.memset(vn, 0.0)
            v.memset(st_b, 0.0).then_inc(init_dve, 1)
            dve.wait_ge(init_dve, 3)
            gdn_pre()
            gdn_inverses()
            v.memset(ku_b, 0.0).then_inc(init_dve, 1)
            gdn_rep(0)
            gdn_prep_decays(0)
            dve.wait_ge(init_dve, 4)
            gdn_prep_products(0)
            gdn_prep_solve(0)
            gdn_u(0)
            gdn_rep(1)
            for t in range(TT):
                gdn(t)
            v.drain().then_inc(phase_done, 1)
            dve.wait_ge(phase_done, 3 * 3)
            project_out(0)
            v.drain().then_inc(phase_done, 1)
            dve.wait_ge(phase_done, 3 * 4)
            experts(0)
            v.drain().then_inc(phase_done, 1)
            dve.wait_ge(phase_done, 3 * 5)
            ada(1)
            norm(1)
            project_swa()
            v.drain().then_inc(phase_done, 1)
            dve.wait_ge(phase_done, 3 * 6)
            swa()
            v.drain().then_inc(phase_done, 1)
            dve.wait_ge(phase_done, 3 * 7)
            project_out(1)
            v.drain().then_inc(phase_done, 1)
            dve.wait_ge(phase_done, 3 * 8)
            experts(1)
            v.drain().then_inc(phase_done, 1)


def laid_out(inputs):
    r = {k: np.ascontiguousarray(v) for k, v in inputs.items()}
    r["c_cols"] = np.ascontiguousarray(r.pop("c").reshape(KD, P).T)
    r["conv_cols"] = np.ascontiguousarray(r.pop("gdn_conv").reshape(4, 12, P).transpose(2, 1, 0).reshape(P, 48))
    r["pos_cols"] = np.ascontiguousarray(r.pop("positions").reshape(TT, P).T)
    r["consts"] = constants()
    return r


def kernel(**inputs):
    import concourse.bacc as bacc
    from concourse.bass_utils import run_bass_kernel_spmd

    nc = bacc.Bacc("TRN2", target_bir_lowering=False, num_devices=1)
    arrays, a = {}, {}
    for name, v in laid_out(inputs).items():
        arrays[f"in_{name}_dram"] = v
        a[name] = nc.dram_tensor(f"in_{name}_dram", v.shape, mybir.dt.from_np(v.dtype), kind="ExternalInput").ap()
    out = nc.dram_tensor("out_0_dram", (1, SEQ, D), F32, kind="ExternalOutput").ap()
    build_block(nc, a, out)
    return run_bass_kernel_spmd(nc, [arrays], core_ids=[0]).results[0]["out_0_dram"]
```
